# Optimizing a Trainium2 kernel written in Bass

```python
import jax, jax.numpy as jnp
from jax import lax
import numpy as np

D_MODEL = 1024
BATCH = 1
SEQ = 1024
DEPTH = 1
DEC_BATCH = 8
DEC_SEQ = 1
PAST_LEN = 8192
PAGE_SIZE = 128

D_RNN = D_MODEL
RG_BLOCKS = 16
RG_BW = D_RNN // RG_BLOCKS
RG_CONV = 4
RG_C = 8.0
GLA_HEADS = 4
GLA_DK = D_MODEL // (2 * GLA_HEADS)
GLA_DV = D_MODEL // GLA_HEADS
QK_DIM = GLA_HEADS * GLA_DK
V_DIM = GLA_HEADS * GLA_DV
GLA_RANK = 16
GLA_TAU = 16.0
GLA_CHUNK = 64
D_FF = 3 * D_MODEL
FFN_CONV = 3
N_META = 16
EPS = 1e-6
IN_SIZES = (D_RNN, D_RNN, QK_DIM, QK_DIM, V_DIM, GLA_RANK, V_DIM, D_MODEL, D_MODEL)
D_IN = sum(IN_SIZES)

kernel_name = "hawk_gla_parallel_convffn_step"

def _rmsnorm(x, g):
    xf = x.astype(jnp.float32)
    y = xf * lax.rsqrt(jnp.mean(xf * xf, axis=-1, keepdims=True) + EPS)
    return (y * g.astype(jnp.float32)).astype(x.dtype)

def _causal_dwconv(x, buf, w, b):
    K = w.shape[0]
    T = x.shape[1]
    xx = jnp.concatenate([buf.astype(x.dtype), x], axis=1)
    y = b + xx[:, 0:T] * w[0]
    for j in range(1, K):
        y = y + xx[:, j:j + T] * w[j]
    return y, xx[:, xx.shape[1] - (K - 1):]

def _lin_comb(left, right):
    a1, b1 = left
    a2, b2 = right
    return a1 * a2, a2 * b1 + b2

def _rglru(x, h0, wa, ba, wx, bx, lam):
    B, T, _ = x.shape
    f32 = jnp.float32
    xf = x.astype(f32)
    xb = xf.reshape(B, T, RG_BLOCKS, RG_BW)
    r = jax.nn.sigmoid(jnp.einsum('btnc,ncd->btnd', xb, wa.astype(f32)).reshape(B, T, D_RNN) + ba.astype(f32))
    i = jax.nn.sigmoid(jnp.einsum('btnc,ncd->btnd', xb, wx.astype(f32)).reshape(B, T, D_RNN) + bx.astype(f32))
    log_a = -RG_C * r * jax.nn.softplus(-lam.astype(f32))
    a = jnp.exp(log_a)
    b = jnp.sqrt(-jnp.expm1(2.0 * log_a)) * (i * xf)
    b = b.at[:, 0].add(a[:, 0] * h0.astype(f32))
    _, h = lax.associative_scan(_lin_comb, (a, b), axis=1)
    return h.astype(x.dtype), h[:, -1].astype(x.dtype)

def _gla(q, k, v, log_alpha, S0, pad_left):
    f32 = jnp.float32
    B, T, H, DK = q.shape
    DV = v.shape[-1]
    C = GLA_CHUNK
    pad_right = (-(pad_left + T)) % C
    pw = ((0, 0), (pad_left, pad_right), (0, 0), (0, 0))
    q, k, v, g = [jnp.pad(t.astype(f32), pw) for t in (q, k, v, log_alpha)]
    Tp = T + pad_left + pad_right
    n = Tp // C

    def blk(t):
        return t.reshape(B, n, C, H, t.shape[-1]).transpose(0, 3, 1, 2, 4)

    q, k, v, g = blk(q), blk(k), blk(v), blk(g)
    bc = jnp.cumsum(g, axis=3)
    bl = bc[:, :, :, -1:]
    qd = q * jnp.exp(bc)
    kd = k * jnp.exp(-bc)
    ke = k * jnp.exp(bl - bc)
    mask = jnp.tril(jnp.ones((C, C), dtype=bool))
    A = jnp.where(mask, jnp.einsum('bhncd,bhnsd->bhncs', qd, kd), 0.0)
    o = jnp.einsum('bhncs,bhnse->bhnce', A, v)
    dS = jnp.einsum('bhncd,bhnce->bhnde', ke, v)
    decay = jnp.exp(bl[:, :, :, 0])

    def step(S, inp):
        dec, ds = inp
        return dec[..., None] * S + ds, S

    S_T, S_starts = lax.scan(step, S0.astype(f32), (jnp.moveaxis(decay, 2, 0), jnp.moveaxis(dS, 2, 0)))
    o = o + jnp.einsum('bhncd,nbhde->bhnce', qd, S_starts)
    o = o.transpose(0, 2, 3, 1, 4).reshape(B, Tp, H, DV)[:, pad_left:pad_left + T]
    return o, S_T

def _layer(x, rg_buf, h0, S0, ffn_buf, pad_left, p):
    B, T, _ = x.shape
    f32 = jnp.float32
    xn = _rmsnorm(x, p['norm1_g'])
    z = jnp.einsum('btd,de->bte', xn, p['w_in'])
    split_points = [int(s) for s in np.cumsum(IN_SIZES)[:-1]]
    rg_x, rg_y, q, k, v, g_lr, g_out, m_a, m_b = jnp.split(z, split_points, axis=-1)
    xc, new_rg_buf = _causal_dwconv(rg_x, rg_buf, p['rg_conv_w'], p['rg_conv_b'])
    h, hT = _rglru(xc, h0, p['rg_wa'], p['rg_ba'], p['rg_wx'], p['rg_bx'], p['rg_lambda'])
    ya = jnp.einsum('btc,cd->btd', h * jax.nn.gelu(rg_y), p['w_branch_a'])
    zg = jnp.einsum('btr,rk->btk', g_lr, p['gla_w_gate']) + p['gla_b_gate']
    log_alpha = (jax.nn.log_sigmoid(zg.astype(f32)) / GLA_TAU).reshape(B, T, GLA_HEADS, GLA_DK)
    qh = q.reshape(B, T, GLA_HEADS, GLA_DK) * (GLA_DK ** -0.5)
    kh = k.reshape(B, T, GLA_HEADS, GLA_DK)
    vh = v.reshape(B, T, GLA_HEADS, GLA_DV)
    o, S_T = _gla(qh, kh, vh, log_alpha, S0, pad_left)
    o = o * lax.rsqrt(jnp.mean(o * o, axis=-1, keepdims=True) + EPS) * p['gla_norm_g'].astype(f32)
    o = o * jax.nn.silu(g_out.reshape(B, T, GLA_HEADS, GLA_DV).astype(f32))
    yb = jnp.einsum('btc,cd->btd', o.astype(x.dtype).reshape(B, T, V_DIM), p['w_branch_b'])
    merged = jax.nn.sigmoid(m_a) * ya + jax.nn.sigmoid(m_b) * yb
    x = x + jnp.einsum('btd,de->bte', merged, p['w_out'])
    xn2 = _rmsnorm(x, p['norm2_g'])
    u = jnp.einsum('btd,df->btf', xn2, p['w_ffn_up'])
    uc, new_ffn_buf = _causal_dwconv(u, ffn_buf, p['ffn_conv_w'], p['ffn_conv_b'])
    gate, val = jnp.split(uc, 2, axis=-1)
    x = x + jnp.einsum('btf,fd->btd', jax.nn.gelu(gate) * val, p['w_ffn_down'])
    return x, new_rg_buf, hT, S_T.astype(x.dtype), new_ffn_buf

def _trunk(x, rg_buf, rg_h, gla_S, ffn_buf, pad_left, p, final_norm_g):
    bufs, hs, Ss, fbufs = [], [], [], []
    for l in range(DEPTH):
        pl = {name: arr[l] for name, arr in p.items()}
        x, nb, nh, nS, nf = _layer(x, rg_buf[l], rg_h[l], gla_S[l], ffn_buf[l], pad_left, pl)
        bufs.append(nb)
        hs.append(nh)
        Ss.append(nS)
        fbufs.append(nf)
    y = _rmsnorm(x, final_norm_g)
    return y, jnp.stack(bufs), jnp.stack(hs), jnp.stack(Ss), jnp.stack(fbufs)

def setup_inputs(seed: int = 0) -> dict:
    key = jax.random.key(seed)
    ks = jax.random.split(key, 32)
    f32 = jnp.float32

    def nrm(k, shape, scale):
        return jax.random.normal(k, shape, f32) * scale

    a0 = jax.random.uniform(ks[12], (DEPTH, D_RNN), f32, 0.9, 0.999)
    return {
        "x_prompt": nrm(ks[0], (BATCH, SEQ, D_MODEL), 1.0),
        "x_sample": nrm(ks[1], (DEC_BATCH, DEC_SEQ, D_MODEL), 1.0),
        "state_rg_conv": nrm(ks[2], (DEPTH, DEC_BATCH, RG_CONV - 1, D_RNN), 1.0),
        "state_rg_h": nrm(ks[3], (DEPTH, DEC_BATCH, D_RNN), 0.5),
        "state_gla": nrm(ks[4], (DEPTH, DEC_BATCH, GLA_HEADS, GLA_DK, GLA_DV), 1.0),
        "state_ffn_conv": nrm(ks[5], (DEPTH, DEC_BATCH, FFN_CONV - 1, 2 * D_FF), 1.0),
        "meta_tokens": nrm(ks[6], (N_META, D_MODEL), 1.0),
        "norm1_g": 1.0 + nrm(ks[7], (DEPTH, D_MODEL), 0.02),
        "w_in": nrm(ks[8], (DEPTH, D_MODEL, D_IN), D_MODEL ** -0.5),
        "rg_conv_w": nrm(ks[9], (DEPTH, RG_CONV, D_RNN), RG_CONV ** -0.5),
        "rg_conv_b": nrm(ks[10], (DEPTH, D_RNN), 0.02),
        "rg_wa": nrm(ks[11], (DEPTH, RG_BLOCKS, RG_BW, RG_BW), RG_BW ** -0.5),
        "rg_ba": nrm(ks[13], (DEPTH, D_RNN), 0.02),
        "rg_wx": nrm(ks[14], (DEPTH, RG_BLOCKS, RG_BW, RG_BW), RG_BW ** -0.5),
        "rg_bx": nrm(ks[15], (DEPTH, D_RNN), 0.02),
        "rg_lambda": jnp.log(a0 / (1.0 - a0)),
        "gla_w_gate": nrm(ks[16], (DEPTH, GLA_RANK, QK_DIM), GLA_RANK ** -0.5),
        "gla_b_gate": nrm(ks[17], (DEPTH, QK_DIM), 0.1),
        "gla_norm_g": 1.0 + nrm(ks[18], (DEPTH, GLA_HEADS, GLA_DV), 0.02),
        "w_branch_a": nrm(ks[19], (DEPTH, D_RNN, D_MODEL), D_RNN ** -0.5),
        "w_branch_b": nrm(ks[20], (DEPTH, V_DIM, D_MODEL), V_DIM ** -0.5),
        "w_out": nrm(ks[21], (DEPTH, D_MODEL, D_MODEL), D_MODEL ** -0.5),
        "norm2_g": 1.0 + nrm(ks[22], (DEPTH, D_MODEL), 0.02),
        "w_ffn_up": nrm(ks[23], (DEPTH, D_MODEL, 2 * D_FF), D_MODEL ** -0.5),
        "ffn_conv_w": nrm(ks[24], (DEPTH, FFN_CONV, 2 * D_FF), FFN_CONV ** -0.5),
        "ffn_conv_b": nrm(ks[25], (DEPTH, 2 * D_FF), 0.02),
        "w_ffn_down": nrm(ks[26], (DEPTH, D_FF, D_MODEL), D_FF ** -0.5),
        "final_norm_g": 1.0 + nrm(ks[27], (D_MODEL,), 0.02),
    }

def reference(x_prompt, x_sample, state_rg_conv, state_rg_h, state_gla, state_ffn_conv,
              meta_tokens, norm1_g, w_in, rg_conv_w, rg_conv_b, rg_wa, rg_ba, rg_wx, rg_bx,
              rg_lambda, gla_w_gate, gla_b_gate, gla_norm_g, w_branch_a, w_branch_b, w_out,
              norm2_g, w_ffn_up, ffn_conv_w, ffn_conv_b, w_ffn_down, final_norm_g):
    p = dict(norm1_g=norm1_g, w_in=w_in, rg_conv_w=rg_conv_w, rg_conv_b=rg_conv_b,
             rg_wa=rg_wa, rg_ba=rg_ba, rg_wx=rg_wx, rg_bx=rg_bx, rg_lambda=rg_lambda,
             gla_w_gate=gla_w_gate, gla_b_gate=gla_b_gate, gla_norm_g=gla_norm_g,
             w_branch_a=w_branch_a, w_branch_b=w_branch_b, w_out=w_out, norm2_g=norm2_g,
             w_ffn_up=w_ffn_up, ffn_conv_w=ffn_conv_w, ffn_conv_b=ffn_conv_b,
             w_ffn_down=w_ffn_down)
    dt = x_prompt.dtype
    B = x_prompt.shape[0]
    xp = jnp.concatenate([jnp.broadcast_to(meta_tokens.astype(dt)[None], (B, N_META, D_MODEL)), x_prompt], axis=1)
    zeros_rg_buf = jnp.zeros((DEPTH, B, RG_CONV - 1, D_RNN), dt)
    zeros_h = jnp.zeros((DEPTH, B, D_RNN), dt)
    zeros_S = jnp.zeros((DEPTH, B, GLA_HEADS, GLA_DK, GLA_DV), dt)
    zeros_ffn = jnp.zeros((DEPTH, B, FFN_CONV - 1, 2 * D_FF), dt)
    meta_pad = (-N_META) % GLA_CHUNK
    yp, rg_conv_prompt, rg_h_prompt, gla_prompt, ffn_conv_prompt = _trunk(
        xp, zeros_rg_buf, zeros_h, zeros_S, zeros_ffn, meta_pad, p, final_norm_g)
    y_prompt = yp[:, N_META:]
    y_sample, rg_conv_sample, rg_h_sample, gla_sample, ffn_conv_sample = _trunk(
        x_sample, state_rg_conv, state_rg_h, state_gla, state_ffn_conv, 0, p, final_norm_g)
    return (y_prompt, y_sample, rg_conv_prompt, rg_h_prompt, gla_prompt, ffn_conv_prompt,
            rg_conv_sample, rg_h_sample, gla_sample, ffn_conv_sample)


_drawn_inputs = setup_inputs


def setup_inputs(seed=0):
    import zlib

    import numpy as np

    out = dict(_drawn_inputs(seed))
    spreads = {}
    factors = {'rg_ba': 8.0,
     'rg_bx': 7.485,
     'gla_norm_g': 8.0,
     'norm2_g': 2.817,
     'ffn_conv_b': 3.709,
     'final_norm_g': 3.115}
    for name, (base, spread) in spreads.items():
        noise = np.random.default_rng([zlib.crc32(name.encode()), seed]).standard_normal(out[name].shape)
        drawn = base * np.exp(spread * noise) if base else spread * noise
        out[name] = __import__('jax').numpy.asarray(drawn.astype(out[name].dtype))
    for name, factor in factors.items():
        out[name] = (out[name] * factor).astype(out[name].dtype)
    return out
```

```python
from contextlib import ExitStack

import concourse.bass as bass
from concourse import mybir

ALU = mybir.AluOpType
ACT = mybir.ActivationFunctionType
F32 = mybir.dt.float32
F32R = mybir.dt.float32r
BF16 = mybir.dt.bfloat16
I32 = mybir.dt.int32
LN_EXP = "natural_log_exp_and_others"

P = 128
D = 1024
KB = D // P
NMETA = 16
SEQ = 1024
NT = NMETA + SEQ
NB = 8
NS = 10
C = NT + NS
NW = C // 3
H = 4
DK = 128
DV = 256
QK = H * DK
RANK = 16
CH = 64
PAIR = 2 * CH
NPAIR = SEQ // PAIR
FF = 3 * D
FB = FF // P
UB = 2 * FB
GRP = 3
NGRP = FB // GRP
RGW = 13
HW = 11
UW = 12
EPS = 1e-6
TINY = 2.0 ** -63

U_QKV = 1
U_RG = U_QKV + 16
U_GO = U_RG + 16
U_B = U_GO + 8
U_A = U_B + 16
U_OUT = U_A + 16
U_FFN = U_OUT + 8
N_UNITS = U_FFN + UB + FB
G_QKV = (1, 1)
G_RG = (9, 9)
G_GO = (25, 25)
G_B = (29, 29)
G_A = (37, 37)
G_OUT = (45, 45)
G_NORM2 = 49
G_FFN = (49, 50)
G_FINAL = 49 + (UB + KB * NGRP) // 2

RP = {n: i * KB for i, n in enumerate(["w0", "w1", "w2", "w3", "b", "ba", "bx", "lam", "g1", "gn", "g2", "gf"])}
RP_N = 12 * KB



def view3(t):
    return t.rearrange("p (a n) -> p a n", a=3)


def hd(t, n, w):
    return t[:, 0:n * w].rearrange("p (h t) -> p h t", h=n)


def state_banks(n):
    return 0 if isinstance(n, int) and n == 0 else 4 * n - 2


def slot_of(u):
    return u % 2


def nth(u, per=0, i=0):
    return u // 2 + per // 2 * i


def build(nc, I, O):
    ctx = ExitStack()
    with ctx:
        base = 16512
        CB = 4 * C
        TB = (CB + 31) // 32 * 32

        def at(name, off, cols, dt=F32, parts=P):
            return nc.alloc_sbuf_tensor_at(name, [parts, cols], dt, offset=base + off)[:, :]

        A0 = 0
        V0 = 16 * CB
        W0 = V0 + KB * CB
        R0 = W0 + 6 * 4096
        B0 = R0
        M0 = B0 + KB * CB
        T0 = M0 + KB * CB
        E0 = T0 + 3 * TB
        XH, XL = at("xn_hi", A0, KB * C, F32R), at("xn_lo", A0 + KB * CB, KB * C, F32R)
        X1 = at("x_in", V0, KB * C)
        V = at("v_o", V0, KB * C)
        raw = [at(f"w_raw{s}", W0 + 4096 * s, D) for s in range(2)]
        whi = [at(f"w_hi{s}", W0 + 8192 + 8192 * s, D, F32R) for s in range(2)]
        wlo = [at(f"w_lo{s}", W0 + 12288 + 8192 * s, D, F32R) for s in range(2)]
        off = [R0]

        def nxt(name, cols, dt=F32, size=4, parts=P):
            t = at(name, off[0], cols, dt, parts)
            off[0] += (cols * size + 31) // 32 * 32
            return t

        ext = nxt("rg_ext", C + 3)
        xc = nxt("rg_xc_h", C)
        rt = nxt("rg_r", C)
        it = nxt("rg_i_b", C)
        av = nxt("rg_a", C)
        th = nxt("rg_mult", C)
        gy = nxt("rg_gelu_ha", C)
        zg = nxt("gla_z_g_osq", 8 * PAIR)
        z_t, g_t = zg[:, 0:4 * PAIR], zg[:, 4 * PAIR:8 * PAIR]
        bc = nxt("gla_bc_keT", 4 * PAIR)
        eb = nxt("gla_exp_bc", 4 * PAIR)
        kk = nxt("gla_kd_ke_vcopy", 8 * PAIR)
        kd, ke = kk[:, 0:4 * PAIR], kk[:, 4 * PAIR:8 * PAIR]
        qd = nxt("gla_qd", 4 * PAIR)
        vtm = nxt("gla_v_tokens", D)
        am = nxt("gla_scores", 4 * PAIR)
        S = nxt("gla_state", 2 * H * DV)
        qkp_at = off[0]
        qkp = nxt("gla_qk_pair", 8 * PAIR)
        rgst = at("rg_states", qkp_at, 3 * KB * NS)
        rgtmp = at("rg_states_tmp", qkp_at + 1024, KB * NS)
        glr = nxt("gla_low_rank", C)
        gw = nxt("rg_gate_weights", 2 * P)
        sS = nxt("smp_state", H * DV)
        skm = nxt("smp_k_masked", QK)
        skt = nxt("smp_k_tokens", QK)
        svt = nxt("smp_v_tokens", D)
        wg = nxt("gla_gate_weights", QK)
        reset = nxt("scan_reset", 4 * PAIR, BF16, 2)
        rs16 = nxt("scan_reset16", 4 * NMETA, BF16, 2)
        ident = nxt("ident", P)
        mask = nxt("causal_mask", P, I32)
        rgp = nxt("rg_smp_conv", KB * NS)
        h0 = nxt("rg_h0", KB * NS)
        der = nxt("rg_derived", 5 * KB)
        gbz = nxt("gla_bias", H)
        sqk = nxt("smp_qk", 8 * NS)
        sdec = nxt("smp_decay", H * NS)
        srv = nxt("smp_rinv", H * NS)
        off[0] = max(off[0], E0)
        rgo = nxt("rg_last_columns", KB * RGW)
        hco = nxt("h_last_columns", KB * HW)
        prm = nxt("params", RP_N)
        ones = nxt("ones", P)
        cst = nxt("consts", 2)
        assert off[0] + base <= 229344, off[0] + base
        OBH, OBL = at("o_hi", B0, KB * C, F32R), at("o_lo", V0, KB * C, F32R)
        HAH, HAL = at("h_hi", V0, KB * C, F32R), at("h_lo", B0, KB * C, F32R)
        HA = at("h", B0, KB * C)
        MG = at("merged", M0, KB * C)
        MGH, MGL = at("merged_hi", A0, KB * C, F32R), at("merged_lo", A0 + KB * CB, KB * C, F32R)
        X2 = at("residual", V0, KB * C)
        X2H, X2L = at("xn2_hi", B0, KB * C, F32R), at("xn2_lo", M0, KB * C, F32R)
        T = [at(f"tmp{i}", T0 + TB * i, C) for i in range(3)]
        sqsum = at("square_sum", M0, C)
        act_bytes = (2 * GRP * CB + 31) // 32 * 32
        AH = at("act_hi", A0, 2 * GRP * C, F32R)
        AL = at("act_lo", A0 + act_bytes, 2 * GRP * C, F32R)
        fst = at("ffn_states", A0, 2 * UB * NS)
        F0 = A0 + 2 * act_bytes
        eg = at("gate_ext", F0, C + 2)
        ev = at("val_ext", F0 + TB, C + 2)
        cg = at("gate_conv", F0 + 2 * TB, C)
        fpr = at("ffn_params", F0 + 3 * TB, 4 * UB)
        fps = at("ffn_smp_conv", F0 + 3 * TB + 768, UB * NS)
        assert F0 + 3 * TB + 768 + 4 * UB * NS <= V0
        cv, act_t, ubuf = T[0], T[1], at("u_last_columns", T0 + 2 * TB, UB * UW)
        ysq, ysum, yrs = at("y_square", F0, C), at("y_square_sum", F0 + TB, C), at("y_rms", F0 + 2 * TB, C)

        acc = [ctx.enter_context(nc.psum_tensor(f"acc{s}", [P, 3, 512], F32)) for s in range(2)]
        sb6 = ctx.enter_context(nc.psum_tensor("small6", [P, 512], F32))
        sb7 = ctx.enter_context(nc.psum_tensor("small7", [P, 512], F32))
        accv = [a[:, :, 0:NW] for a in acc]

        qk_scr = nc.dram_tensor("qk_scratch", (8, P, C), F32).ap()
        ha_scr = nc.dram_tensor("ha_scratch", (KB, P, C), F32).ap()

        def sem(n):
            return ctx.enter_context(nc.semaphore(n))

        def sems(n, k=2):
            return [sem(f"{n}{i}") for i in range(k)]

        def col(t, j, n=1, w=1):
            return t[:, bass.ds(j * w, n)]

        def blk(t, j):
            return t[:, bass.ds(j * C, C)]

        def par(name, j):
            return prm[:, bass.ds(j + RP[name], 1)]

        V3 = V.rearrange("p (k c) -> p k c", k=KB)

        w_loaded, w_hi_done, w_split, unit_done = sems("w_loaded"), sems("w_hi_done"), sems("w_split"), sems("unit_done")
        acc_free = sems("acc_free")
        sum_mm, gate_mm, down_mm = sem("sum_mm"), sem("gate_mm"), sem("down_mm")
        x_loaded = sems("x_loaded", 4)
        par_loaded, const_loaded, gwt_loaded = sem("par_loaded"), sem("const_loaded"), sem("gwt_loaded")
        sq1_done, sum1_done, lnr1_done, r1_done = sem("sq1_done"), sem("sum1_done"), sem("lnr1_done"), sem("r1_done")
        xn1_done, xh1_done, xl1_done = sem("xn1_done"), sem("xh1_done"), sem("xl1_done")
        set_v, set_a = sem("set_v"), sem("set_a")
        pads_done, ones_done = sem("pads_done"), sem("ones_done")
        qk_stored = sems("qk_stored")
        qk_loaded = sem("qk_loaded")
        zg_mm, z_ready, absz_done, expz_done, lnz_done = (sem(n) for n in ("zg_mm", "z_ready", "absz_done", "expz_done", "lnz_done"))
        g_ready, bc_ready, bl_ready, eb_ready, enb_ready, eke_ready = (
            sem(n) for n in ("g_ready", "bc_ready", "bl_ready", "eb_ready", "enb_ready", "eke_ready"))
        qd_ready, kd_ready, ke_ready = sem("qd_ready"), sem("kd_ready"), sem("ke_ready")
        vT_mm, vT_ready, keT_mm, keT_ready, A_mm, A_ready = (
            sem(n) for n in ("vT_mm", "vT_ready", "keT_mm", "keT_ready", "A_mm", "A_ready"))
        vcp_ready = sem("vcp_ready")
        dS_mm, S_ready, O_mm, o_copied, o_squared = (sem(n) for n in ("dS_mm", "S_ready", "O_mm", "o_copied", "o_squared"))
        onorm_mm, olog_done, orinv_ready, o_ready = (sem(n) for n in ("onorm_mm", "olog_done", "orinv_ready", "o_ready"))
        sqk_loaded, sT_mm, sT_ready, sg_ready, sS_loaded, sS_stored = (
            sem(n) for n in ("sqk_loaded", "sT_mm", "sT_ready", "sg_ready", "sS_loaded", "sS_stored"))
        skm_ready, skv_mm, sS_ready, so_mm, so_ready = (sem(n) for n in ("skm_ready", "skv_mm", "sS_ready", "so_mm", "so_ready"))
        s_act = sem("s_act")
        xraw_ready, xc_step, rgo_kept, gelu_ready, r_ready, i_ready, th_ready, a_ready, a2_ready, w_ready, ml_done, m_ready = (
            sem(n) for n in ("xraw_ready", "xc_step", "rgo_kept", "gelu_ready", "r_ready", "i_ready", "th_ready", "a_ready",
                             "a2_ready", "w_ready", "ml_done", "m_ready"))
        ix_ready, b_ready, h_step, ha_ready, ha_stored = (
            sem(n) for n in ("ix_ready", "b_ready", "h_step", "ha_ready", "ha_stored"))
        silu_done, og_done, obh_done, obl_done = sem("silu_done"), sem("og_done"), sem("obh_done"), sem("obl_done")
        hl_loaded, o_used = sems("hl_loaded", KB), sem("o_used")
        hah_done, hal_done, ma_done = sem("hah_done"), sem("hal_done"), sem("ma_done")
        mgh_done, mgl_done = sem("mgh_done"), sem("mgl_done")
        xr_loaded = sems("xr_loaded")
        sq2_done, sum2_done, lnr2_done, r2_done, xn2_done, xh2_done, xl2_done = (
            sem(n) for n in ("sq2_done", "sum2_done", "lnr2_done", "r2_done", "xn2_done", "xh2_done", "xl2_done"))
        fst_loaded, set_f = sem("fst_loaded"), sem("set_f")
        graw_ready, gconv_step, vraw_ready, vconv_step, gkept, vkept = (
            sem(n) for n in ("graw_ready", "gconv_step", "vraw_ready", "vconv_step", "gkept", "vkept"))
        ggelu_done, act_done, acth_done, actl_done = (
            sem(n) for n in ("ggelu_done", "act_done", "acth_done", "actl_done"))
        sq3_done, sum3_done, lnr3_done, r3_done, y_done = (sem(n) for n in ("sq3_done", "sum3_done", "lnr3_done", "r3_done", "y_done"))
        stored = sem("stored")
        y_stored = sems("y_stored")

        block = ctx.enter_context(nc.Block())

        @block.sync
        def _(sp):
            for q in range(2):
                sp.dma_start(X1[:, 4 * q * C:(4 * q + 2) * C].rearrange("p (k c) -> p k c", k=2),
                             I["x"][4 * q:4 * q + 2].rearrange("k p c -> p k c")).then_inc(x_loaded[2 * q], 16)
            for s in range(2):
                sp.dma_start(raw[s], I["w"][s]).then_inc(w_loaded[s], 16)
            with sp.Fori(1, N_UNITS // 2) as i:
                for s in range(2):
                    sp.wait_ge(w_split[s], i)
                    sp.dma_start(raw[s], I["w"][2 * i + s]).then_inc(w_loaded[s], 16)
            sp.wait_ge(w_split[0], N_UNITS // 2)
            sp.dma_start(raw[0], I["w"][N_UNITS - 1]).then_inc(w_loaded[0], 16)
            sp.wait_ge(rgo_kept, KB)
            sp.wait_ge(h_step, 4 * KB)
            sp.dma_start(O["rg_last"], rgo).then_inc(stored, 16)
            sp.dma_start(O["h_last"], hco).then_inc(stored, 16)
            sp.wait_ge(gkept, FB)
            sp.wait_ge(vkept, FB)
            sp.dma_start(O["u_last"], ubuf).then_inc(stored, 16)
            for k in range(KB):
                sp.wait_ge(y_done, k + 1)
                sp.dma_start(O["y"][k], T[k % 2]).then_inc(y_stored[k % 2], 16)
            for s in range(2):
                sp.wait_ge(y_stored[s], 16 * KB // 2)
            sp.wait_ge(stored, 16 * 6)
            sp.wait_ge(sS_stored, 16 * NB)

        @block.gpsimd
        def _(pool):
            def split(i, s):
                pool.wait_ge(w_loaded[s], 16 * i + 16)
                if not isinstance(i, int) or i > 0:
                    pool.wait_ge(unit_done[s], i)
                nc.gpsimd.tensor_tensor(whi[s], raw[s], one, ALU.mult).then_inc(w_hi_done[s], 1)
                pool.wait_ge(w_hi_done[s], i + 1)
                nc.gpsimd.tensor_tensor(wlo[s], raw[s], whi[s].bitcast(F32), ALU.subtract).then_inc(w_split[s], 1)

            pool.wait_ge(ones_done, 1)
            one = ones[:, 0:1].broadcast_to([P, D])
            split(0, 0)
            split(0, 1)
            with pool.Fori(1, N_UNITS // 2) as i:
                split(i, 0)
                split(i, 1)
            split(N_UNITS // 2, 0)

        @block.tensor
        def _(pe):
            def tile_products(s, t, g, xh, xl, first, last):
                for w, x, a, z in ((whi, xh, first, False), (whi, xl, False, False), (wlo, xh, False, last)):
                    for n in range(3):
                        mm = nc.tensor.matmul(accv[g][:, n], w[s][:, t * P:(t + 1) * P], x[:, n * NW:(n + 1) * NW],
                                              start=a, stop=z)
                return mm

            def unit(u, n_slot, g, n_grp, xh, xl, pieces=(), gate=None, used=None):
                s = slot_of(u)
                pe.wait_ge(w_split[s], n_slot + 1)
                pe.wait_ge(acc_free[g], n_grp)
                for k in range(KB):
                    if gate:
                        gate(k)
                    mm = tile_products(s, k, g, xh[:, k * C:(k + 1) * C], xl[:, k * C:(k + 1) * C], k == 0, k == KB - 1)
                    if k == KB - 1:
                        mm.then_inc(unit_done[s], 1)
                    elif used:
                        mm.then_inc(used, 1)
                    for f in dict(pieces).get(k, ()):
                        f()

            def sum_features(src, g):
                for n in range(3):
                    mm = nc.tensor.matmul(accv[g][:, n], ones, src[:, n * NW:(n + 1) * NW], start=True, stop=True)
                mm.then_inc(sum_mm, 1)

            pe.wait_ge(ones_done, 1)
            pe.wait_ge(sum1_done, KB)
            sum_features(xc, 1)

            def xn1_gate(k):
                pe.wait_ge(xh1_done, k + 1)
                pe.wait_ge(xl1_done, k + 1)
            unit(0, 0, 0, 0, XH, XL, gate=xn1_gate)
            with pe.Fori(0, 4) as i:
                unit(U_QKV, nth(U_QKV, 2, i), 1, G_QKV[1] + i, XH, XL)
                unit(U_QKV + 1, nth(U_QKV + 1, 2, i), 0, G_QKV[0] + i, XH, XL)

            def zg_piece(n, w, c0):
                pe.wait_ge(olog_done, n)
                for h in range(H):
                    mm = nc.tensor.matmul(sb6[:, h * w:(h + 1) * w], wg[0:RANK, h * DK:(h + 1) * DK],
                                          glr[0:RANK, bass.ds(c0, w)], start=True, stop=True)
                mm.then_inc(zg_mm, 1)

            def vT_piece(n, w, half):
                if half == 0:
                    pe.wait_ge(vcp_ready, n + 1)
                    pe.wait_ge(S_ready, state_banks(n))
                pe.wait_ge(vT_ready, 2 * n + half)
                for e in range(4):
                    k = 4 * half + e
                    mm = nc.tensor.transpose(sb7[0:w, e * P:(e + 1) * P], kk[:, k * w:(k + 1) * w], ident)
                mm.then_inc(vT_mm, 1)

            def keT_piece(n, w, bank7_free, count):
                pe.wait_ge(ke_ready, n + 1)
                pe.wait_ge(bank7_free, count)
                for h in range(H):
                    mm = nc.tensor.transpose(sb7[0:w, h * DK:(h + 1) * DK], ke[:, h * w:(h + 1) * w], ident)
                mm.then_inc(keT_mm, 1)

            def A_piece(n, w, bank6_free, count):
                pe.wait_ge(qd_ready, n + 1)
                pe.wait_ge(kd_ready, n + 1)
                pe.wait_ge(bank6_free, count)
                for h in range(H):
                    mm = nc.tensor.matmul(sb6[0:w, h * w:(h + 1) * w], kd[:, h * w:(h + 1) * w],
                                          qd[:, h * w:(h + 1) * w], start=True, stop=True)
                mm.then_inc(A_mm, 1)

            def O_piece(bank, w, cl, hh, inter):
                for q in range(4):
                    h, e = 2 * hh + q // 2, q % 2
                    mm = nc.tensor.matmul(bank[:, q * w:(q + 1) * w], vtm[0:w, h * DV + e * P:h * DV + (e + 1) * P],
                                          am[0:w, h * w:(h + 1) * w], start=True, stop=not inter)
                    for ck in range(w // cl if inter else 0):
                        s0 = ck * H * DV + h * DV + e * P
                        mm = nc.tensor.matmul(bank[:, q * w + ck * cl:q * w + (ck + 1) * cl], S[:, s0:s0 + P],
                                              qd[:, h * w + ck * cl:h * w + (ck + 1) * cl], start=False,
                                              stop=ck == w // cl - 1)
                mm.then_inc(O_mm, 1)

            def dS_piece(bank, cl, ck, hh):
                r = slice(ck * cl, (ck + 1) * cl)
                for h in (2 * hh, 2 * hh + 1):
                    mm = nc.tensor.matmul(bank[:, (h % 2) * DV:(h % 2 + 1) * DV], bc[r, h * DK:(h + 1) * DK],
                                          vtm[r, h * DV:(h + 1) * DV], start=True, stop=True)
                mm.then_inc(dS_mm, 1)

            def onorm_piece(n, w):
                pe.wait_ge(o_squared, 2 * n + 2)
                for e in range(2):
                    osq = zg[:, 0:8 * w].rearrange("p (h e t) -> p h e t", h=H, e=2)[:, :, e, :]
                    mm = nc.tensor.matmul(hd(sb6, H, w), ones, osq, start=e == 0, stop=e == 1)
                mm.then_inc(onorm_mm, 1)

            def zg_head():
                pe.wait_ge(const_loaded, 16 * 5)
                pe.wait_ge(acc_free[0], 1)
                zg_piece(0, NMETA, 0)

            def zg_samples():
                pe.wait_ge(z_ready, 1)
                for h in range(H):
                    mm = nc.tensor.matmul(sb6[:, h * NS:(h + 1) * NS], wg[0:RANK, h * DK:(h + 1) * DK],
                                          glr[0:RANK, NT:C], start=True, stop=True)
                mm.then_inc(zg_mm, 1)

            def kT_samples():
                pe.wait_ge(sqk_loaded, 16)
                for h in range(H):
                    mm = nc.tensor.transpose(sb7[0:NS, h * DK:(h + 1) * DK], sqk[:, (H + h) * NS:(H + h + 1) * NS], ident)
                mm.then_inc(sT_mm, 1)

            def vT_samples(half):
                for e in range(4):
                    k = 4 * half + e
                    mm = nc.tensor.transpose(sb6[0:NS, e * P:(e + 1) * P], V[:, k * C + NT:k * C + NT + NS], ident)
                mm.then_inc(sT_mm, 1)

            unit(U_QKV + 8, nth(U_QKV + 8), 1, G_QKV[1] + 4, XH, XL, {1: [zg_head], 3: [zg_samples], 7: [kT_samples]})
            unit(U_QKV + 9, nth(U_QKV + 9), 0, G_QKV[0] + 4, XH, XL, {
                1: [lambda: keT_piece(0, NMETA, sT_ready, 1)], 3: [lambda: A_piece(0, NMETA, z_ready, 2)]})
            with pe.Fori(5, 8) as i:
                unit(U_QKV, nth(U_QKV, 2, i), 1, G_QKV[1] + i, XH, XL)
                unit(U_QKV + 1, nth(U_QKV + 1, 2, i), 0, G_QKV[0] + i, XH, XL)
            pe.wait_ge(keT_ready, 1)
            vT_piece(0, NMETA, 0)
            pe.wait_ge(A_ready, 1)
            vT_samples(0)
            vT_piece(0, NMETA, 1)
            pe.wait_ge(sT_ready, 2)
            vT_samples(1)
            pe.wait_ge(vT_ready, 2)
            O_piece(sb7, NMETA, NMETA, 0, False)
            pe.wait_ge(sT_ready, 3)
            O_piece(sb6, NMETA, NMETA, 1, False)
            for hh, bank in ((0, sb7), (1, sb6)):
                pe.wait_ge(o_copied, hh + 1)
                dS_piece(bank, NMETA, 0, hh)
            pe.wait_ge(S_ready, 2)
            onorm_piece(0, NMETA)

            def smp_kv(j, hh, bank):
                if hh == 0:
                    pe.wait_ge(skm_ready, j + 1)
                for h in (2 * hh, 2 * hh + 1):
                    mm = nc.tensor.matmul(bank[:, (h % 2) * DV:(h % 2 + 1) * DV], skm[0:NS, h * DK:(h + 1) * DK],
                                          svt[0:NS, h * DV:(h + 1) * DV], start=True, stop=True)
                mm.then_inc(skv_mm, 1)

            def smp_o(j):
                pe.wait_ge(sS_ready, 2 * j + 2)
                for h in range(H):
                    for e in range(2):
                        mm = nc.tensor.matmul(sb7[:, 2 * h + e:2 * h + e + 1], sS[:, h * DV + e * P:h * DV + (e + 1) * P],
                                              sqk[:, bass.ds(h * NS + j, 1)], start=True, stop=True)
                mm.then_inc(so_mm, 1)

            def gate_product(g, n_grp, half):
                pe.wait_ge(acc_free[g], n_grp)
                for n in range(3):
                    mm = nc.tensor.matmul(accv[g][:, n], gw[:, half * P:(half + 1) * P], xc[:, n * NW:(n + 1) * NW],
                                          start=True, stop=True)
                mm.then_inc(gate_mm, 1)

            with pe.Fori(0, NPAIR) as j:
                n = j + 1
                zn = j + 2

                def zg_pair():
                    pe.wait_ge(ones_done, 1)
                    pe.wait_ge(olog_done, n)
                    for h in range(H):
                        mm = nc.tensor.matmul(sb6[:, h * PAIR:(h + 1) * PAIR], wg[0:RANK, h * DK:(h + 1) * DK],
                                              glr[0:RANK, bass.ds(NMETA + PAIR * j, PAIR)], start=True, stop=True)
                    mm.then_inc(zg_mm, 1)

                def smp_h01():
                    pe.wait_ge(vT_ready, 2 * n + 2)
                    smp_kv(j, 0, sb7)

                def smp_h23():
                    pe.wait_ge(z_ready, zn + 1)
                    smp_kv(j, 1, sb6)

                def dS0_01():
                    pe.wait_ge(keT_ready, n + 1)
                    pe.wait_ge(A_ready, n + 1)
                    dS_piece(sb6, CH, 0, 0)

                def dS0_23():
                    dS_piece(sb7, CH, 0, 1)

                def O_pair(hh, bank):
                    pe.wait_ge(S_ready, state_banks(n) + hh + 1)
                    O_piece(bank, PAIR, CH, hh, True)

                def dS1(hh, bank):
                    pe.wait_ge(o_copied, 2 * n + hh + 1)
                    dS_piece(bank, CH, 1, hh)

                unit(U_RG, nth(U_RG, 2, j), 1, G_RG[1] + 2 * j, XH, XL, {
                    0: [lambda: vT_piece(n, PAIR, 0)], 2: [zg_pair], 3: [lambda: vT_piece(n, PAIR, 1)],
                    5: [smp_h01, smp_h23]})
                unit(U_RG + 1, nth(U_RG + 1, 2, j), 0, G_RG[0] + 2 * j, XH, XL, {
                    0: [lambda: smp_o(j)],
                    2: [lambda: keT_piece(n, PAIR, so_ready, j + 1), lambda: A_piece(n, PAIR, sS_ready, 2 * j + 2)],
                    4: [dS0_01, dS0_23], 5: [lambda: O_pair(0, sb6)], 6: [lambda: O_pair(1, sb7)],
                    7: [lambda: dS1(0, sb6)]})
                pe.wait_ge(xc_step, 4 * j + 4)
                pe.wait_ge(gwt_loaded, 16 * j + 16)
                gate_product(1, G_RG[1] + 2 * j + 1, 0)
                dS1(1, sb7)
                pe.wait_ge(S_ready, state_banks(n) + 3)
                onorm_piece(n, PAIR)
                gate_product(0, G_RG[0] + 2 * j + 1, 1)

            def onorm_samples():
                pe.wait_ge(s_act, 3)
                pe.wait_ge(olog_done, NPAIR + 1)
                for e in range(2):
                    osq = zg[:, 0:8 * NS].rearrange("p (h e t) -> p h e t", h=H, e=2)[:, :, e, :]
                    mm = nc.tensor.matmul(hd(sb6, H, NS), ones, osq, start=e == 0, stop=e == 1)
                mm.then_inc(onorm_mm, 1)

            unit(U_GO, nth(U_GO), 1, G_GO[1], XH, XL, {5: [onorm_samples]})
            unit(U_GO + 1, nth(U_GO + 1), 0, G_GO[0], XH, XL)
            with pe.Fori(1, KB // 2) as i:
                unit(U_GO, nth(U_GO, 2, i), 1, G_GO[1] + i, XH, XL)
                unit(U_GO + 1, nth(U_GO + 1, 2, i), 0, G_GO[0] + i, XH, XL)
            pe.wait_ge(obh_done, KB)
            pe.wait_ge(obl_done, KB)
            with pe.Fori(0, KB - 1) as j:
                unit(U_B, nth(U_B, 2, j), 1, G_B[1] + j, XH, XL)
                unit(U_B + 1, nth(U_B + 1, 2, j), 0, G_B[0] + j, OBH, OBL)
            j = KB - 1
            unit(U_B, nth(U_B, 2, j), 1, G_B[1] + j, XH, XL)
            unit(U_B + 1, nth(U_B + 1, 2, j), 0, G_B[0] + j, OBH, OBL, used=o_used)

            def h_gate(k):
                pe.wait_ge(hah_done, k + 1)
                pe.wait_ge(hal_done, k + 1)
            unit(U_A, nth(U_A), 1, G_A[1], XH, XL)
            unit(U_A + 1, nth(U_A + 1), 0, G_A[0], HAH, HAL, gate=h_gate)
            with pe.Fori(1, KB) as j:
                unit(U_A, nth(U_A, 2, j), 1, G_A[1] + j, XH, XL)
                unit(U_A + 1, nth(U_A + 1, 2, j), 0, G_A[0] + j, HAH, HAL)

            def mg_gate(k):
                pe.wait_ge(mgh_done, k + 1)
                pe.wait_ge(mgl_done, k + 1)
            unit(U_OUT, nth(U_OUT), 1, G_OUT[1], MGH, MGL, gate=mg_gate)
            unit(U_OUT + 1, nth(U_OUT + 1), 0, G_OUT[0], MGH, MGL)
            with pe.Fori(1, KB // 2) as i:
                unit(U_OUT, nth(U_OUT, 2, i), 1, G_OUT[1] + i, MGH, MGL)
                unit(U_OUT + 1, nth(U_OUT + 1, 2, i), 0, G_OUT[0] + i, MGH, MGL)
            pe.wait_ge(sum2_done, KB)
            pe.wait_ge(acc_free[1], G_NORM2)
            sum_features(sqsum, 1)

            def up_unit(u, n_slot, g, n_grp, gate=None):
                unit(u, n_slot, g, n_grp, X2H, X2L, gate=gate)

            def up(u0, per, i, grp0, gper, gate=None):
                for f in range(GRP):
                    for c in range(2):
                        u = u0 + 2 * f + c
                        up_unit(u, nth(u, per, i), c, G_FFN[c] + grp0 + f + gper * i, gate if u == U_FFN else None)

            def down(u0, per, i, grp0, gper, half, n_act):
                pe.wait_ge(acth_done, n_act)
                pe.wait_ge(actl_done, n_act)
                for m in range(KB):
                    g = m % 2
                    pe.wait_ge(acc_free[g], G_FFN[g] + grp0 + m // 2 + gper * i)
                    for k in range(GRP):
                        t = m * GRP + k
                        u = u0 + t // KB
                        s = slot_of(u)
                        if t % KB == 0:
                            pe.wait_ge(w_split[s], nth(u, per, i) + 1)
                        b = (half * GRP + k) * C
                        mm = tile_products(s, t % KB, g, AH[:, b:b + C], AL[:, b:b + C], k == 0, k == GRP - 1)
                        if t % KB == KB - 1:
                            mm.then_inc(unit_done[s], 1)
                    if m < KB - 1:
                        mm.then_inc(down_mm, 1)

            def xn2_gate(k):
                pe.wait_ge(xh2_done, k + 1)
                pe.wait_ge(xl2_done, k + 1)
            NU, ND = 2 * GRP, GRP
            GU, GD = GRP, KB // 2
            up(U_FFN, 0, 0, 0, 0, gate=xn2_gate)
            per, gper = 2 * (NU + ND), 2 * (GU + GD)
            with pe.Fori(0, NGRP // 2 - 1) as i:
                up(U_FFN + NU, per, i, GU, gper)
                down(U_FFN + 2 * NU, per, i, 2 * GU, gper, 0, 2 * GRP * i + GRP)
                up(U_FFN + 2 * NU + ND, per, i, 2 * GU + GD, gper)
                down(U_FFN + 3 * NU + ND, per, i, 3 * GU + GD, gper, 1, 2 * GRP * i + 2 * GRP)
            n, gn = NGRP // 2 - 1, NGRP // 2 - 1
            u, g = U_FFN + NU + n * per, GU + gn * gper
            up(u, 0, 0, g, 0)
            down(u + NU, 0, 0, g + GU, 0, 0, GRP * (NGRP - 1))
            down(u + NU + ND, 0, 0, g + GU + GD, 0, 1, GRP * NGRP)
            pe.wait_ge(sum3_done, KB)
            pe.wait_ge(acc_free[0], G_FINAL)
            sum_features(ysum, 0)

        @block.scalar
        def _(act):
            def ready(u, per=0, i=0):
                act.wait_ge(unit_done[slot_of(u)], nth(u, per, i) + 1)

            def plain():
                act.wait_ge(ones_done, 1)

            for q in range(2):
                act.dma_start(X1[:, (4 * q + 2) * C:(4 * q + 4) * C].rearrange("p (k c) -> p k c", k=2),
                              I["x"][4 * q + 2:4 * q + 4].rearrange("k p c -> p k c")).then_inc(x_loaded[2 * q + 1], 16)
            for t, name in ((prm, "params"), (rgst, "rg_states"), (h0, "h0"), (gbz, "gla_bias")):
                act.dma_start(t, I[name]).then_inc(par_loaded, 16)
            act.dma_start(wg[0:RANK, :], I["gla_w_gate"]).then_inc(const_loaded, 16)
            for t, name in ((reset, "reset"), (rs16, "reset16"), (ident, "ident"), (mask, "mask")):
                act.dma_start(t, I[name]).then_inc(const_loaded, 16)
            act.dma_start(gw, I["rg_gates"][0]).then_inc(gwt_loaded, 16)
            act.dma_start(O["rg_old"], I["rg_old"]).then_inc(stored, 16)
            act.dma_start(O["ffn_old"], I["ffn_old"]).then_inc(stored, 16)
            act.dma_start(sS, I["gla_state"][0]).then_inc(sS_loaded, 16)

            for k in range(KB):
                act.wait_ge(x_loaded[k // 2], 16)
                if k >= 2:
                    act.wait_ge(sum1_done, k - 1)
                nc.scalar.activation((rt, it)[k % 2], blk(X1, k), ACT.Square).then_inc(sq1_done, 1)
            act.preload_act_table_set(LN_EXP)
            act.wait_ge(ones_done, 1)
            act.wait_ge(sum_mm, 1)
            nc.scalar.activation(view3(th), accv[1], ACT.Ln, scale=1.0 / D, bias=cst[:, 0:1]).then_inc(acc_free[1], 1)
            act.wait_ge(acc_free[1], 1)
            nc.scalar.activation(th, th, ACT.Exp, scale=-0.5).then_inc(r1_done, 1)
            for k in range(KB):
                act.wait_ge(xn1_done, k + 1)
                nc.scalar.activation(blk(XH, k), blk(X1, k), ACT.Copy).then_inc(xh1_done, 1)

            act.wait_ge(par_loaded, 64)
            lam = prm[:, RP["lam"]:RP["lam"] + KB]
            nc.scalar.activation(der[:, 0:KB], lam, ACT.Abs).then_inc(set_a, 1)
            act.wait_ge(set_a, 1)
            nc.scalar.activation(der[:, 0:KB], der[:, 0:KB], ACT.Exp, scale=-1.0).then_inc(set_a, 1)
            act.wait_ge(set_a, 2)
            nc.scalar.activation(der[:, 0:KB], der[:, 0:KB], ACT.Ln, bias=1.0).then_inc(set_a, 1)

            ready(0)
            nc.scalar.activation(view3(glr[0:RANK, :]), acc[0][0:RANK, :, 0:NW], ACT.Copy)\
                .then_inc(acc_free[0], 1)
            act.wait_ge(r1_done, 1)
            act.wait_ge(xn1_done, KB)
            act.wait_ge(sum1_done, KB)
            def stage_qk(i):
                for s, g in ((0, 1), (1, 0)):
                    ready(U_QKV + s, 2, i)
                    if not isinstance(i, int):
                        act.wait_ge(qk_stored[s], 16 * i)
                    nc.scalar.activation(view3((rt, it)[s]), accv[g], ACT.Copy).then_inc(acc_free[g], 1)
                    act.wait_ge(acc_free[g], G_QKV[g] + i + 1)
                    act.dma_start(qk_scr[2 * i + s], (rt, it)[s]).then_inc(qk_stored[s], 16)
            stage_qk(0)
            with act.Fori(1, 4) as i:
                stage_qk(i)
            def load_qk(w, c0):
                act.dma_start(hd(qkp, 8, w), qk_scr[:, :, bass.ds(c0, w)].rearrange("k p c -> p k c")).then_inc(qk_loaded, 16)

            def v_copy(n, w, c0, n_k):
                plain()
                act.wait_ge(vT_mm, 2 * n)
                act.wait_ge(A_mm, n_k)
                act.wait_ge(keT_mm, n_k)
                nc.scalar.activation(hd(kk, 8, w), V3[:, :, bass.ds(c0, w)], ACT.Copy).then_inc(vcp_ready, 1)

            def log_gate(nz, z, g, between=None):
                act.wait_ge(z_ready, nz + 1)
                nc.scalar.activation(g, z, ACT.Abs).then_inc(absz_done, 1)
                act.wait_ge(absz_done, nz + 1)
                nc.scalar.activation(g, g, ACT.Exp, scale=-1.0).then_inc(expz_done, 1)
                if between:
                    between()
                act.wait_ge(expz_done, nz + 1)
                nc.scalar.activation(g, g, ACT.Ln, bias=1.0).then_inc(lnz_done, 1)

            def v_tokens(n, w, half):
                act.wait_ge(vT_mm, 2 * n + half + 1)
                act.wait_ge(dS_mm, state_banks(n))
                nc.scalar.activation(vtm[0:w, half * 512:(half + 1) * 512], sb7[0:w, :], ACT.Copy).then_inc(vT_ready, 1)

            def decays(n, w):
                act.wait_ge(bc_ready, n + 1)
                nc.scalar.activation(eb[:, 0:4 * w], bc[:, 0:4 * w], ACT.Exp, scale=1.0 / 16).then_inc(eb_ready, 1)
                act.wait_ge(bl_ready, n + 1)
                nc.scalar.activation(g_t[:, 0:4 * w], bc[:, 0:4 * w], ACT.Exp, scale=-1.0 / 16).then_inc(enb_ready, 1)
                nc.scalar.activation(z_t[:, 0:4 * w], z_t[:, 0:4 * w], ACT.Exp, scale=1.0 / 16).then_inc(eke_ready, 1)

            def ke_tokens(n, w):
                act.wait_ge(keT_mm, n + 1)
                nc.scalar.activation(bc[0:w, :], sb7[0:w, :], ACT.Copy).then_inc(keT_ready, 1)

            def o_square(n, w, c0, hh):
                plain()
                act.wait_ge(o_copied, 2 * n + hh + 1)
                nc.scalar.activation(zg[:, 4 * w * hh:4 * w * (hh + 1)].rearrange("p (k t) -> p k t", k=4),
                                     V3[:, 4 * hh:4 * hh + 4, bass.ds(c0, w)], ACT.Square).then_inc(o_squared, 1)

            def o_rms(nn, out, w):
                act.wait_ge(onorm_mm, nn + 1)
                nc.scalar.activation(out, sb6[:, 0:4 * w], ACT.Ln, scale=1.0 / DV, bias=cst[:, 0:1]).then_inc(olog_done, 1)
                act.wait_ge(olog_done, nn + 1)
                nc.scalar.activation(out, out, ACT.Exp, scale=-0.5).then_inc(orinv_ready, 1)

            for s in range(2):
                act.wait_ge(qk_stored[s], 64)
            act.wait_ge(set_v, 12)
            load_qk(NMETA, 0)
            act.dma_start(hd(sqk, 8, NS), qk_scr[:, :, NT:C].rearrange("k p c -> p k c")).then_inc(sqk_loaded, 16)
            act.preload_act_table_set(LN_EXP)
            log_gate(0, z_t[:, 0:4 * NMETA], g_t[:, 0:4 * NMETA])
            decays(0, NMETA)
            log_gate(1, sdec, srv)
            act.wait_ge(sg_ready, 1)
            nc.scalar.activation(sdec, sdec, ACT.Exp, scale=1.0 / 16).then_inc(s_act, 1)

            def evacuate_v(i, s, g):
                plain()
                ready(U_QKV + 8 + s, 2, i)
                nc.scalar.activation(view3(blk(V, 2 * i + s)), accv[g], ACT.Copy).then_inc(acc_free[g], 1)

            def sample_tokens(q, t, bank):
                act.wait_ge(sT_mm, q + 1)
                nc.scalar.activation(t, bank[0:NS, :], ACT.Copy).then_inc(sT_ready, 1)

            evacuate_v(0, 0, 1)
            sample_tokens(0, skt[0:NS, :], sb7)
            ke_tokens(0, NMETA)
            for used in (qd_ready, kd_ready, ke_ready):
                act.wait_ge(used, 1)
            load_qk(PAIR, NMETA)
            evacuate_v(0, 1, 0)
            with act.Fori(1, 4) as i:
                evacuate_v(i, 0, 1)
                evacuate_v(i, 1, 0)
            act.wait_ge(acc_free[0], G_RG[0])
            act.wait_ge(acc_free[1], G_RG[1])
            v_copy(0, NMETA, 0, 1)
            v_tokens(0, NMETA, 0)
            sample_tokens(1, svt[0:NS, 0:512], sb6)
            v_tokens(0, NMETA, 1)
            sample_tokens(2, svt[0:NS, 512:1024], sb6)
            v_copy(1, PAIR, NMETA, 1)
            o_square(0, NMETA, 0, 0)
            o_square(0, NMETA, 0, 1)
            o_rms(0, qd[:, 0:4 * NMETA], NMETA)
            v_tokens(1, PAIR, 0)

            def rg_tail_exps(m):
                plain()
                act.wait_ge(h_step, 4 * m)
                nc.scalar.activation(av, rt, ACT.Exp, scale=col(der, m + 2 * KB), bias=col(der, m + 2 * KB)).then_inc(a_ready, 1)
                nc.scalar.activation(rt, rt, ACT.Exp, scale=col(der, m + 3 * KB), bias=col(der, m + 3 * KB)).then_inc(a2_ready, 1)

            def rg_tail_mult(m):
                act.wait_ge(w_ready, m + 1)
                nc.scalar.activation(th, th, ACT.Ln, bias=cst[:, 1:2]).then_inc(ml_done, 1)
                act.wait_ge(ml_done, m + 1)
                nc.scalar.activation(th, th, ACT.Exp, scale=0.5).then_inc(m_ready, 1)

            def rg_body(j, first, last):
                n = j + 1
                if not first:
                    rg_tail_exps(j - 1)
                log_gate(j + 2, z_t, g_t, lambda: v_tokens(n, PAIR, 1))
                if not first:
                    rg_tail_mult(j - 1)
                decays(n, PAIR)
                if not first:
                    act.wait_ge(ha_ready, j)
                    act.dma_start(ha_scr[j - 1], gy).then_inc(ha_stored, 16)
                    act.wait_ge(xc_step, 4 * j)
                    act.wait_ge(rgo_kept, j)
                ready(U_RG, 2, j)
                nc.scalar.activation(view3(ext[:, 3:3 + C]), accv[1], ACT.Copy).then_inc(xraw_ready, 1)
                nc.scalar.activation(view3(xc), accv[1], ACT.Identity, scale=par("w3", j), bias=par("b", j))\
                    .then_inc(acc_free[1], 1)
                act.wait_ge(sS_ready, 2 * j + 2)
                act.dma_start(O["gla_sample"][j], sS).then_inc(sS_stored, 16)
                ke_tokens(n, PAIR)
                if not last:
                    v_copy(n + 1, PAIR, NMETA + PAIR * (j + 1), n + 1)
                o_square(n, PAIR, NMETA + PAIR * j, 0)
                o_square(n, PAIR, NMETA + PAIR * j, 1)
                ready(U_RG + 1, 2, j)
                act.wait_ge(ha_stored, 16 * j)
                nc.scalar.activation(view3(gy), accv[0], ACT.Gelu_apprx_tanh).then_inc(acc_free[0], 1)
                plain()
                act.wait_ge(gate_mm, 2 * j + 1)
                nc.scalar.activation(view3(rt), accv[1], ACT.Tanh, scale=0.5, bias=col(der, j)).then_inc(acc_free[1], 1)
                plain()
                act.wait_ge(acc_free[1], G_RG[1] + 2 * j + 2)
                act.wait_ge(b_ready, j)
                nc.scalar.activation(th, rt, ACT.Tanh, scale=col(der, j + 4 * KB), bias=col(der, j + 4 * KB)).then_inc(th_ready, 1)
                plain()
                act.wait_ge(gate_mm, 2 * j + 2)
                act.wait_ge(h_step, 4 * j)
                nc.scalar.activation(view3(it), accv[0], ACT.Tanh, scale=0.5, bias=col(der, j + KB)).then_inc(acc_free[0], 1)
                act.preload_act_table_set(LN_EXP)
                if not last:
                    v_tokens(n + 1, PAIR, 0)
                o_rms(n, qd, PAIR)

            def rg_prefetch(j):
                for used in (qd_ready, kd_ready, ke_ready):
                    act.wait_ge(used, j + 2)
                load_qk(PAIR, NMETA + PAIR * (j + 1))
                act.dma_start(gw, I["rg_gates"][j + 1]).then_inc(gwt_loaded, 16)
                act.wait_ge(sS_stored, 16 * j + 16)
                act.wait_ge(so_mm, j + 1)
                act.dma_start(sS, I["gla_state"][j + 1]).then_inc(sS_loaded, 16)

            rg_body(0, True, False)
            rg_prefetch(0)
            with act.Fori(1, NPAIR - 1) as j:
                rg_body(j, False, False)
                rg_prefetch(j)
            rg_body(NPAIR - 1, False, True)
            act.wait_ge(so_ready, NB)
            act.wait_ge(onorm_mm, NPAIR + 1)
            nc.scalar.activation(hd(zg, 8, NS), V3[:, :, NT:C], ACT.Square).then_inc(s_act, 2)
            rg_tail_exps(NPAIR - 1)
            o_rms(NPAIR + 1, srv, NS)
            rg_tail_mult(NPAIR - 1)
            act.wait_ge(ha_ready, NPAIR)
            act.dma_start(ha_scr[NPAIR - 1], gy).then_inc(ha_stored, 16)
            act.dma_start(O["gla_prompt"], S[:, 0:H * DV]).then_inc(stored, 16)
            act.wait_ge(stored, 48)
            act.wait_ge(ha_stored, 16 * NPAIR)
            act.wait_ge(h_step, 4 * NPAIR)
            act.wait_ge(sS_stored, 16 * NB)
            act.wait_ge(o_ready, NPAIR + 2)

            def gate_o(i):
                for s, g in ((0, 1), (1, 0)):
                    ready(U_GO + s, 2, i)
                    if not isinstance(i, int):
                        act.wait_ge(obl_done, 2 * i + s - 1)
                    nc.scalar.activation(view3(T[s]), accv[g], ACT.Silu).then_inc(acc_free[g], 1)
                    plain()
                    act.wait_ge(og_done, 2 * i + s + 1)
                    nc.scalar.activation(blk(OBH, 2 * i + s), T[s], ACT.Copy).then_inc(obh_done, 1)
            gate_o(0)
            with act.Fori(1, KB // 2) as i:
                gate_o(i)
            with act.Fori(0, KB) as j:
                ready(U_B, 2, j)
                act.wait_ge(acc_free[0], G_B[0] + j)
                nc.scalar.activation(view3(T[2]), accv[1], ACT.Tanh, scale=0.5).then_inc(acc_free[1], 1)
            for k in range(KB):
                if k < KB - 1:
                    act.wait_ge(o_used, k + 1)
                else:
                    ready(U_A - 1)
                act.dma_start(blk(HA, k), ha_scr[k]).then_inc(hl_loaded[k], 16)
            for k in range(KB):
                act.wait_ge(hl_loaded[k], 16)
                nc.scalar.activation(blk(HAH, k), blk(HA, k), ACT.Copy).then_inc(hah_done, 1)
            with act.Fori(0, KB) as j:
                ready(U_A, 2, j)
                act.wait_ge(acc_free[0], G_A[0] + j)
                nc.scalar.activation(view3(T[2]), accv[1], ACT.Tanh, scale=0.5).then_inc(acc_free[1], 1)
            act.wait_ge(acc_free[1], G_OUT[1])
            for k in range(KB):
                act.wait_ge(ma_done, KB if k == KB - 1 else k + 1)
                nc.scalar.activation(blk(MGH, k), blk(MG, k), ACT.Copy, scale=0.5).then_inc(mgh_done, 1)
            for s in range(2):
                act.dma_start(T[s], I["x"][s]).then_inc(xr_loaded[s], 16)
            for k in range(KB):
                act.wait_ge(acc_free[1 - k % 2], G_OUT[0] + k // 2 + 1)
                if k + 2 < KB:
                    act.dma_start(T[k % 2], I["x"][k + 2]).then_inc(xr_loaded[k % 2], 16)
                act.wait_ge(sum2_done, k)
                nc.scalar.activation(T[2], blk(X2, k), ACT.Square).then_inc(sq2_done, 1)
            act.dma_start(fst, I["ffn_states"]).then_inc(fst_loaded, 16)
            act.dma_start(fpr, I["ffn_params"]).then_inc(fst_loaded, 16)
            act.preload_act_table_set(LN_EXP)
            act.wait_ge(sum_mm, 2)
            act.wait_ge(sum2_done, KB)
            nc.scalar.activation(view3(T[2]), accv[1], ACT.Ln, scale=1.0 / D, bias=cst[:, 0:1]).then_inc(acc_free[1], 1)
            act.wait_ge(acc_free[1], G_NORM2 + 1)
            nc.scalar.activation(T[2], T[2], ACT.Exp, scale=-0.5).then_inc(r2_done, 1)
            for k in range(KB):
                act.wait_ge(xn2_done, k + 1)
                nc.scalar.activation(blk(X2H, k), T[k % 2], ACT.Copy).then_inc(xh2_done, 1)

            def ffn_block(F, u0, f, per, i):
                plain()
                act.wait_ge(gconv_step, 3 * F)
                act.wait_ge(gkept, F)
                act.wait_ge(act_done, F)
                ready(u0 + 2 * f, per, i)
                nc.scalar.activation(view3(eg[:, 2:2 + C]), accv[0], ACT.Copy).then_inc(graw_ready, 1)
                nc.scalar.activation(view3(cg), accv[0], ACT.Identity, scale=fpr[:, bass.ds(2 * UB + F, 1)],
                                     bias=fpr[:, bass.ds(3 * UB + F, 1)]).then_inc(acc_free[0], 1)
                plain()
                act.wait_ge(vconv_step, 3 * F)
                act.wait_ge(vkept, F)
                ready(u0 + 2 * f + 1, per, i)
                nc.scalar.activation(view3(ev[:, 2:2 + C]), accv[1], ACT.Copy).then_inc(vraw_ready, 1)
                nc.scalar.activation(view3(cv), accv[1], ACT.Identity, scale=fpr[:, bass.ds(2 * UB + FB + F, 1)],
                                     bias=fpr[:, bass.ds(3 * UB + FB + F, 1)]).then_inc(acc_free[1], 1)
                act.wait_ge(gconv_step, 3 * F + 3)
                nc.scalar.activation(cg, cg, ACT.Gelu_apprx_tanh).then_inc(ggelu_done, 1)
                act.wait_ge(act_done, F + 1)

            def ffn_hi(half, f):
                b = (half * GRP + f) * C
                nc.scalar.activation(AH[:, b:b + C], act_t, ACT.Copy).then_inc(acth_done, 1)

            GU, GD = GRP, KB // 2

            def ffn_group(F0_, u0, per, i, half):
                for f in range(GRP):
                    ffn_block(F0_ + f, u0, f, per, i)
                    ffn_hi(half, f)

            act.wait_ge(set_f, 4)
            ffn_group(0, U_FFN, 0, 0, 0)
            NU, ND = 2 * GRP, GRP
            per, gper = 2 * (NU + ND), 2 * (GU + GD)
            with act.Fori(0, NGRP // 2 - 1) as i:
                ffn_group(2 * GRP * i + GRP, U_FFN + NU, per, i, 1)
                act.wait_ge(acc_free[1], G_FFN[1] + 2 * GU + GD + gper * i)
                ffn_group(2 * GRP * i + 2 * GRP, U_FFN + 2 * NU + ND, per, i, 0)
                act.wait_ge(acc_free[1], G_FFN[1] + 3 * GU + 2 * GD + gper * i)
            n = NGRP // 2 - 1
            ffn_group(GRP * (NGRP - 1), U_FFN + NU + n * per, 0, 0, 1)
            y_use = 2 * GU + GD + gper * n
            for k in range(KB):
                act.wait_ge(acc_free[k % 2], G_FFN[k % 2] + y_use + k // 2 + 1)
                act.wait_ge(sum3_done, k)
                nc.scalar.activation(ysq, blk(X2, k), ACT.Square).then_inc(sq3_done, 1)
            act.preload_act_table_set(LN_EXP)
            act.wait_ge(sum_mm, 3)
            nc.scalar.activation(view3(yrs), accv[0], ACT.Ln, scale=1.0 / D, bias=cst[:, 0:1]).then_inc(lnr3_done, 1)
            act.wait_ge(lnr3_done, 1)
            nc.scalar.activation(yrs, yrs, ACT.Exp, scale=-0.5).then_inc(r3_done, 1)

        @block.vector
        def _(dve):
            nc.vector.memset(ones, 1.0)
            nc.vector.memset(cst[:, 0:1], EPS)
            nc.vector.memset(ext[:, 0:3], 0.0)
            nc.vector.memset(am, 0.0)
            nc.vector.memset(cst[:, 1:2], TINY).then_inc(ones_done, 1)
            def plain():
                dve.wait_ge(ones_done, 1)

            for k in range(KB):
                dve.wait_ge(sq1_done, k + 1)
                if k == 0:
                    nc.vector.tensor_copy(xc, rt).then_inc(sum1_done, 1)
                else:
                    dve.wait_ge(sum1_done, k)
                    nc.vector.tensor_tensor(xc, xc, (rt, it)[k % 2], ALU.add).then_inc(sum1_done, 1)
            dve.wait_ge(par_loaded, 64)
            dve.wait_ge(r1_done, 1)
            for k in range(KB):
                nc.vector.scalar_tensor_tensor(blk(X1, k), blk(X1, k), par("g1", k), th, ALU.mult, ALU.mult)\
                    .then_inc(xn1_done, 1)
                dve.wait_ge(xh1_done, k + 1)
                nc.vector.tensor_tensor(blk(XL, k), blk(X1, k), blk(XH, k).bitcast(F32), ALU.subtract).then_inc(xl1_done, 1)

            steps = [0]

            def step(ins):
                steps[0] += 1
                ins.then_inc(set_v, 1)
                dve.wait_ge(set_v, steps[0])

            st = rgst.rearrange("p (r k b) -> p r k b", r=3, k=KB)

            def wide(name):
                return prm[:, RP[name]:RP[name] + KB].unsqueeze(2).broadcast_to([P, KB, NS])
            pk, tk = hd(rgp, KB, NS), hd(rgtmp, KB, NS)
            step(nc.vector.tensor_tensor(pk, st[:, 0], wide("w0"), ALU.mult))
            for r in (1, 2):
                step(nc.vector.tensor_tensor(tk, st[:, r], wide(f"w{r}"), ALU.mult))
                step(nc.vector.tensor_tensor(pk, pk, tk, ALU.add))
            step(nc.vector.tensor_tensor(pk, pk, wide("b"), ALU.add))
            dve.wait_ge(set_a, 3)
            d = [der[:, i * KB:(i + 1) * KB] for i in range(5)]
            lam = prm[:, RP["lam"]:RP["lam"] + KB]
            step(nc.vector.tensor_scalar(d[1], lam, -1.0, 0.0, ALU.mult, ALU.max))
            step(nc.vector.tensor_tensor(d[4], d[0], d[1], ALU.add))
            step(nc.vector.tensor_scalar(d[2], d[4], -4.0, None, ALU.mult))
            step(nc.vector.tensor_scalar(d[3], d[4], -8.0, None, ALU.mult))
            step(nc.vector.tensor_scalar(d[4], d[4], 4.0, None, ALU.mult))
            step(nc.vector.tensor_scalar(d[0], prm[:, RP["ba"]:RP["ba"] + KB], 0.5, None, ALU.mult))
            step(nc.vector.tensor_scalar(d[1], prm[:, RP["bx"]:RP["bx"] + KB], 0.5, None, ALU.mult))

            def logits(nz, w, z):
                dve.wait_ge(zg_mm, nz + 1)
                nc.vector.tensor_tensor(hd(z, H, w), hd(sb6, H, w), gbz.unsqueeze(2).broadcast_to([P, H, w]), ALU.add)\
                    .then_inc(z_ready, 1)

            def log_sigmoid(nz, z, g, out):
                dve.wait_ge(lnz_done, nz + 1)
                return nc.vector.scalar_tensor_tensor(out, z, 0.0, g, ALU.min, ALU.subtract)

            def running_sum(n, w, cl, reset_t):
                log_sigmoid(n if isinstance(n, int) and n == 0 else n + 1, z_t[:, 0:4 * w], g_t[:, 0:4 * w],
                            g_t[:, 0:4 * w]).then_inc(g_ready, 1)
                dve.wait_ge(g_ready, n + 1)
                dve.wait_ge(dS_mm, state_banks(n))
                nc.vector.tensor_tensor_scan(bc[:, 0:4 * w], reset_t, g_t[:, 0:4 * w], 0.0, ALU.mult, ALU.add)\
                    .then_inc(bc_ready, 1)
                dve.wait_ge(bc_ready, n + 1)
                b = bc[:, 0:4 * w].rearrange("p (c t) -> p c t", t=cl)
                z = z_t[:, 0:4 * w].rearrange("p (c t) -> p c t", t=cl)
                nc.vector.tensor_tensor(z, b[:, :, cl - 1:cl].broadcast_to([P, 4 * w // cl, cl]), b, ALU.subtract)\
                    .then_inc(bl_ready, 1)

            def scaled_qk(n, w):
                dve.wait_ge(qk_loaded, 16 * n + 16)
                dve.wait_ge(eb_ready, n + 1)
                nc.vector.scalar_tensor_tensor(qd[:, 0:4 * w], qkp[:, 0:4 * w], DK ** -0.5, eb[:, 0:4 * w],
                                               ALU.mult, ALU.mult).then_inc(qd_ready, 1)
                if not isinstance(n, int):
                    dve.wait_ge(vT_mm, 2 * n + 2)
                dve.wait_ge(enb_ready, n + 1)
                nc.vector.tensor_tensor(kd[:, 0:4 * w], qkp[:, 4 * w:8 * w], g_t[:, 0:4 * w], ALU.mult).then_inc(kd_ready, 1)
                dve.wait_ge(eke_ready, n + 1)
                nc.vector.tensor_tensor(ke_w(w), qkp[:, 4 * w:8 * w], z_t[:, 0:4 * w], ALU.mult).then_inc(ke_ready, 1)

            def ke_w(w):
                return ke[:, 0:4 * w]

            def scores(n, w):
                dve.wait_ge(const_loaded, 16 * 5)
                dve.wait_ge(A_mm, n + 1)
                nc.vector.copy_predicated(hd(am[0:w], H, w), mask[0:w, 0:w].unsqueeze(1).broadcast_to([w, H, w]),
                                          hd(sb6[0:w], H, w)).then_inc(A_ready, 1)

            def o_copy(n, w, c0, hh, bank):
                plain()
                dve.wait_ge(O_mm, 2 * n + hh + 1)
                nc.vector.tensor_copy(V3[:, 4 * hh:4 * hh + 4, bass.ds(c0, w)], hd(bank, 4, w)).then_inc(o_copied, 1)

            def state(n_bank, w, cl, src, dst, ck, hh, bank):
                dve.wait_ge(dS_mm, n_bank + 1)
                for h in (2 * hh, 2 * hh + 1):
                    last = h * w + (ck + 1) * cl - 1
                    a, b = src * H * DV + h * DV, dst * H * DV + h * DV
                    ins = nc.vector.scalar_tensor_tensor(S[:, b:b + DV], S[:, a:a + DV], eb[:, last:last + 1],
                                                         bank[:, (h % 2) * DV:(h % 2 + 1) * DV], ALU.mult, ALU.add)
                ins.then_inc(S_ready, 1)

            def o_scale(n, w, c0, rinv):
                dve.wait_ge(orinv_ready, n + 1)
                dve.wait_ge(o_copied, 2 * n + 2)
                o = V3[:, :, bass.ds(c0, w)].rearrange("p (h e) t -> p h e t", h=H)
                r = hd(rinv, H, w).unsqueeze(2).broadcast_to([P, H, 2, w])
                nc.vector.tensor_tensor(o, o, r, ALU.mult).then_inc(o_ready, 1)

            dve.wait_ge(const_loaded, 16 * 5)
            logits(0, NMETA, z_t)
            running_sum(0, NMETA, NMETA, rs16)
            logits(1, NS, sdec)
            scaled_qk(0, NMETA)
            log_sigmoid(1, sdec, srv, sdec).then_inc(sg_ready, 1)
            dve.wait_ge(sqk_loaded, 16)
            nc.vector.tensor_scalar(sqk[:, 0:H * NS], sqk[:, 0:H * NS], DK ** -0.5, None, ALU.mult).then_inc(sg_ready, 1)
            scores(0, NMETA)
            o_copy(0, NMETA, 0, 0, sb7)
            o_copy(0, NMETA, 0, 1, sb6)
            for hh, bank in ((0, sb7), (1, sb6)):
                dve.wait_ge(dS_mm, hh + 1)
                nc.vector.tensor_copy(S[:, hh * 2 * DV:(hh + 1) * 2 * DV], bank[:, :]).then_inc(S_ready, 1)
            o_scale(0, NMETA, 0, qd)
            def sample_state(j):
                dve.wait_ge(sS_loaded, 16 * j + 16)
                for hh, bank in ((0, sb7), (1, sb6)):
                    dve.wait_ge(skv_mm, 2 * j + hh + 1)
                    for h in (2 * hh, 2 * hh + 1):
                        t = sS[:, h * DV:(h + 1) * DV]
                        ins = nc.vector.scalar_tensor_tensor(t, t, sdec[:, bass.ds(h * NS + j, 1)],
                                                             bank[:, (h % 2) * DV:(h % 2 + 1) * DV], ALU.mult, ALU.add)
                    ins.then_inc(sS_ready, 1)

            def rg_tail_w(m):
                dve.wait_ge(acc_free[0], G_RG[0] + 2 * m + 2)
                nc.vector.scalar_tensor_tensor(it, it, 1.0, xc, ALU.add, ALU.mult).then_inc(ix_ready, 1)
                dve.wait_ge(a2_ready, m + 1)
                dve.wait_ge(th_ready, m + 1)
                nc.vector.scalar_tensor_tensor(th, rt, 1.0, th, ALU.add, ALU.mult).then_inc(w_ready, 1)

            def rg_tail_b(m):
                dve.wait_ge(m_ready, m + 1)
                dve.wait_ge(ix_ready, m + 1)
                nc.vector.scalar_tensor_tensor(it, it, 0.5, th, ALU.mult, ALU.mult).then_inc(b_ready, 1)

            def rg_tail_h(m):
                dve.wait_ge(a_ready, m + 1)
                dve.wait_ge(b_ready, m + 1)
                nc.vector.tensor_tensor(xc[:, NT:C], av[:, NT:C], col(h0, m, NS, NS), ALU.mult).then_inc(h_step, 1)
                nc.vector.tensor_tensor_scan(xc[:, 0:NT], av[:, 0:NT], it[:, 0:NT], 0.0, ALU.mult, ALU.add).then_inc(h_step, 1)
                dve.wait_ge(h_step, 4 * m + 1)
                nc.vector.tensor_tensor(xc[:, NT:C], xc[:, NT:C], it[:, NT:C], ALU.add).then_inc(h_step, 1)
                plain()
                dve.wait_ge(h_step, 4 * m + 3)
                nc.vector.tensor_copy(col(hco, m, HW, HW), xc[:, NT - 1:C]).then_inc(h_step, 1)
                dve.wait_ge(acc_free[0], G_RG[0] + 2 * m + 1)
                nc.vector.tensor_tensor(gy, xc, gy, ALU.mult).then_inc(ha_ready, 1)

            def rg_body(j, first):
                n = j + 1
                logits(j + 2, PAIR, z_t)
                dve.wait_ge(skv_mm, 2 * j)
                dve.wait_ge(sT_ready, 3)
                nc.vector.tensor_scalar(skm[0:NS, :], skt[0:NS, :], ident[0:NS, bass.ds(j, 1)], None, ALU.mult)\
                    .then_inc(skm_ready, 1)
                if not first:
                    rg_tail_w(j - 1)
                running_sum(n, PAIR, CH, reset)
                sample_state(j)
                if not first:
                    rg_tail_b(j - 1)
                scaled_qk(n, PAIR)
                plain()
                dve.wait_ge(so_mm, j + 1)
                nc.vector.tensor_copy(V3[:, :, bass.ds(NT + j, 1)], hd(sb7, 8, 1)).then_inc(so_ready, 1)
                if not first:
                    rg_tail_h(j - 1)
                scores(n, PAIR)
                c0 = NMETA + PAIR * j
                nb = state_banks(n)
                dve.wait_ge(acc_free[1], G_RG[1] + 2 * j + 1)
                dve.wait_ge(xraw_ready, j + 1)
                for t in range(3):
                    if t == 2:
                        state(nb, PAIR, CH, 0, 1, 0, 0, sb6)
                        state(nb + 1, PAIR, CH, 0, 1, 0, 1, sb7)
                    dve.wait_ge(xc_step, 4 * j + t)
                    nc.vector.scalar_tensor_tensor(xc[:, 0:NT], ext[:, t:t + NT], par(f"w{t}", j), xc[:, 0:NT],
                                                   ALU.mult, ALU.add).then_inc(xc_step, 1)
                nc.vector.scalar_tensor_tensor(xc[:, NT:C], ext[:, NT + 3:C + 3], par("w3", j), col(rgp, j, NS, NS),
                                               ALU.mult, ALU.add).then_inc(xc_step, 1)
                nc.vector.tensor_copy(col(rgo, j, RGW, RGW), ext[:, C + 3 - RGW:C + 3]).then_inc(rgo_kept, 1)
                o_copy(n, PAIR, c0, 0, sb6)
                o_copy(n, PAIR, c0, 1, sb7)
                state(nb + 2, PAIR, CH, 1, 0, 1, 0, sb6)
                state(nb + 3, PAIR, CH, 1, 0, 1, 1, sb7)
                o_scale(n, PAIR, c0, qd)

            dve.wait_ge(s_act, 1)
            dve.wait_ge(sg_ready, 2)
            dve.wait_ge(set_v, steps[0])
            rg_body(0, True)
            with dve.Fori(1, NPAIR) as j:
                rg_body(j, False)
            rg_tail_w(NPAIR - 1)
            rg_tail_b(NPAIR - 1)
            rg_tail_h(NPAIR - 1)
            dve.wait_ge(orinv_ready, NPAIR + 2)
            dve.wait_ge(so_ready, NB)
            o = V3[:, :, NT:C].rearrange("p (h e) t -> p h e t", h=H)
            nc.vector.tensor_tensor(o, o, hd(srv, H, NS).unsqueeze(2).broadcast_to([P, H, 2, NS]), ALU.mult).then_inc(o_ready, 1)
            dve.wait_ge(o_ready, NPAIR + 2)

            with dve.Fori(0, KB // 2) as i:
                for s, g in ((0, 1), (1, 0)):
                    k = 2 * i + s
                    dve.wait_ge(acc_free[g], G_GO[g] + i + 1)
                    nc.vector.scalar_tensor_tensor(T[s], blk(V, k), par("gn", k), T[s], ALU.mult, ALU.mult).then_inc(og_done, 1)
                    dve.wait_ge(obh_done, k + 1)
                    nc.vector.tensor_tensor(blk(OBL, k), T[s], blk(OBH, k).bitcast(F32), ALU.subtract).then_inc(obl_done, 1)
            with dve.Fori(0, KB) as j:
                dve.wait_ge(acc_free[1], G_B[1] + j + 1)
                dve.wait_ge(unit_done[0], nth(U_B + 1, 2, j) + 1)
                nc.vector.scalar_tensor_tensor(view3(blk(MG, j)), view3(T[2]), 1.0, accv[0], ALU.add, ALU.mult)\
                    .then_inc(acc_free[0], 1)
            for k in range(KB):
                dve.wait_ge(hah_done, k + 1)
                nc.vector.tensor_tensor(blk(HAL, k), blk(HA, k), blk(HAH, k).bitcast(F32), ALU.subtract).then_inc(hal_done, 1)

            def merged_low(k):
                dve.wait_ge(mgh_done, k + 1)
                nc.vector.scalar_tensor_tensor(blk(MGL, k), blk(MG, k), 0.5, blk(MGH, k).bitcast(F32), ALU.mult, ALU.subtract)\
                    .then_inc(mgl_done, 1)

            def merge(j):
                dve.wait_ge(acc_free[1], G_A[1] + j + 1)
                dve.wait_ge(unit_done[0], nth(U_A + 1, 2, j) + 1)
                nc.vector.scalar_tensor_tensor(view3(T[0]), view3(T[2]), 1.0, accv[0], ALU.add, ALU.mult)\
                    .then_inc(acc_free[0], 1)
                dve.wait_ge(acc_free[0], G_A[0] + j + 1)
                nc.vector.tensor_tensor(blk(MG, j), blk(MG, j), T[0], ALU.add).then_inc(ma_done, 1)
                dve.wait_ge(ma_done, j + 1)
            with dve.Fori(0, KB - 1) as j:
                merge(j)
            for k in range(KB - 1):
                merged_low(k)
            merge(KB - 1)
            merged_low(KB - 1)
            def out_block(i, s, g, first):
                k = 2 * i + s
                dve.wait_ge(unit_done[g], nth(U_OUT + s, 2, i) + 1)
                dve.wait_ge(xr_loaded[s], 16 * i + 16)
                nc.vector.tensor_tensor(view3(blk(X2, k)), accv[g], view3(T[s]), ALU.add)\
                    .then_inc(acc_free[g], 1)
                dve.wait_ge(sq2_done, k + 1)
                if first:
                    nc.vector.tensor_copy(sqsum, T[2]).then_inc(sum2_done, 1)
                else:
                    dve.wait_ge(sum2_done, k)
                    nc.vector.tensor_tensor(sqsum, sqsum, T[2], ALU.add).then_inc(sum2_done, 1)
            out_block(0, 0, 1, True)
            out_block(0, 1, 0, False)
            with dve.Fori(1, KB // 2) as i:
                out_block(i, 0, 1, False)
                out_block(i, 1, 0, False)
            dve.wait_ge(fst_loaded, 32)
            fs = fst.rearrange("p (r k b) -> p r k b", r=2, k=UB)

            def fwide(r):
                return fpr[:, r * UB:(r + 1) * UB].unsqueeze(2).broadcast_to([P, UB, NS])
            pf = hd(fps, UB, NS)
            nc.vector.tensor_tensor(pf, fs[:, 0], fwide(0), ALU.mult).then_inc(set_f, 1)
            nc.vector.tensor_tensor(fs[:, 1], fs[:, 1], fwide(1), ALU.mult).then_inc(set_f, 1)
            dve.wait_ge(set_f, 2)
            nc.vector.tensor_tensor(pf, pf, fs[:, 1], ALU.add).then_inc(set_f, 1)
            dve.wait_ge(set_f, 3)
            nc.vector.memset(eg[:, 0:2], 0.0)
            nc.vector.memset(ev[:, 0:2], 0.0)
            nc.vector.tensor_tensor(pf, pf, fwide(3), ALU.add).then_inc(set_f, 1)
            dve.wait_ge(r2_done, 1)
            for k in range(KB):
                if k >= 2:
                    dve.wait_ge(xl2_done, k - 1)
                nc.vector.scalar_tensor_tensor(T[k % 2], blk(X2, k), par("g2", k), T[2], ALU.mult, ALU.mult).then_inc(xn2_done, 1)
                dve.wait_ge(xh2_done, k + 1)
                nc.vector.tensor_tensor(blk(X2L, k), T[k % 2], blk(X2H, k).bitcast(F32), ALU.subtract).then_inc(xl2_done, 1)
            dve.wait_ge(set_f, 4)
            dve.wait_ge(xl2_done, KB)

            def conv(F, off_b, ready_sem, ready_n, raw_sem, e_t, c_t, step_sem, kept):
                dve.wait_ge(ready_sem, ready_n)
                dve.wait_ge(raw_sem, F + 1)
                for t in range(2):
                    dve.wait_ge(step_sem, 3 * F + t)
                    nc.vector.scalar_tensor_tensor(c_t[:, 0:NT], e_t[:, t:t + NT], fpr[:, bass.ds(t * UB + off_b + F, 1)],
                                                   c_t[:, 0:NT], ALU.mult, ALU.add).then_inc(step_sem, 1)
                nc.vector.scalar_tensor_tensor(c_t[:, NT:C], e_t[:, NT + 2:C + 2], fpr[:, bass.ds(2 * UB + off_b + F, 1)],
                                               fps[:, bass.ds((off_b + F) * NS, NS)], ALU.mult, ALU.add).then_inc(step_sem, 1)
                nc.vector.tensor_copy(ubuf[:, bass.ds((off_b + F) * UW, UW)], e_t[:, C + 2 - UW:C + 2]).then_inc(kept, 1)

            def ffn_block(F, grp, half, f, adds):
                conv(F, 0, acc_free[0], G_FFN[0] + grp + 1, graw_ready, eg, cg, gconv_step, gkept)
                conv(F, FB, acc_free[1], G_FFN[1] + grp + 1, vraw_ready, ev, cv, vconv_step, vkept)
                adds(0)
                dve.wait_ge(ggelu_done, F + 1)
                dve.wait_ge(vconv_step, 3 * F + 3)
                dve.wait_ge(acth_done, F)
                dve.wait_ge(actl_done, F)
                nc.vector.tensor_tensor(act_t, cg, cv, ALU.mult).then_inc(act_done, 1)
                adds(1)
                dve.wait_ge(acth_done, F + 1)
                b = (half * GRP + f) * C
                nc.vector.tensor_tensor(AL[:, b:b + C], act_t, AH[:, b:b + C].bitcast(F32), ALU.subtract).then_inc(actl_done, 1)

            def add(n_down, grp, m, u_last, per, i):
                g = m % 2
                if m < KB - 1:
                    dve.wait_ge(down_mm, (KB - 1) * n_down + m + 1)
                else:
                    dve.wait_ge(unit_done[slot_of(u_last)], nth(u_last, per, i) + 1)
                dve.wait_ge(acc_free[g], G_FFN[g] + grp + m // 2)
                nc.vector.tensor_tensor(view3(blk(X2, m)), accv[g], view3(blk(X2, m)), ALU.add).then_inc(acc_free[g], 1)

            def ffn_group(F0_, grp0, half, n_down=None, u_last=0, per=0, i=0):
                def down(m):
                    add(n_down, grp0 + GRP, m, u_last, per, i)
                for f in range(GRP):
                    last = f == GRP - 1 and n_down is not None
                    ffn_block(F0_ + f, grp0 + f, half, f, down if last else lambda k: None)
                if n_down is not None:
                    for m in range(2, KB):
                        down(m)

            GU, GD = GRP, KB // 2
            NU, ND = 2 * GRP, GRP
            per, gper = 2 * (NU + ND), 2 * (GU + GD)
            ffn_group(0, 0, 0)
            with dve.Fori(0, NGRP // 2 - 1) as i:
                ffn_group(2 * GRP * i + GRP, GU + gper * i, 1, 2 * i, U_FFN + 2 * NU + ND - 1, per, i)
                ffn_group(2 * GRP * i + 2 * GRP, 2 * GU + GD + gper * i, 0, 2 * i + 1, U_FFN + 3 * NU + 2 * ND - 1, per, i)
            n = NGRP // 2 - 1
            ffn_group(GRP * (NGRP - 1), GU + gper * n, 1, 2 * n, U_FFN + 2 * NU + ND - 1 + n * per)
            for m in range(KB):
                add(NGRP - 1, 2 * GU + GD + gper * n, m, N_UNITS - 1, 0, 0)
                dve.wait_ge(sq3_done, m + 1)
                if m == 0:
                    nc.vector.tensor_copy(ysum, ysq).then_inc(sum3_done, 1)
                else:
                    dve.wait_ge(sum3_done, m)
                    nc.vector.tensor_tensor(ysum, ysum, ysq, ALU.add).then_inc(sum3_done, 1)
            dve.wait_ge(r3_done, 1)
            for k in range(KB):
                if k >= 2:
                    dve.wait_ge(y_stored[k % 2], 16 * (k // 2))
                nc.vector.scalar_tensor_tensor(T[k % 2], blk(X2, k), par("gf", k), yrs, ALU.mult, ALU.mult).then_inc(y_done, 1)


def weight_units(w_in, w_a, w_b, w_out, w_up, w_down):
    import numpy as np

    def column_units(w):
        n = w.shape[1] // P
        return w.reshape(KB, P, n, P).transpose(2, 1, 0, 3).reshape(n, P, D)

    edges = np.cumsum([D, D, QK, QK, D, RANK, D, D, D])
    rg_x, rg_y, q, k, v, low, go, m_a, m_b = np.split(w_in, edges[:-1], axis=1)
    low = np.concatenate([low, np.zeros((D, P - RANK), w_in.dtype)], axis=1)

    def paired(a, b):
        return np.stack([column_units(a), column_units(b)], axis=1).reshape(-1, P, D)

    ups = paired(w_up[:, :FF], w_up[:, FF:])

    def down_units(g):
        t = w_down[g * GRP * P:(g + 1) * GRP * P].reshape(GRP, P, KB, P).transpose(2, 0, 1, 3)
        return t.reshape(GRP, KB, P, P).transpose(0, 2, 1, 3).reshape(GRP, P, D)

    parts = [column_units(low), column_units(q), column_units(k), column_units(v), paired(rg_x, rg_y),
             column_units(go), paired(m_b, w_b), paired(m_a, w_a), column_units(w_out)]
    n = 2 * GRP
    parts.append(ups[:n])
    for g in range(1, NGRP):
        parts += [ups[g * n:(g + 1) * n], down_units(g - 1)]
    parts.append(down_units(NGRP - 1))
    return np.ascontiguousarray(np.concatenate(parts))


def kernel(**inputs):
    import ml_dtypes
    import numpy as np
    from concourse import bacc
    from concourse.bass_utils import run_bass_kernel_spmd

    a = {k: np.asarray(v) for k, v in inputs.items()}
    f32 = np.float32

    def by_partition(rows):
        r = rows.reshape(rows.shape[:-1] + (-1, P))
        return np.moveaxis(r, -1, 0)

    def samples_last(s, r0, r1):
        t = by_partition(s[:, r0:r1])
        t = t.transpose(0, 2, 3, 1)
        return np.concatenate([t, np.zeros(t.shape[:3] + (NS - NB,), f32)], axis=3)

    tokens = np.concatenate([a["meta_tokens"], a["x_prompt"][0], a["x_sample"][:, 0], np.zeros((NS - NB, D), f32)])
    x = np.ascontiguousarray(tokens.T.reshape(KB, P, C))
    vecs = [a["rg_conv_w"][0][i] for i in range(4)] + [a["rg_conv_b"][0], a["rg_ba"][0], a["rg_bx"][0],
            a["rg_lambda"][0], a["norm1_g"][0], a["gla_norm_g"][0].reshape(-1), a["norm2_g"][0], a["final_norm_g"]]
    gates = np.zeros((KB, P, 2, P), f32)
    for c, w in enumerate((a["rg_wa"][0], a["rg_wx"][0])):
        w = w.reshape(KB, 2, 64, 64)
        gates[:, 0:64, c, 0:64] = w[:, 0]
        gates[:, 64:128, c, 64:128] = w[:, 1]
    t = np.arange(P)
    ins = {
        "x": x,
        "w": weight_units(a["w_in"][0], a["w_branch_a"][0], a["w_branch_b"][0], a["w_out"][0], a["w_ffn_up"][0],
                          a["w_ffn_down"][0]),
        "params": np.ascontiguousarray(by_partition(np.stack(vecs)).reshape(P, RP_N)),
        "rg_states": np.ascontiguousarray(samples_last(a["state_rg_conv"][0], 0, 3).reshape(P, -1)),
        "h0": np.ascontiguousarray(samples_last(a["state_rg_h"][0][:, None], 0, 1).reshape(P, -1)),
        "rg_old": np.ascontiguousarray(a["state_rg_conv"][0][:, 1:].reshape(16, -1)),
        "ffn_old": np.ascontiguousarray(a["state_ffn_conv"][0][:, 1:].reshape(16, -1)),
        "gla_bias": np.ascontiguousarray(by_partition(a["gla_b_gate"][0])),
        "gla_w_gate": np.ascontiguousarray(a["gla_w_gate"][0]),
        "gla_state": np.ascontiguousarray(a["state_gla"][0].transpose(0, 2, 1, 3).reshape(NB, P, H * DV)),
        "rg_gates": gates.reshape(KB, P, 2 * P),
        "ffn_states": np.ascontiguousarray(samples_last(a["state_ffn_conv"][0], 0, 2).reshape(P, -1)),
        "ffn_params": np.ascontiguousarray(by_partition(np.concatenate([a["ffn_conv_w"][0], a["ffn_conv_b"]])).reshape(P, -1)),
        "reset": np.tile((np.arange(4 * PAIR) % CH != 0), (P, 1)).astype(ml_dtypes.bfloat16),
        "reset16": np.tile((np.arange(4 * NMETA) % NMETA != 0), (P, 1)).astype(ml_dtypes.bfloat16),
        "ident": np.eye(P, dtype=f32),
        "mask": ((t[None, :] >= t[:, None]) & (t[None, :] // CH == t[:, None] // CH)).astype(np.int32),
    }
    out_shapes = {
        "y": (KB, P, C), "gla_prompt": (P, H * DV), "gla_sample": (NB, P, H * DV), "rg_last": (P, KB * RGW),
        "h_last": (P, KB * HW), "u_last": (P, UB * UW), "rg_old": ins["rg_old"].shape, "ffn_old": ins["ffn_old"].shape,
    }
    nc = bacc.Bacc("TRN2", target_bir_lowering=False, num_devices=1)
    I = {n: nc.dram_tensor(f"in_{n}", v.shape, mybir.dt.from_np(v.dtype), kind="ExternalInput").ap() for n, v in ins.items()}
    O = {n: nc.dram_tensor(f"out_{n}", s, F32, kind="ExternalOutput").ap() for n, s in out_shapes.items()}
    build(nc, I, O)
    got = run_bass_kernel_spmd(nc, [{f"in_{n}": v for n, v in ins.items()}], core_ids=[0]).results[0]
    o = {n: np.asarray(got[f"out_{n}"]) for n in out_shapes}

    y = o["y"].reshape(D, C).T
    def rows(packed, n, w):
        return packed.reshape(P, n, w).transpose(2, 1, 0).reshape(w, n * P)
    rg, h, u = rows(o["rg_last"], KB, RGW), rows(o["h_last"], KB, HW), rows(o["u_last"], UB, UW)
    rg_old = o["rg_old"].reshape(NB, 2, D)
    ffn_old = o["ffn_old"].reshape(NB, 1, 2 * FF)
    c = np.ascontiguousarray
    return (
        c(y[NMETA:NT])[None], c(y[NT:NT + NB])[:, None],
        c(rg[0:3])[None, None], c(h[0])[None, None],
        c(o["gla_prompt"].reshape(P, H, DV).transpose(1, 0, 2))[None, None], c(u[0:2])[None, None],
        np.concatenate([rg_old, rg[3:3 + NB][:, None]], axis=1)[None], c(h[1:1 + NB])[None],
        c(o["gla_sample"].reshape(NB, P, H, DV).transpose(0, 2, 1, 3))[None],
        np.concatenate([ffn_old, u[2:2 + NB][:, None]], axis=1)[None],
    )
```

```python
from contextlib import ExitStack

import concourse.bass as bass
from concourse import mybir

ALU = mybir.AluOpType
ACT = mybir.ActivationFunctionType
F32 = mybir.dt.float32
F32R = mybir.dt.float32r
BF16 = mybir.dt.bfloat16
I32 = mybir.dt.int32
LN_EXP = "natural_log_exp_and_others"

P = 128
D = 1024
KB = D // P
NMETA = 16
SEQ = 1024
NT = NMETA + SEQ
NB = 8
NS = 10
C = NT + NS
NW = C // 3
H = 4
DK = 128
DV = 256
QK = H * DK
RANK = 16
CH = 64
PAIR = 2 * CH
NPAIR = SEQ // PAIR
FF = 3 * D
FB = FF // P
UB = 2 * FB
GRP = 3
NGRP = FB // GRP
RGW = 13
HW = 11
UW = 12
EPS = 1e-6
TINY = 2.0 ** -63

U_QKV = 1
U_RG = U_QKV + 16
U_GO = U_RG + 16
U_B = U_GO + 8
U_A = U_B + 16
U_OUT = U_A + 16
U_FFN = U_OUT + 8
N_UNITS = U_FFN + UB + FB
G_QKV = (1, 0)
G_RG = (9, 8)
G_GO = (25, 24)
G_B = (29, 28)
G_A = (37, 36)
G_OUT = (45, 44)
G_FFN = (49, 48)
G_FINAL = 49 + (UB + KB * NGRP) // 2

RP = {n: i * KB for i, n in enumerate(["w0", "w1", "w2", "w3", "b", "ba", "bx", "lam", "g1", "gn", "g2", "gf"])}
RP_N = 12 * KB



def view3(t):
    return t.rearrange("p (a n) -> p a n", a=3)


def hd(t, n, w):
    return t[:, 0:n * w].rearrange("p (h t) -> p h t", h=n)


def state_banks(n):
    return 0 if isinstance(n, int) and n == 0 else 4 * n - 2


def slot_of(u):
    return u % 2


def nth(u, per=0, i=0):
    return u // 2 + per // 2 * i


def build(nc, I, O):
    ctx = ExitStack()
    with ctx:
        base = 16512
        CB = 4 * C
        TB = (CB + 31) // 32 * 32

        def at(name, off, cols, dt=F32, parts=P):
            return nc.alloc_sbuf_tensor_at(name, [parts, cols], dt, offset=base + off)[:, :]

        A0 = 0
        V0 = 16 * CB
        W0 = V0 + KB * CB
        R0 = W0 + 6 * 4096
        B0 = R0
        M0 = B0 + KB * CB
        T0 = M0 + KB * CB
        E0 = T0 + 3 * TB
        XH, XL = at("xn_hi", A0, KB * C, F32R), at("xn_lo", A0 + KB * CB, KB * C, F32R)
        X1 = at("x_in", V0, KB * C)
        V = at("v_o", V0, KB * C)
        raw = [at(f"w_raw{s}", W0 + 4096 * s, D) for s in range(2)]
        whi = [at(f"w_hi{s}", W0 + 8192 + 8192 * s, D, F32R) for s in range(2)]
        wlo = [at(f"w_lo{s}", W0 + 12288 + 8192 * s, D, F32R) for s in range(2)]
        off = [R0]

        def nxt(name, cols, dt=F32, size=4, parts=P):
            t = at(name, off[0], cols, dt, parts)
            off[0] += (cols * size + 31) // 32 * 32
            return t

        ext = nxt("rg_ext", C + 3)
        xc = nxt("rg_xc_h", C)
        rt = nxt("rg_r", C)
        it = nxt("rg_i_b", C)
        av = nxt("rg_a", C)
        th = nxt("rg_mult", C)
        gy = nxt("rg_gelu_ha", C)
        zg = nxt("gla_z_g_osq", 8 * PAIR)
        z_t, g_t = zg[:, 0:4 * PAIR], zg[:, 4 * PAIR:8 * PAIR]
        bc = nxt("gla_bc_keT", 4 * PAIR)
        eb = nxt("gla_exp_bc", 4 * PAIR)
        kk = nxt("gla_kd_ke_vcopy", 8 * PAIR)
        kd, ke = kk[:, 0:4 * PAIR], kk[:, 4 * PAIR:8 * PAIR]
        qd = nxt("gla_qd", 4 * PAIR)
        vtm = nxt("gla_v_tokens", D)
        am = nxt("gla_scores", 4 * PAIR)
        S = nxt("gla_state", 2 * H * DV)
        qkp_at = off[0]
        qkp = nxt("gla_qk_pair", 8 * PAIR)
        rgst = at("rg_states", qkp_at, 3 * KB * NS)
        rgtmp = at("rg_states_tmp", qkp_at + 1024, KB * NS)
        glr = nxt("gla_low_rank", C)
        gw = nxt("rg_gate_weights", 2 * P)
        sS = nxt("smp_state", H * DV)
        svb = nxt("smp_v_rows", D)
        svt = svb
        wg = nxt("gla_gate_weights", QK)
        reset = nxt("scan_reset", 4 * PAIR, BF16, 2)
        rs16 = nxt("scan_reset16", 4 * NMETA, BF16, 2)
        ident = nxt("ident", P)
        mask = nxt("causal_mask", P, I32)
        rgp = nxt("rg_smp_conv", KB * NS)
        h0 = nxt("rg_h0", KB * NS)
        der = nxt("rg_derived", 5 * KB)
        gbz = nxt("gla_bias", H)
        sqk = nxt("smp_qk", 8 * NS)
        sdec = nxt("smp_decay", H * NS)
        srv = nxt("smp_rinv", H * NS)
        off[0] = max(off[0], E0)
        rgo = nxt("rg_last_columns", KB * RGW)
        hco = nxt("h_last_columns", KB * HW)
        prm = nxt("params", RP_N)
        ones = nxt("ones", P)
        cst = nxt("consts", 2)
        rms = nxt("rms", C)
        assert off[0] + base <= 229344, off[0] + base
        OBH, OBL = at("o_hi", B0, KB * C, F32R), at("o_lo", V0, KB * C, F32R)
        HAH, HAL = at("h_hi", V0, KB * C, F32R), at("h_lo", B0, KB * C, F32R)
        HA = at("h", B0, KB * C)
        MG = at("merged", M0, KB * C)
        MGH, MGL = at("merged_hi", A0, KB * C, F32R), at("merged_lo", A0 + KB * CB, KB * C, F32R)
        X2 = at("residual", V0, KB * C)
        X2H, X2L = at("xn2_hi", B0, KB * C, F32R), at("xn2_lo", M0, KB * C, F32R)
        T = [at(f"tmp{i}", T0 + TB * i, C) for i in range(3)]
        sqsum = T[2]
        act_bytes = (2 * GRP * CB + 31) // 32 * 32
        AH = at("act_hi", A0, 2 * GRP * C, F32R)
        AL = at("act_lo", A0 + act_bytes, 2 * GRP * C, F32R)
        fst = at("ffn_states", A0, 2 * UB * NS)
        F0 = A0 + 2 * act_bytes
        eg = at("gate_ext", F0, C + 2)
        ev = at("val_ext", F0 + TB, C + 2)
        cg = at("gate_conv", F0 + 2 * TB, C)
        fpr = at("ffn_params", F0 + 3 * TB, 4 * UB)
        fps = at("ffn_smp_conv", F0 + 3 * TB + 768, UB * NS)
        assert F0 + 3 * TB + 768 + 4 * UB * NS <= V0
        cv, act_t, ubuf = T[0], T[1], at("u_last_columns", T0 + 2 * TB, UB * UW)
        ysq, ysum, yrs = at("y_square", F0, C), at("y_square_sum", F0 + TB, C), at("y_rms", F0 + 2 * TB, C)

        acc = [ctx.enter_context(nc.psum_tensor(f"acc{s}", [P, 3, 512], F32)) for s in range(2)]
        sb6 = ctx.enter_context(nc.psum_tensor("small6", [P, 512], F32))
        sb7 = ctx.enter_context(nc.psum_tensor("small7", [P, 512], F32))
        accv = [a[:, :, 0:NW] for a in acc]

        qk_scr = nc.dram_tensor("qk_scratch", (8, P, C), F32).ap()
        sv_scr = nc.dram_tensor("smp_v_scratch", (NB, D), F32).ap()
        ha_scr = nc.dram_tensor("ha_scratch", (KB, P, C), F32).ap()

        def sem(n):
            return ctx.enter_context(nc.semaphore(n))

        def sems(n, k=2):
            return [sem(f"{n}{i}") for i in range(k)]

        def col(t, j, n=1, w=1):
            return t[:, bass.ds(j * w, n)]

        def blk(t, j):
            return t[:, bass.ds(j * C, C)]

        def par(name, j):
            return prm[:, bass.ds(j + RP[name], 1)]

        def squares(w):
            return zg[:, 0:8 * w].rearrange("p (h e t) -> p h e t", h=H, e=2)

        V3 = V.rearrange("p (k c) -> p k c", k=KB)

        w_loaded, w_hi_done, w_split, unit_done = sems("w_loaded"), sems("w_hi_done"), sems("w_split"), sems("unit_done")
        acc_free = sems("acc_free")
        sum_mm, gate_mm, down_mm = sem("sum_mm"), sem("gate_mm"), sem("down_mm")
        x_loaded, prm_loaded = sems("x_loaded", KB), sem("prm_loaded")
        par_loaded, const_loaded, gwt_loaded = sem("par_loaded"), sem("const_loaded"), sem("gwt_loaded")
        sq1_done, sum1_done, sum1_mm, lnr1_done, r1_done = (
            sem(n) for n in ("sq1_done", "sum1_done", "sum1_mm", "lnr1_done", "r1_done"))
        xh1_done, xl1_done = sem("xh1_done"), sem("xl1_done")
        set_v, set_a = sem("set_v"), sem("set_a")
        pads_done, ones_done = sem("pads_done"), sem("ones_done")
        qk_stored = sems("qk_stored")
        qk_loaded = sem("qk_loaded")
        zg_mm, z_ready, absz_done, expz_done, lnz_done = (sem(n) for n in ("zg_mm", "z_ready", "absz_done", "expz_done", "lnz_done"))
        g_ready, bc_ready, bl_ready, eb_ready, enb_ready, eke_ready = (
            sem(n) for n in ("g_ready", "bc_ready", "bl_ready", "eb_ready", "enb_ready", "eke_ready"))
        qd_ready, kd_ready, ke_ready = sem("qd_ready"), sem("kd_ready"), sem("ke_ready")
        vT_mm, vT_ready, keT_mm, keT_ready, A_mm, A_ready = (
            sem(n) for n in ("vT_mm", "vT_ready", "keT_mm", "keT_ready", "A_mm", "A_ready"))
        vcp_ready = sem("vcp_ready")
        dS_mm, S_ready, O_mm, o_copied, o_squared, o_summed = (
            sem(n) for n in ("dS_mm", "S_ready", "O_mm", "o_copied", "o_squared", "o_summed"))
        onorm_mm, olog_done, orinv_ready, o_ready = (sem(n) for n in ("onorm_mm", "olog_done", "orinv_ready", "o_ready"))
        sqk_loaded, sT_mm, sT_ready, sg_ready, sS_loaded, sS_stored = (
            sem(n) for n in ("sqk_loaded", "sT_mm", "sT_ready", "sg_ready", "sS_loaded", "sS_stored"))
        sv_stored, svb_loaded, sS_decayed, sS_ready, so_mm, so_ready = (
            sem(n) for n in ("sv_stored", "svb_loaded", "sS_decayed", "sS_ready", "so_mm", "so_ready"))
        s_act = sem("s_act")
        xbias_ready, xc_step, rgo_kept, gelu_ready, r_ready, i_ready, th_ready, a_ready, a2_ready, w_ready, ml_done, m_ready = (
            sem(n) for n in ("xbias_ready", "xc_step", "rgo_kept", "gelu_ready", "r_ready", "i_ready", "th_ready", "a_ready",
                             "a2_ready", "w_ready", "ml_done", "m_ready"))
        ix_ready, b_ready, h_step, ha_ready, ha_stored = (
            sem(n) for n in ("ix_ready", "b_ready", "h_step", "ha_ready", "ha_stored"))
        tanh_done = sem("tanh_done")
        silu_done, og_done, obh_done, obl_done = sem("silu_done"), sem("og_done"), sem("obh_done"), sem("obl_done")
        hl_loaded, o_used = sems("hl_loaded", KB), sem("o_used")
        hah_done, hal_done, ma_done = sem("hah_done"), sem("hal_done"), sem("ma_done")
        mgh_done, mgl_done = sem("mgh_done"), sem("mgl_done")
        xr_loaded = sems("xr_loaded", KB)
        sq2_done, sum2_done, sum2_mm, lnr2_done, r2_done, xh2_done, xl2_done = (
            sem(n) for n in ("sq2_done", "sum2_done", "sum2_mm", "lnr2_done", "r2_done", "xh2_done", "xl2_done"))
        fst_loaded, set_f = sem("fst_loaded"), sem("set_f")
        gbias_ready, gconv_step, vbias_ready, vconv_step, gkept, vkept = (
            sem(n) for n in ("gbias_ready", "gconv_step", "vbias_ready", "vconv_step", "gkept", "vkept"))
        ggelu_done, act_done, acth_done, actl_done = (
            sem(n) for n in ("ggelu_done", "act_done", "acth_done", "actl_done"))
        sq3_done, sum3_done, lnr3_done, r3_done, y_done = (sem(n) for n in ("sq3_done", "sum3_done", "lnr3_done", "r3_done", "y_done"))
        stored = sem("stored")
        y_stored = sem("y_stored")

        block = ctx.enter_context(nc.Block())

        @block.sync
        def _(sp):
            sp.dma_start(prm, I["params"]).then_inc(prm_loaded, 16)
            sp.dma_start(raw[0], I["w"][0]).then_inc(w_loaded[0], 16)
            sp.dma_start(blk(X1, 1), I["x"][1]).then_inc(x_loaded[1], 16)
            sp.dma_start(raw[1], I["w"][1]).then_inc(w_loaded[1], 16)
            for k in range(3, KB, 2):
                sp.dma_start(blk(X1, k), I["x"][k]).then_inc(x_loaded[k], 16)
            for t, name in ((rgst, "rg_states"), (h0, "h0"), (gbz, "gla_bias")):
                sp.dma_start(t, I[name]).then_inc(par_loaded, 16)
            sp.dma_start(wg[0:RANK, :], I["gla_w_gate"]).then_inc(const_loaded, 16)
            for t, name in ((reset, "reset"), (rs16, "reset16"), (ident, "ident"), (mask, "mask")):
                sp.dma_start(t, I[name]).then_inc(const_loaded, 16)
            sp.dma_start(gw, I["rg_gates"][0]).then_inc(gwt_loaded, 16)
            sp.dma_start(O["rg_old"], I["rg_old"]).then_inc(stored, 16)
            sp.dma_start(O["ffn_old"], I["ffn_old"]).then_inc(stored, 16)
            sp.dma_start(sS, I["gla_state"][0]).then_inc(sS_loaded, 16)
            with sp.Fori(1, N_UNITS // 2) as i:
                for s in range(2):
                    sp.wait_ge(w_split[s], i)
                    sp.dma_start(raw[s], I["w"][2 * i + s]).then_inc(w_loaded[s], 16)
            sp.wait_ge(w_split[0], N_UNITS // 2)
            sp.dma_start(raw[0], I["w"][N_UNITS - 1]).then_inc(w_loaded[0], 16)
            sp.wait_ge(rgo_kept, KB)
            sp.wait_ge(h_step, 4 * KB)
            sp.dma_start(O["rg_last"], rgo).then_inc(stored, 16)
            sp.dma_start(O["h_last"], hco).then_inc(stored, 16)
            sp.wait_ge(gkept, FB)
            sp.wait_ge(vkept, FB)
            sp.dma_start(O["u_last"], ubuf).then_inc(stored, 16)
            for k in range(KB):
                sp.wait_ge(y_done, k + 1)
                sp.dma_start(O["y"][k], blk(X2, k)).then_inc(y_stored, 16)
            sp.wait_ge(y_stored, 16 * KB)
            sp.wait_ge(stored, 16 * 6)
            sp.wait_ge(sS_stored, 16 * NB)

        @block.gpsimd
        def _(pool):
            def split(i, s):
                pool.wait_ge(w_loaded[s], 16 * i + 16)
                if not isinstance(i, int) or i > 0:
                    pool.wait_ge(unit_done[s], i)
                nc.gpsimd.tensor_tensor(whi[s], raw[s], one, ALU.mult).then_inc(w_hi_done[s], 1)
                pool.wait_ge(w_hi_done[s], i + 1)
                nc.gpsimd.tensor_tensor(wlo[s], raw[s], whi[s].bitcast(F32), ALU.subtract).then_inc(w_split[s], 1)

            pool.wait_ge(ones_done, 1)
            one = ones[:, 0:1].broadcast_to([P, D])
            split(0, 0)
            split(0, 1)
            with pool.Fori(1, N_UNITS // 2) as i:
                split(i, 0)
                split(i, 1)
            split(N_UNITS // 2, 0)

        @block.tensor
        def _(pe):
            def tile_products(s, t, g, xh, xl, first, last):
                for w, x, a, z in ((whi, xh, first, False), (whi, xl, False, False), (wlo, xh, False, last)):
                    for n in range(3):
                        mm = nc.tensor.matmul(accv[g][:, n], w[s][:, t * P:(t + 1) * P], x[:, n * NW:(n + 1) * NW],
                                              start=a, stop=z)
                return mm

            def unit(u, n_slot, g, n_grp, xh, xl, pieces=(), gate=None, used=None):
                s = slot_of(u)
                pe.wait_ge(w_split[s], n_slot + 1)
                pe.wait_ge(acc_free[g], n_grp)
                for k in range(KB):
                    if gate:
                        gate(k)
                    mm = tile_products(s, k, g, xh[:, k * C:(k + 1) * C], xl[:, k * C:(k + 1) * C], k == 0, k == KB - 1)
                    if k == KB - 1:
                        mm.then_inc(unit_done[s], 1)
                    elif used:
                        mm.then_inc(used, 1)
                    for f in dict(pieces).get(k, ()):
                        f()

            def sum_features(src, g):
                for n in range(3):
                    mm = nc.tensor.matmul(accv[g][:, n], ones, src[:, n * NW:(n + 1) * NW], start=True, stop=True)
                mm.then_inc(sum_mm, 1)

            def norm_sum(src, n, bank, mm_sem):
                nc.tensor.matmul(bank[:, 0:NW], ones, src[:, n * NW:(n + 1) * NW], start=True, stop=True).then_inc(mm_sem, 1)

            order = [(0, 0), (0, 1), (0, 2)]
            for k in range(3, KB):
                order += [(1, k - 3), (0, k)]
            order += [(1, k) for k in range(KB - 3, KB)]
            for g, k in order:
                s = slot_of(g)
                if k == 0:
                    pe.wait_ge(w_split[s], 1)
                if g == 0:
                    pe.wait_ge(xh1_done, k + 1)
                    pe.wait_ge(xl1_done, k + 1)
                mm = tile_products(s, k, g, XH[:, k * C:(k + 1) * C], XL[:, k * C:(k + 1) * C], k == 0, k == KB - 1)
                if k == KB - 1:
                    mm.then_inc(unit_done[s], 1)
                if (g, k) == (1, KB - 2):
                    pe.wait_ge(sum1_done, KB)
                    norm_sum(xc, 0, sb6, sum1_mm)
                    norm_sum(xc, 1, sb7, sum1_mm)
            pe.wait_ge(lnr1_done, 1)
            norm_sum(xc, 2, sb6, sum1_mm)
            with pe.Fori(0, 3) as i:
                unit(U_QKV + 1, nth(U_QKV + 1, 2, i), 0, G_QKV[0] + i, XH, XL)
                unit(U_QKV + 2, nth(U_QKV + 2, 2, i), 1, G_QKV[1] + 1 + i, XH, XL)
            unit(U_QKV + 7, nth(U_QKV + 7), 0, G_QKV[0] + 3, XH, XL)

            def zg_piece(n, w, c0):
                pe.wait_ge(olog_done, n)
                for h in range(H):
                    mm = nc.tensor.matmul(sb6[:, h * w:(h + 1) * w], wg[0:RANK, h * DK:(h + 1) * DK],
                                          glr[0:RANK, bass.ds(c0, w)], start=True, stop=True)
                mm.then_inc(zg_mm, 1)

            def vT_piece(n, w, half):
                if half == 0:
                    pe.wait_ge(vcp_ready, n + 1)
                    pe.wait_ge(S_ready, state_banks(n))
                pe.wait_ge(vT_ready, 2 * n + half)
                for e in range(4):
                    k = 4 * half + e
                    mm = nc.tensor.transpose(sb7[0:w, e * P:(e + 1) * P], kk[:, k * w:(k + 1) * w], ident)
                mm.then_inc(vT_mm, 1)

            def keT_piece(n, w, bank7_free=None, count=0):
                pe.wait_ge(ke_ready, n + 1)
                if bank7_free:
                    pe.wait_ge(bank7_free, count)
                for h in range(H):
                    mm = nc.tensor.transpose(sb7[0:w, h * DK:(h + 1) * DK], ke[:, h * w:(h + 1) * w], ident)
                mm.then_inc(keT_mm, 1)

            def A_piece(n, w, bank6_free, count):
                pe.wait_ge(qd_ready, n + 1)
                pe.wait_ge(kd_ready, n + 1)
                pe.wait_ge(bank6_free, count)
                for h in range(H):
                    mm = nc.tensor.matmul(sb6[0:w, h * w:(h + 1) * w], kd[:, h * w:(h + 1) * w],
                                          qd[:, h * w:(h + 1) * w], start=True, stop=True)
                mm.then_inc(A_mm, 1)

            def O_piece(bank, w, cl, hh, inter):
                for q in range(4):
                    h, e = 2 * hh + q // 2, q % 2
                    mm = nc.tensor.matmul(bank[:, q * w:(q + 1) * w], vtm[0:w, h * DV + e * P:h * DV + (e + 1) * P],
                                          am[0:w, h * w:(h + 1) * w], start=True, stop=not inter)
                    for ck in range(w // cl if inter else 0):
                        s0 = ck * H * DV + h * DV + e * P
                        mm = nc.tensor.matmul(bank[:, q * w + ck * cl:q * w + (ck + 1) * cl], S[:, s0:s0 + P],
                                              qd[:, h * w + ck * cl:h * w + (ck + 1) * cl], start=False,
                                              stop=ck == w // cl - 1)
                mm.then_inc(O_mm, 1)

            def dS_piece(bank, cl, ck, hh):
                r = slice(ck * cl, (ck + 1) * cl)
                for h in (2 * hh, 2 * hh + 1):
                    mm = nc.tensor.matmul(bank[:, (h % 2) * DV:(h % 2 + 1) * DV], bc[r, h * DK:(h + 1) * DK],
                                          vtm[r, h * DV:(h + 1) * DV], start=True, stop=True)
                mm.then_inc(dS_mm, 1)

            def onorm_piece(n, w):
                pe.wait_ge(o_summed, n + 1)
                nc.tensor.matmul(hd(sb6, H, w), ones, squares(w)[:, :, 0], start=True, stop=True).then_inc(onorm_mm, 1)

            def zg_head():
                pe.wait_ge(lnr1_done, 3)
                pe.wait_ge(const_loaded, 16 * 5)
                pe.wait_ge(acc_free[0], 1)
                zg_piece(0, NMETA, 0)

            def zg_samples():
                pe.wait_ge(z_ready, 1)
                for h in range(H):
                    mm = nc.tensor.matmul(sb6[:, h * NS:(h + 1) * NS], wg[0:RANK, h * DK:(h + 1) * DK],
                                          glr[0:RANK, NT:C], start=True, stop=True)
                mm.then_inc(zg_mm, 1)

            def vT_samples(half):
                for e in range(4):
                    k = 4 * half + e
                    mm = nc.tensor.transpose(sb6[0:NS, e * P:(e + 1) * P], V[:, k * C + NT:k * C + NT + NS], ident)
                mm.then_inc(sT_mm, 1)

            unit(U_QKV + 8, nth(U_QKV + 8), 1, G_QKV[1] + 4, XH, XL, {1: [zg_head], 3: [zg_samples]})
            unit(U_QKV + 9, nth(U_QKV + 9), 0, G_QKV[0] + 4, XH, XL, {
                1: [lambda: keT_piece(0, NMETA)], 3: [lambda: A_piece(0, NMETA, z_ready, 2)]})
            with pe.Fori(5, 8) as i:
                unit(U_QKV, nth(U_QKV, 2, i), 1, G_QKV[1] + i, XH, XL)
                unit(U_QKV + 1, nth(U_QKV + 1, 2, i), 0, G_QKV[0] + i, XH, XL)
            pe.wait_ge(keT_ready, 1)
            vT_piece(0, NMETA, 0)
            pe.wait_ge(A_ready, 1)
            vT_samples(0)
            vT_piece(0, NMETA, 1)
            pe.wait_ge(sT_ready, 1)
            vT_samples(1)
            pe.wait_ge(vT_ready, 2)
            O_piece(sb7, NMETA, NMETA, 0, False)
            pe.wait_ge(sT_ready, 2)
            O_piece(sb6, NMETA, NMETA, 1, False)
            for hh, bank in ((0, sb7), (1, sb6)):
                pe.wait_ge(o_copied, hh + 1)
                dS_piece(bank, NMETA, 0, hh)
            pe.wait_ge(S_ready, 2)
            onorm_piece(0, NMETA)

            def smp_o(j):
                pe.wait_ge(sS_ready, j + 1)
                pe.wait_ge(vT_ready, 2 * (j + 1) + 2)
                for h in range(H):
                    for e in range(2):
                        mm = nc.tensor.matmul(sb7[:, 2 * h + e:2 * h + e + 1], sS[:, h * DV + e * P:h * DV + (e + 1) * P],
                                              sqk[:, bass.ds(h * NS + j, 1)], start=True, stop=True)
                mm.then_inc(so_mm, 1)

            def gate_product(g, n_grp, half):
                pe.wait_ge(acc_free[g], n_grp)
                for n in range(3):
                    mm = nc.tensor.matmul(accv[g][:, n], gw[:, half * P:(half + 1) * P], xc[:, n * NW:(n + 1) * NW],
                                          start=True, stop=True)
                mm.then_inc(gate_mm, 1)

            with pe.Fori(0, NPAIR) as j:
                n = j + 1
                zn = j + 2

                def zg_pair():
                    pe.wait_ge(ones_done, 1)
                    pe.wait_ge(olog_done, n)
                    for h in range(H):
                        mm = nc.tensor.matmul(sb6[:, h * PAIR:(h + 1) * PAIR], wg[0:RANK, h * DK:(h + 1) * DK],
                                              glr[0:RANK, bass.ds(NMETA + PAIR * j, PAIR)], start=True, stop=True)
                    mm.then_inc(zg_mm, 1)

                def dS0_01():
                    pe.wait_ge(keT_ready, n + 1)
                    pe.wait_ge(A_ready, n + 1)
                    dS_piece(sb6, CH, 0, 0)

                def dS0_23():
                    dS_piece(sb7, CH, 0, 1)

                def O_pair(hh, bank):
                    pe.wait_ge(S_ready, state_banks(n) + hh + 1)
                    O_piece(bank, PAIR, CH, hh, True)

                def dS1(hh, bank):
                    pe.wait_ge(o_copied, 2 * n + hh + 1)
                    dS_piece(bank, CH, 1, hh)

                unit(U_RG, nth(U_RG, 2, j), 1, G_RG[1] + 2 * j, XH, XL, {
                    0: [lambda: vT_piece(n, PAIR, 0)], 2: [zg_pair], 3: [lambda: vT_piece(n, PAIR, 1)],
                    6: [lambda: smp_o(j)]})
                unit(U_RG + 1, nth(U_RG + 1, 2, j), 0, G_RG[0] + 2 * j, XH, XL, {
                    1: [lambda: keT_piece(n, PAIR, so_ready, j + 1), lambda: A_piece(n, PAIR, z_ready, zn + 1)],
                    3: [dS0_01, dS0_23], 5: [lambda: O_pair(0, sb6)], 6: [lambda: O_pair(1, sb7)],
                    7: [lambda: dS1(0, sb6)]})
                pe.wait_ge(xc_step, 4 * j + 4)
                pe.wait_ge(gwt_loaded, 16 * j + 16)
                gate_product(1, G_RG[1] + 2 * j + 1, 0)
                dS1(1, sb7)
                pe.wait_ge(S_ready, state_banks(n) + 3)
                onorm_piece(n, PAIR)
                gate_product(0, G_RG[0] + 2 * j + 1, 1)

            def onorm_samples():
                pe.wait_ge(olog_done, NPAIR + 1)
                onorm_piece(NPAIR + 1, NS)

            unit(U_GO, nth(U_GO), 1, G_GO[1], XH, XL, {5: [onorm_samples]})
            unit(U_GO + 1, nth(U_GO + 1), 0, G_GO[0], XH, XL)
            with pe.Fori(1, KB // 2) as i:
                unit(U_GO, nth(U_GO, 2, i), 1, G_GO[1] + i, XH, XL)
                unit(U_GO + 1, nth(U_GO + 1, 2, i), 0, G_GO[0] + i, XH, XL)
            with pe.Fori(0, KB - 1) as j:
                unit(U_B, nth(U_B, 2, j), 1, G_B[1] + j, XH, XL)
                pe.wait_ge(obh_done, KB)
                pe.wait_ge(obl_done, KB)
                unit(U_B + 1, nth(U_B + 1, 2, j), 0, G_B[0] + j, OBH, OBL)
            j = KB - 1
            unit(U_B, nth(U_B, 2, j), 1, G_B[1] + j, XH, XL)
            unit(U_B + 1, nth(U_B + 1, 2, j), 0, G_B[0] + j, OBH, OBL, used=o_used)

            def h_gate(k):
                pe.wait_ge(hah_done, k + 1)
                pe.wait_ge(hal_done, k + 1)
            unit(U_A, nth(U_A), 1, G_A[1], XH, XL)
            unit(U_A + 1, nth(U_A + 1), 0, G_A[0], HAH, HAL, gate=h_gate)
            with pe.Fori(1, KB) as j:
                unit(U_A, nth(U_A, 2, j), 1, G_A[1] + j, XH, XL)
                unit(U_A + 1, nth(U_A + 1, 2, j), 0, G_A[0] + j, HAH, HAL)

            def mg_gate(k):
                pe.wait_ge(mgh_done, k + 1)
                pe.wait_ge(mgl_done, k + 1)
            unit(U_OUT, nth(U_OUT), 1, G_OUT[1], MGH, MGL, gate=mg_gate)
            unit(U_OUT + 1, nth(U_OUT + 1), 0, G_OUT[0], MGH, MGL)
            with pe.Fori(1, KB // 2) as i:
                unit(U_OUT, nth(U_OUT, 2, i), 1, G_OUT[1] + i, MGH, MGL)
                unit(U_OUT + 1, nth(U_OUT + 1, 2, i), 0, G_OUT[0] + i, MGH, MGL)
            def up(u0, per, i, grp0, gper, f0=0):
                for f in range(f0, GRP):
                    for c in range(2):
                        u = u0 + 2 * f + c
                        unit(u, nth(u, per, i), c, G_FFN[c] + grp0 + f + gper * i, X2H, X2L)

            def down(u0, per, i, grp0, gper, half, n_act):
                pe.wait_ge(acth_done, n_act)
                pe.wait_ge(actl_done, n_act)
                for m in range(KB):
                    g = m % 2
                    pe.wait_ge(acc_free[g], G_FFN[g] + grp0 + m // 2 + gper * i)
                    for k in range(GRP):
                        t = m * GRP + k
                        u = u0 + t // KB
                        s = slot_of(u)
                        if t % KB == 0:
                            pe.wait_ge(w_split[s], nth(u, per, i) + 1)
                        b = (half * GRP + k) * C
                        mm = tile_products(s, t % KB, g, AH[:, b:b + C], AL[:, b:b + C], k == 0, k == GRP - 1)
                        if t % KB == KB - 1:
                            mm.then_inc(unit_done[s], 1)
                    if m < KB - 1:
                        mm.then_inc(down_mm, 1)

            def xn2_gate(k):
                pe.wait_ge(xh2_done, k + 1)
                pe.wait_ge(xl2_done, k + 1)
            NU, ND = 2 * GRP, GRP
            GU, GD = GRP, KB // 2

            def sums2():
                pe.wait_ge(sum2_done, KB)
                norm_sum(sqsum, 0, sb6, sum2_mm)
                norm_sum(sqsum, 1, sb7, sum2_mm)

            def last_sum2():
                pe.wait_ge(lnr2_done, 1)
                norm_sum(sqsum, 2, sb6, sum2_mm)
            unit(U_FFN, nth(U_FFN), 0, G_FFN[0], X2H, X2L, {6: [sums2]}, gate=xn2_gate)
            unit(U_FFN + 1, nth(U_FFN + 1), 1, G_FFN[1], X2H, X2L, {0: [last_sum2]})
            up(U_FFN, 0, 0, 0, 0, f0=1)
            per, gper = 2 * (NU + ND), 2 * (GU + GD)
            with pe.Fori(0, NGRP // 2 - 1) as i:
                up(U_FFN + NU, per, i, GU, gper)
                down(U_FFN + 2 * NU, per, i, 2 * GU, gper, 0, 2 * GRP * i + GRP)
                up(U_FFN + 2 * NU + ND, per, i, 2 * GU + GD, gper)
                down(U_FFN + 3 * NU + ND, per, i, 3 * GU + GD, gper, 1, 2 * GRP * i + 2 * GRP)
            n, gn = NGRP // 2 - 1, NGRP // 2 - 1
            u, g = U_FFN + NU + n * per, GU + gn * gper
            up(u, 0, 0, g, 0)
            down(u + NU, 0, 0, g + GU, 0, 0, GRP * (NGRP - 1))
            down(u + NU + ND, 0, 0, g + GU + GD, 0, 1, GRP * NGRP)
            pe.wait_ge(sum3_done, KB)
            pe.wait_ge(acc_free[0], G_FINAL)
            sum_features(ysum, 0)

        @block.scalar
        def _(act):
            def ready(u, per=0, i=0):
                act.wait_ge(unit_done[slot_of(u)], nth(u, per, i) + 1)

            def plain():
                act.wait_ge(ones_done, 1)

            for k in range(0, KB, 2):
                act.dma_start(blk(X1, k), I["x"][k]).then_inc(x_loaded[k], 16)

            def norm_factor(mm_sem, ln_sem, r_sem):
                for n, bank in enumerate((sb6, sb7, sb6)):
                    act.wait_ge(mm_sem, n + 1)
                    nc.scalar.activation(rms[:, n * NW:(n + 1) * NW], bank[:, 0:NW], ACT.Ln, scale=1.0 / D, bias=cst[:, 0:1])\
                        .then_inc(ln_sem, 1)
                act.wait_ge(ln_sem, 3)
                nc.scalar.activation(rms, rms, ACT.Exp, scale=-0.5).then_inc(r_sem, 1)

            act.preload_act_table_set(LN_EXP)
            act.wait_ge(prm_loaded, 16)
            for k in range(KB):
                act.wait_ge(x_loaded[k], 16)
                nc.scalar.activation(blk(XH, k), blk(X1, k), ACT.Identity, scale=par("g1", k)).then_inc(xh1_done, 1)
                if k >= 2:
                    act.wait_ge(sum1_done, k - 1)
                nc.scalar.activation((rt, it)[k % 2], blk(X1, k), ACT.Square).then_inc(sq1_done, 1)
            act.wait_ge(ones_done, 1)
            norm_factor(sum1_mm, lnr1_done, r1_done)

            lam = prm[:, RP["lam"]:RP["lam"] + KB]
            nc.scalar.activation(der[:, 0:KB], lam, ACT.Abs).then_inc(set_a, 1)
            act.wait_ge(set_a, 1)
            nc.scalar.activation(der[:, 0:KB], der[:, 0:KB], ACT.Exp, scale=-1.0).then_inc(set_a, 1)
            act.wait_ge(set_a, 2)
            nc.scalar.activation(der[:, 0:KB], der[:, 0:KB], ACT.Ln, bias=1.0).then_inc(set_a, 1)

            with act.Fori(0, 4) as i:
                for s, g in ((0, 1), (1, 0)):
                    act.wait_ge(acc_free[g], G_QKV[g] + i + 1)
                    act.dma_start(qk_scr[2 * i + s], (rt, it)[s]).then_inc(qk_stored[s], 16)

            def load_qk(w, c0):
                act.dma_start(hd(qkp, 8, w), qk_scr[:, :, bass.ds(c0, w)].rearrange("k p c -> p k c")).then_inc(qk_loaded, 16)

            def v_copy(n, w, c0, n_k):
                plain()
                act.wait_ge(vT_mm, 2 * n)
                act.wait_ge(A_mm, n_k)
                act.wait_ge(keT_mm, n_k)
                nc.scalar.activation(hd(kk, 8, w), V3[:, :, bass.ds(c0, w)], ACT.Copy).then_inc(vcp_ready, 1)

            def log_gate(nz, z, g, between=None):
                act.wait_ge(z_ready, nz + 1)
                nc.scalar.activation(g, z, ACT.Abs).then_inc(absz_done, 1)
                act.wait_ge(absz_done, nz + 1)
                nc.scalar.activation(g, g, ACT.Exp, scale=-1.0).then_inc(expz_done, 1)
                if between:
                    between()
                act.wait_ge(expz_done, nz + 1)
                nc.scalar.activation(g, g, ACT.Ln, bias=1.0).then_inc(lnz_done, 1)

            def v_tokens(n, w, half):
                act.wait_ge(vT_mm, 2 * n + half + 1)
                act.wait_ge(dS_mm, state_banks(n))
                nc.scalar.activation(vtm[0:w, half * 512:(half + 1) * 512], sb7[0:w, :], ACT.Copy).then_inc(vT_ready, 1)

            def decays(n, w):
                act.wait_ge(bc_ready, n + 1)
                nc.scalar.activation(eb[:, 0:4 * w], bc[:, 0:4 * w], ACT.Exp, scale=1.0 / 16).then_inc(eb_ready, 1)
                act.wait_ge(bl_ready, n + 1)
                nc.scalar.activation(g_t[:, 0:4 * w], bc[:, 0:4 * w], ACT.Exp, scale=-1.0 / 16).then_inc(enb_ready, 1)
                nc.scalar.activation(z_t[:, 0:4 * w], z_t[:, 0:4 * w], ACT.Exp, scale=1.0 / 16).then_inc(eke_ready, 1)

            def ke_tokens(n, w):
                act.wait_ge(keT_mm, n + 1)
                nc.scalar.activation(bc[0:w, :], sb7[0:w, :], ACT.Copy).then_inc(keT_ready, 1)

            def o_square(n, w, c0, hh):
                plain()
                act.wait_ge(o_copied, 2 * n + hh + 1)
                nc.scalar.activation(zg[:, 4 * w * hh:4 * w * (hh + 1)].rearrange("p (k t) -> p k t", k=4),
                                     V3[:, 4 * hh:4 * hh + 4, bass.ds(c0, w)], ACT.Square).then_inc(o_squared, 1)

            def o_rms(nn, out, w):
                act.wait_ge(onorm_mm, nn + 1)
                nc.scalar.activation(out, sb6[:, 0:4 * w], ACT.Ln, scale=1.0 / DV, bias=cst[:, 0:1]).then_inc(olog_done, 1)
                act.wait_ge(olog_done, nn + 1)
                nc.scalar.activation(out, out, ACT.Exp, scale=-0.5).then_inc(orinv_ready, 1)

            for s in range(2):
                act.wait_ge(qk_stored[s], 64)
            act.wait_ge(set_v, 12)
            load_qk(NMETA, 0)
            act.dma_start(hd(sqk, 8, NS), qk_scr[:, :, NT:C].rearrange("k p c -> p k c")).then_inc(sqk_loaded, 16)
            act.preload_act_table_set(LN_EXP)
            log_gate(0, z_t[:, 0:4 * NMETA], g_t[:, 0:4 * NMETA])
            decays(0, NMETA)
            log_gate(1, sdec, srv)
            act.wait_ge(sg_ready, 1)
            nc.scalar.activation(sdec, sdec, ACT.Exp, scale=1.0 / 16).then_inc(s_act, 1)

            def sample_tokens(q, t, bank):
                act.wait_ge(sT_mm, q + 1)
                nc.scalar.activation(t, bank[0:NS, :], ACT.Copy).then_inc(sT_ready, 1)

            ke_tokens(0, NMETA)
            for used in (qd_ready, kd_ready, ke_ready):
                act.wait_ge(used, 1)
            load_qk(PAIR, NMETA)
            act.wait_ge(acc_free[0], G_RG[0])
            act.wait_ge(acc_free[1], G_RG[1])
            v_copy(0, NMETA, 0, 1)
            v_tokens(0, NMETA, 0)
            sample_tokens(0, svt[0:NS, 0:512], sb6)
            v_tokens(0, NMETA, 1)
            sample_tokens(1, svt[0:NS, 512:1024], sb6)
            act.wait_ge(sT_ready, 2)
            act.dma_start(sv_scr, svt[0:NB, :]).then_inc(sv_stored, 16)
            v_copy(1, PAIR, NMETA, 1)
            o_square(0, NMETA, 0, 0)
            o_square(0, NMETA, 0, 1)
            o_rms(0, qd[:, 0:4 * NMETA], NMETA)
            v_tokens(1, PAIR, 0)

            def load_sample_v(j):
                act.dma_start(svb, sv_scr[bass.ds(j, 1)].broadcast_to([P, D])).then_inc(svb_loaded, 16)
            act.wait_ge(sv_stored, 16)
            load_sample_v(0)

            def rg_tail_exps(m):
                plain()
                act.wait_ge(h_step, 4 * m)
                nc.scalar.activation(av, rt, ACT.Exp, scale=col(der, m + 2 * KB), bias=col(der, m + 2 * KB)).then_inc(a_ready, 1)
                nc.scalar.activation(rt, rt, ACT.Exp, scale=col(der, m + 3 * KB), bias=col(der, m + 3 * KB)).then_inc(a2_ready, 1)

            def rg_tail_mult(m):
                act.wait_ge(w_ready, m + 1)
                nc.scalar.activation(th, th, ACT.Ln, bias=cst[:, 1:2]).then_inc(ml_done, 1)
                act.wait_ge(ml_done, m + 1)
                nc.scalar.activation(th, th, ACT.Exp, scale=0.5).then_inc(m_ready, 1)

            def rg_prefetch(j):
                for used in (qd_ready, kd_ready, ke_ready):
                    act.wait_ge(used, j + 2)
                load_qk(PAIR, NMETA + PAIR * (j + 1))
                load_sample_v(j + 1)
                act.wait_ge(sS_stored, 16 * j + 16)
                act.wait_ge(so_mm, j + 1)
                act.dma_start(sS, I["gla_state"][j + 1]).then_inc(sS_loaded, 16)

            def rg_body(j, first, last):
                n = j + 1
                if not first:
                    rg_tail_exps(j - 1)
                log_gate(j + 2, z_t, g_t, lambda: v_tokens(n, PAIR, 1))
                if not first:
                    rg_tail_mult(j - 1)
                decays(n, PAIR)
                if not first:
                    act.wait_ge(ha_ready, j)
                    act.dma_start(ha_scr[j - 1], gy).then_inc(ha_stored, 16)
                plain()
                act.wait_ge(acc_free[1], G_RG[1] + 2 * j + 1)
                act.wait_ge(ha_ready, j)
                nc.scalar.activation(xc, ext[:, 3:3 + C], ACT.Identity, scale=par("w3", j), bias=par("b", j))\
                    .then_inc(xbias_ready, 1)
                act.wait_ge(sS_ready, j + 1)
                act.dma_start(O["gla_sample"][j], sS).then_inc(sS_stored, 16)
                ke_tokens(n, PAIR)
                if not last:
                    v_copy(n + 1, PAIR, NMETA + PAIR * (j + 1), n + 1)
                    rg_prefetch(j)
                o_square(n, PAIR, NMETA + PAIR * j, 0)
                o_square(n, PAIR, NMETA + PAIR * j, 1)
                act.wait_ge(acc_free[0], G_RG[0] + 2 * j + 1)
                nc.scalar.activation(gy, gy, ACT.Gelu_apprx_tanh).then_inc(gelu_ready, 1)
                plain()
                act.wait_ge(gate_mm, 2 * j + 1)
                nc.scalar.activation(view3(rt), accv[1], ACT.Tanh, scale=0.5, bias=col(der, j)).then_inc(acc_free[1], 1)
                plain()
                act.wait_ge(acc_free[1], G_RG[1] + 2 * j + 2)
                act.wait_ge(b_ready, j)
                nc.scalar.activation(th, rt, ACT.Tanh, scale=col(der, j + 4 * KB), bias=col(der, j + 4 * KB)).then_inc(th_ready, 1)
                plain()
                act.wait_ge(gate_mm, 2 * j + 2)
                act.wait_ge(h_step, 4 * j)
                nc.scalar.activation(view3(it), accv[0], ACT.Tanh, scale=0.5, bias=col(der, j + KB)).then_inc(acc_free[0], 1)
                act.preload_act_table_set(LN_EXP)
                if not last:
                    v_tokens(n + 1, PAIR, 0)
                o_rms(n, qd, PAIR)

            def gate_weights(j):
                act.dma_start(gw, I["rg_gates"][j + 1]).then_inc(gwt_loaded, 16)

            rg_body(0, True, False)
            gate_weights(0)
            with act.Fori(1, NPAIR - 1) as j:
                rg_body(j, False, False)
                gate_weights(j)
            rg_body(NPAIR - 1, False, True)
            act.wait_ge(so_ready, NB)
            act.wait_ge(onorm_mm, NPAIR + 1)
            nc.scalar.activation(hd(zg, 8, NS), V3[:, :, NT:C], ACT.Square).then_inc(s_act, 2)
            rg_tail_exps(NPAIR - 1)
            o_rms(NPAIR + 1, srv, NS)
            rg_tail_mult(NPAIR - 1)
            act.wait_ge(ha_ready, NPAIR)
            act.dma_start(ha_scr[NPAIR - 1], gy).then_inc(ha_stored, 16)
            act.dma_start(O["gla_prompt"], S[:, 0:H * DV]).then_inc(stored, 16)
            act.wait_ge(h_step, 4 * NPAIR)
            act.wait_ge(sS_stored, 16 * NB)
            act.wait_ge(o_ready, NPAIR + 2)

            def gate_o(i):
                for s, g in ((0, 1), (1, 0)):
                    act.wait_ge(acc_free[g], G_GO[g] + i + 1)
                    nc.scalar.activation(T[s], T[s], ACT.Silu).then_inc(silu_done, 1)
                    plain()
                    act.wait_ge(og_done, 2 * i + s + 1)
                    nc.scalar.activation(blk(OBH, 2 * i + s), T[s], ACT.Copy).then_inc(obh_done, 1)
            gate_o(0)
            act.wait_ge(ha_stored, 16 * NPAIR)
            act.wait_ge(stored, 48)
            with act.Fori(1, KB // 2) as i:
                gate_o(i)
            with act.Fori(0, KB) as j:
                act.wait_ge(acc_free[1], G_B[1] + j + 1)
                nc.scalar.activation(T[2], T[2], ACT.Tanh, scale=0.5).then_inc(tanh_done, 1)
            for k in range(KB):
                if k < KB - 1:
                    act.wait_ge(o_used, k + 1)
                else:
                    ready(U_A - 1)
                act.dma_start(blk(HA, k), ha_scr[k]).then_inc(hl_loaded[k], 16)
            for k in range(KB):
                act.wait_ge(hl_loaded[k], 16)
                nc.scalar.activation(blk(HAH, k), blk(HA, k), ACT.Copy).then_inc(hah_done, 1)
            with act.Fori(0, KB) as j:
                act.wait_ge(acc_free[1], G_A[1] + j + 1)
                nc.scalar.activation(T[2], T[2], ACT.Tanh, scale=0.5).then_inc(tanh_done, 1)
            act.wait_ge(acc_free[1], G_OUT[1])
            for k in range(KB):
                if k == KB - 1:
                    ready(U_OUT - 1)
                    for m in range(KB):
                        act.dma_start(blk(X2, m), I["x"][m]).then_inc(xr_loaded[m], 16)
                act.wait_ge(ma_done, KB if k == KB - 1 else k + 1)
                nc.scalar.activation(blk(MGH, k), blk(MG, k), ACT.Copy, scale=0.5).then_inc(mgh_done, 1)
            for k in range(KB):
                act.wait_ge(acc_free[1 - k % 2], G_OUT[1 - k % 2] + k // 2 + 1)
                nc.scalar.activation(blk(X2H, k), blk(X2, k), ACT.Identity, scale=par("g2", k)).then_inc(xh2_done, 1)
                if k >= 2:
                    act.wait_ge(sum2_done, k - 1)
                nc.scalar.activation(T[k % 2], blk(X2, k), ACT.Square).then_inc(sq2_done, 1)
            act.dma_start(fst, I["ffn_states"]).then_inc(fst_loaded, 16)
            act.dma_start(fpr, I["ffn_params"]).then_inc(fst_loaded, 16)
            act.preload_act_table_set(LN_EXP)
            norm_factor(sum2_mm, lnr2_done, r2_done)

            def ffn_block(F, grp):
                plain()
                act.wait_ge(acc_free[0], G_FFN[0] + grp + 1)
                act.wait_ge(act_done, F)
                nc.scalar.activation(cg, eg[:, 2:2 + C], ACT.Identity, scale=fpr[:, bass.ds(2 * UB + F, 1)],
                                     bias=fpr[:, bass.ds(3 * UB + F, 1)]).then_inc(gbias_ready, 1)
                act.wait_ge(gconv_step, 3 * F + 3)
                nc.scalar.activation(cg, cg, ACT.Gelu_apprx_tanh).then_inc(ggelu_done, 1)
                plain()
                act.wait_ge(acc_free[1], G_FFN[1] + grp + 1)
                nc.scalar.activation(cv, ev[:, 2:2 + C], ACT.Identity, scale=fpr[:, bass.ds(2 * UB + FB + F, 1)],
                                     bias=fpr[:, bass.ds(3 * UB + FB + F, 1)]).then_inc(vbias_ready, 1)
                act.wait_ge(act_done, F + 1)

            def ffn_hi(half, f):
                b = (half * GRP + f) * C
                nc.scalar.activation(AH[:, b:b + C], act_t, ACT.Copy).then_inc(acth_done, 1)

            GU, GD = GRP, KB // 2

            def ffn_group(F0_, grp, half):
                for f in range(GRP):
                    ffn_block(F0_ + f, grp + f)
                    ffn_hi(half, f)

            act.wait_ge(set_f, 4)
            ffn_group(0, 0, 0)
            gper = 2 * (GU + GD)
            with act.Fori(0, NGRP // 2 - 1) as i:
                ffn_group(2 * GRP * i + GRP, GU + gper * i, 1)
                act.wait_ge(acc_free[1], G_FFN[1] + 2 * GU + GD + gper * i)
                ffn_group(2 * GRP * i + 2 * GRP, 2 * GU + GD + gper * i, 0)
                act.wait_ge(acc_free[1], G_FFN[1] + 3 * GU + 2 * GD + gper * i)
            n = NGRP // 2 - 1
            ffn_group(GRP * (NGRP - 1), GU + gper * n, 1)
            y_use = 2 * GU + GD + gper * n
            for k in range(KB):
                act.wait_ge(acc_free[k % 2], G_FFN[k % 2] + y_use + k // 2 + 1)
                act.wait_ge(sum3_done, k)
                nc.scalar.activation(ysq, blk(X2, k), ACT.Square).then_inc(sq3_done, 1)
            act.preload_act_table_set(LN_EXP)
            act.wait_ge(sum_mm, 1)
            nc.scalar.activation(view3(yrs), accv[0], ACT.Ln, scale=1.0 / D, bias=cst[:, 0:1]).then_inc(lnr3_done, 1)
            act.wait_ge(lnr3_done, 1)
            nc.scalar.activation(yrs, yrs, ACT.Exp, scale=-0.5).then_inc(r3_done, 1)

        @block.vector
        def _(dve):
            nc.vector.memset(ones, 1.0)
            nc.vector.memset(cst[:, 0:1], EPS)
            nc.vector.memset(ext[:, 0:3], 0.0)
            nc.vector.memset(am, 0.0)
            nc.vector.memset(cst[:, 1:2], TINY).then_inc(ones_done, 1)
            def plain():
                dve.wait_ge(ones_done, 1)

            dve.wait_ge(prm_loaded, 16)
            for k in range(KB):
                dve.wait_ge(xh1_done, k + 1)
                nc.vector.scalar_tensor_tensor(blk(XL, k), blk(X1, k), par("g1", k), blk(XH, k).bitcast(F32),
                                               ALU.mult, ALU.subtract).then_inc(xl1_done, 1)
                dve.wait_ge(sq1_done, k + 1)
                if k == 0:
                    nc.vector.tensor_copy(xc, rt).then_inc(sum1_done, 1)
                else:
                    dve.wait_ge(sum1_done, k)
                    nc.vector.tensor_tensor(xc, xc, (rt, it)[k % 2], ALU.add).then_inc(sum1_done, 1)

            def evacuate(u, per, i, g, out, n_part=P):
                dve.wait_ge(unit_done[slot_of(u)], nth(u, per, i) + 1)
                nc.vector.tensor_tensor(view3(out), acc[g][0:n_part, :, 0:NW], view3(rms[0:n_part, :]), ALU.mult)\
                    .then_inc(acc_free[g], 1)

            dve.wait_ge(r1_done, 1)
            evacuate(0, 0, 0, 0, glr[0:RANK, :], RANK)
            dve.wait_ge(sum1_done, KB)

            def stage_qk(i):
                for s, g in ((0, 1), (1, 0)):
                    if not isinstance(i, int):
                        dve.wait_ge(qk_stored[s], 16 * i)
                    evacuate(U_QKV + s, 2, i, g, (rt, it)[s])
            stage_qk(0)

            dve.wait_ge(par_loaded, 48)
            steps = [0]

            def step(ins):
                steps[0] += 1
                ins.then_inc(set_v, 1)
                dve.wait_ge(set_v, steps[0])

            st = rgst.rearrange("p (r k b) -> p r k b", r=3, k=KB)

            def wide(name):
                return prm[:, RP[name]:RP[name] + KB].unsqueeze(2).broadcast_to([P, KB, NS])
            pk, tk = hd(rgp, KB, NS), hd(rgtmp, KB, NS)
            step(nc.vector.tensor_tensor(pk, st[:, 0], wide("w0"), ALU.mult))
            for r in (1, 2):
                step(nc.vector.tensor_tensor(tk, st[:, r], wide(f"w{r}"), ALU.mult))
                step(nc.vector.tensor_tensor(pk, pk, tk, ALU.add))
            step(nc.vector.tensor_tensor(pk, pk, wide("b"), ALU.add))
            dve.wait_ge(set_a, 3)
            d = [der[:, i * KB:(i + 1) * KB] for i in range(5)]
            lam = prm[:, RP["lam"]:RP["lam"] + KB]
            step(nc.vector.tensor_scalar(d[1], lam, -1.0, 0.0, ALU.mult, ALU.max))
            step(nc.vector.tensor_tensor(d[4], d[0], d[1], ALU.add))
            step(nc.vector.tensor_scalar(d[2], d[4], -4.0, None, ALU.mult))
            step(nc.vector.tensor_scalar(d[3], d[4], -8.0, None, ALU.mult))
            step(nc.vector.tensor_scalar(d[4], d[4], 4.0, None, ALU.mult))
            step(nc.vector.tensor_scalar(d[0], prm[:, RP["ba"]:RP["ba"] + KB], 0.5, None, ALU.mult))
            step(nc.vector.tensor_scalar(d[1], prm[:, RP["bx"]:RP["bx"] + KB], 0.5, None, ALU.mult))

            with dve.Fori(1, 4) as i:
                stage_qk(i)

            def logits(nz, w, z):
                dve.wait_ge(zg_mm, nz + 1)
                nc.vector.tensor_tensor(hd(z, H, w), hd(sb6, H, w), gbz.unsqueeze(2).broadcast_to([P, H, w]), ALU.add)\
                    .then_inc(z_ready, 1)

            def log_sigmoid(nz, z, g, out):
                dve.wait_ge(lnz_done, nz + 1)
                return nc.vector.scalar_tensor_tensor(out, z, 0.0, g, ALU.min, ALU.subtract)

            def running_sum(n, w, cl, reset_t):
                log_sigmoid(n if isinstance(n, int) and n == 0 else n + 1, z_t[:, 0:4 * w], g_t[:, 0:4 * w],
                            g_t[:, 0:4 * w]).then_inc(g_ready, 1)
                dve.wait_ge(g_ready, n + 1)
                dve.wait_ge(dS_mm, state_banks(n))
                nc.vector.tensor_tensor_scan(bc[:, 0:4 * w], reset_t, g_t[:, 0:4 * w], 0.0, ALU.mult, ALU.add)\
                    .then_inc(bc_ready, 1)
                dve.wait_ge(bc_ready, n + 1)
                b = bc[:, 0:4 * w].rearrange("p (c t) -> p c t", t=cl)
                z = z_t[:, 0:4 * w].rearrange("p (c t) -> p c t", t=cl)
                nc.vector.tensor_tensor(z, b[:, :, cl - 1:cl].broadcast_to([P, 4 * w // cl, cl]), b, ALU.subtract)\
                    .then_inc(bl_ready, 1)

            def scaled_qk(n, w):
                dve.wait_ge(qk_loaded, 16 * n + 16)
                dve.wait_ge(eb_ready, n + 1)
                nc.vector.scalar_tensor_tensor(qd[:, 0:4 * w], qkp[:, 0:4 * w], DK ** -0.5, eb[:, 0:4 * w],
                                               ALU.mult, ALU.mult).then_inc(qd_ready, 1)
                if not isinstance(n, int):
                    dve.wait_ge(vT_mm, 2 * n + 2)
                dve.wait_ge(enb_ready, n + 1)
                nc.vector.tensor_tensor(kd[:, 0:4 * w], qkp[:, 4 * w:8 * w], g_t[:, 0:4 * w], ALU.mult).then_inc(kd_ready, 1)
                dve.wait_ge(eke_ready, n + 1)
                nc.vector.tensor_tensor(ke_w(w), qkp[:, 4 * w:8 * w], z_t[:, 0:4 * w], ALU.mult).then_inc(ke_ready, 1)

            def ke_w(w):
                return ke[:, 0:4 * w]

            def scores(n, w):
                dve.wait_ge(const_loaded, 16 * 5)
                dve.wait_ge(A_mm, n + 1)
                nc.vector.copy_predicated(hd(am[0:w], H, w), mask[0:w, 0:w].unsqueeze(1).broadcast_to([w, H, w]),
                                          hd(sb6[0:w], H, w)).then_inc(A_ready, 1)

            def o_copy(n, w, c0, hh, bank):
                plain()
                dve.wait_ge(O_mm, 2 * n + hh + 1)
                nc.vector.tensor_copy(V3[:, 4 * hh:4 * hh + 4, bass.ds(c0, w)], hd(bank, 4, w)).then_inc(o_copied, 1)

            def state(n_bank, w, cl, src, dst, ck, hh, bank):
                dve.wait_ge(dS_mm, n_bank + 1)
                for h in (2 * hh, 2 * hh + 1):
                    last = h * w + (ck + 1) * cl - 1
                    a, b = src * H * DV + h * DV, dst * H * DV + h * DV
                    ins = nc.vector.scalar_tensor_tensor(S[:, b:b + DV], S[:, a:a + DV], eb[:, last:last + 1],
                                                         bank[:, (h % 2) * DV:(h % 2 + 1) * DV], ALU.mult, ALU.add)
                ins.then_inc(S_ready, 1)

            def sum_halves(n, w):
                q = squares(w)
                nc.vector.tensor_tensor(q[:, :, 0], q[:, :, 0], q[:, :, 1], ALU.add).then_inc(o_summed, 1)

            def o_scale(n, w, c0, rinv):
                dve.wait_ge(orinv_ready, n + 1)
                dve.wait_ge(o_copied, 2 * n + 2)
                o = V3[:, :, bass.ds(c0, w)].rearrange("p (h e) t -> p h e t", h=H)
                r = hd(rinv, H, w).unsqueeze(2).broadcast_to([P, H, 2, w])
                nc.vector.tensor_tensor(o, o, r, ALU.mult).then_inc(o_ready, 1)

            dve.wait_ge(const_loaded, 16 * 5)
            logits(0, NMETA, z_t)
            running_sum(0, NMETA, NMETA, rs16)
            logits(1, NS, sdec)
            scaled_qk(0, NMETA)
            log_sigmoid(1, sdec, srv, sdec).then_inc(sg_ready, 1)
            dve.wait_ge(sqk_loaded, 16)
            nc.vector.tensor_scalar(sqk[:, 0:H * NS], sqk[:, 0:H * NS], DK ** -0.5, None, ALU.mult).then_inc(sg_ready, 1)
            dve.wait_ge(xl1_done, KB)
            evacuate(U_QKV + 8, 0, 0, 1, blk(V, 0))
            scores(0, NMETA)
            evacuate(U_QKV + 9, 0, 0, 0, blk(V, 1))
            with dve.Fori(1, 4) as i:
                evacuate(U_QKV + 8, 2, i, 1, blk(V, 2 * i))
                evacuate(U_QKV + 9, 2, i, 0, blk(V, 2 * i + 1))
            o_copy(0, NMETA, 0, 0, sb7)
            o_copy(0, NMETA, 0, 1, sb6)
            for hh, bank in ((0, sb7), (1, sb6)):
                dve.wait_ge(dS_mm, hh + 1)
                nc.vector.tensor_copy(S[:, hh * 2 * DV:(hh + 1) * 2 * DV], bank[:, :]).then_inc(S_ready, 1)
            dve.wait_ge(o_squared, 2)
            sum_halves(0, NMETA)
            o_scale(0, NMETA, 0, qd)
            def sample_state(j):
                dve.wait_ge(sS_loaded, 16 * j + 16)
                heads = [sS[:, h * DV:(h + 1) * DV] for h in range(H)]
                for h, t in enumerate(heads):
                    ins = nc.vector.tensor_scalar(t, t, sdec[:, bass.ds(h * NS + j, 1)], None, ALU.mult)
                ins.then_inc(sS_decayed, 1)
                dve.wait_ge(svb_loaded, 16 * j + 16)
                dve.wait_ge(sS_decayed, j + 1)
                for h, t in enumerate(heads):
                    ins = nc.vector.scalar_tensor_tensor(t, svb[:, h * DV:(h + 1) * DV], sqk[:, bass.ds((H + h) * NS + j, 1)], t,
                                                         ALU.mult, ALU.add)
                ins.then_inc(sS_ready, 1)

            def rg_tail_w(m):
                dve.wait_ge(acc_free[0], G_RG[0] + 2 * m + 2)
                nc.vector.scalar_tensor_tensor(it, it, 1.0, xc, ALU.add, ALU.mult).then_inc(ix_ready, 1)
                dve.wait_ge(a2_ready, m + 1)
                dve.wait_ge(th_ready, m + 1)
                nc.vector.scalar_tensor_tensor(th, rt, 1.0, th, ALU.add, ALU.mult).then_inc(w_ready, 1)

            def rg_tail_b(m):
                dve.wait_ge(m_ready, m + 1)
                dve.wait_ge(ix_ready, m + 1)
                nc.vector.scalar_tensor_tensor(it, it, 0.5, th, ALU.mult, ALU.mult).then_inc(b_ready, 1)

            def rg_tail_h(m):
                dve.wait_ge(a_ready, m + 1)
                dve.wait_ge(b_ready, m + 1)
                nc.vector.tensor_tensor(xc[:, NT:C], av[:, NT:C], col(h0, m, NS, NS), ALU.mult).then_inc(h_step, 1)
                nc.vector.tensor_tensor_scan(xc[:, 0:NT], av[:, 0:NT], it[:, 0:NT], 0.0, ALU.mult, ALU.add).then_inc(h_step, 1)
                dve.wait_ge(h_step, 4 * m + 1)
                nc.vector.tensor_tensor(xc[:, NT:C], xc[:, NT:C], it[:, NT:C], ALU.add).then_inc(h_step, 1)
                plain()
                dve.wait_ge(h_step, 4 * m + 3)
                nc.vector.tensor_copy(col(hco, m, HW, HW), xc[:, NT - 1:C]).then_inc(h_step, 1)
                dve.wait_ge(gelu_ready, m + 1)
                nc.vector.tensor_tensor(gy, xc, gy, ALU.mult).then_inc(ha_ready, 1)

            def rg_body(j, first):
                n = j + 1
                sample_state(j)
                if not first:
                    o_scale(n - 1, PAIR, NMETA + PAIR * (j - 1), qd)
                logits(j + 2, PAIR, z_t)
                if not first:
                    rg_tail_w(j - 1)
                running_sum(n, PAIR, CH, reset)
                if not first:
                    rg_tail_b(j - 1)
                scaled_qk(n, PAIR)
                plain()
                dve.wait_ge(so_mm, j + 1)
                nc.vector.tensor_copy(V3[:, :, bass.ds(NT + j, 1)], hd(sb7, 8, 1)).then_inc(so_ready, 1)
                if not first:
                    rg_tail_h(j - 1)
                    dve.wait_ge(xc_step, 4 * j)
                    dve.wait_ge(rgo_kept, j)
                    dve.wait_ge(xbias_ready, j)
                evacuate(U_RG, 2, j, 1, ext[:, 3:3 + C])
                scores(n, PAIR)
                c0 = NMETA + PAIR * j
                nb = state_banks(n)
                dve.wait_ge(xbias_ready, j + 1)
                dve.wait_ge(acc_free[1], G_RG[1] + 2 * j + 1)
                for t in range(3):
                    if t == 2:
                        state(nb, PAIR, CH, 0, 1, 0, 0, sb6)
                        state(nb + 1, PAIR, CH, 0, 1, 0, 1, sb7)
                    dve.wait_ge(xc_step, 4 * j + t)
                    nc.vector.scalar_tensor_tensor(xc[:, 0:NT], ext[:, t:t + NT], par(f"w{t}", j), xc[:, 0:NT],
                                                   ALU.mult, ALU.add).then_inc(xc_step, 1)
                nc.vector.scalar_tensor_tensor(xc[:, NT:C], ext[:, NT + 3:C + 3], par("w3", j), col(rgp, j, NS, NS),
                                               ALU.mult, ALU.add).then_inc(xc_step, 1)
                nc.vector.tensor_copy(col(rgo, j, RGW, RGW), ext[:, C + 3 - RGW:C + 3]).then_inc(rgo_kept, 1)
                o_copy(n, PAIR, c0, 0, sb6)
                o_copy(n, PAIR, c0, 1, sb7)
                state(nb + 2, PAIR, CH, 1, 0, 1, 0, sb6)
                dve.wait_ge(o_squared, 2 * n + 2)
                sum_halves(n, PAIR)
                if not first:
                    dve.wait_ge(ha_stored, 16 * j)
                evacuate(U_RG + 1, 2, j, 0, gy)
                state(nb + 3, PAIR, CH, 1, 0, 1, 1, sb7)

            dve.wait_ge(s_act, 1)
            dve.wait_ge(sg_ready, 2)
            dve.wait_ge(set_v, steps[0])
            rg_body(0, True)
            with dve.Fori(1, NPAIR) as j:
                rg_body(j, False)
            o_scale(NPAIR, PAIR, NMETA + PAIR * (NPAIR - 1), qd)
            dve.wait_ge(s_act, 3)
            sum_halves(NPAIR + 1, NS)
            rg_tail_w(NPAIR - 1)
            rg_tail_b(NPAIR - 1)
            rg_tail_h(NPAIR - 1)
            dve.wait_ge(orinv_ready, NPAIR + 2)
            dve.wait_ge(so_ready, NB)
            o = V3[:, :, NT:C].rearrange("p (h e) t -> p h e t", h=H)
            nc.vector.tensor_tensor(o, o, hd(srv, H, NS).unsqueeze(2).broadcast_to([P, H, 2, NS]), ALU.mult).then_inc(o_ready, 1)
            dve.wait_ge(o_ready, NPAIR + 2)

            dve.wait_ge(sS_stored, 16 * NB)
            dve.wait_ge(gate_mm, 2 * NPAIR)

            def gate_o(i):
                for s, g in ((0, 1), (1, 0)):
                    k = 2 * i + s
                    if not isinstance(i, int):
                        dve.wait_ge(obl_done, k - 1)
                    evacuate(U_GO + s, 2, i, g, T[s])
                    dve.wait_ge(silu_done, k + 1)
                    nc.vector.scalar_tensor_tensor(T[s], blk(V, k), par("gn", k), T[s], ALU.mult, ALU.mult).then_inc(og_done, 1)
                    dve.wait_ge(obh_done, k + 1)
                    nc.vector.tensor_tensor(blk(OBL, k), T[s], blk(OBH, k).bitcast(F32), ALU.subtract).then_inc(obl_done, 1)
            gate_o(0)
            with dve.Fori(1, KB // 2) as i:
                gate_o(i)
            with dve.Fori(0, KB) as j:
                dve.wait_ge(acc_free[0], G_B[0] + j)
                evacuate(U_B, 2, j, 1, T[2])
                dve.wait_ge(tanh_done, j + 1)
                dve.wait_ge(unit_done[0], nth(U_B + 1, 2, j) + 1)
                nc.vector.scalar_tensor_tensor(view3(blk(MG, j)), view3(T[2]), 1.0, accv[0], ALU.add, ALU.mult)\
                    .then_inc(acc_free[0], 1)
            for k in range(KB):
                dve.wait_ge(hah_done, k + 1)
                nc.vector.tensor_tensor(blk(HAL, k), blk(HA, k), blk(HAH, k).bitcast(F32), ALU.subtract).then_inc(hal_done, 1)

            def merged_low(k):
                dve.wait_ge(mgh_done, k + 1)
                nc.vector.scalar_tensor_tensor(blk(MGL, k), blk(MG, k), 0.5, blk(MGH, k).bitcast(F32), ALU.mult, ALU.subtract)\
                    .then_inc(mgl_done, 1)

            def merge_gate(j):
                dve.wait_ge(acc_free[0], G_A[0] + j)
                evacuate(U_A, 2, j, 1, T[2])

            def merge(j):
                dve.wait_ge(tanh_done, j + KB + 1)
                dve.wait_ge(unit_done[0], nth(U_A + 1, 2, j) + 1)
                nc.vector.scalar_tensor_tensor(view3(T[0]), view3(T[2]), 1.0, accv[0], ALU.add, ALU.mult)\
                    .then_inc(acc_free[0], 1)
                dve.wait_ge(acc_free[0], G_A[0] + j + 1)
                nc.vector.tensor_tensor(blk(MG, j), blk(MG, j), T[0], ALU.add).then_inc(ma_done, 1)
                dve.wait_ge(ma_done, j + 1)
            with dve.Fori(0, KB - 1) as j:
                merge_gate(j)
                merge(j)
            merge_gate(KB - 1)
            for k in range(KB - 1):
                merged_low(k)
            merge(KB - 1)
            merged_low(KB - 1)
            for k in range(KB):
                g = 1 - k % 2
                dve.wait_ge(unit_done[slot_of(U_OUT + k)], nth(U_OUT + k) + 1)
                dve.wait_ge(xr_loaded[k], 16)
                nc.vector.tensor_tensor(view3(blk(X2, k)), accv[g], view3(blk(X2, k)), ALU.add).then_inc(acc_free[g], 1)
                dve.wait_ge(xh2_done, k + 1)
                nc.vector.scalar_tensor_tensor(blk(X2L, k), blk(X2, k), par("g2", k), blk(X2H, k).bitcast(F32),
                                               ALU.mult, ALU.subtract).then_inc(xl2_done, 1)
                dve.wait_ge(sq2_done, k + 1)
                if k == 0:
                    nc.vector.tensor_copy(sqsum, T[0]).then_inc(sum2_done, 1)
                else:
                    dve.wait_ge(sum2_done, k)
                    nc.vector.tensor_tensor(sqsum, sqsum, T[k % 2], ALU.add).then_inc(sum2_done, 1)
            dve.wait_ge(fst_loaded, 32)
            fs = fst.rearrange("p (r k b) -> p r k b", r=2, k=UB)

            def fwide(r):
                return fpr[:, r * UB:(r + 1) * UB].unsqueeze(2).broadcast_to([P, UB, NS])
            pf = hd(fps, UB, NS)
            nc.vector.tensor_tensor(pf, fs[:, 0], fwide(0), ALU.mult).then_inc(set_f, 1)
            nc.vector.tensor_tensor(fs[:, 1], fs[:, 1], fwide(1), ALU.mult).then_inc(set_f, 1)
            dve.wait_ge(set_f, 2)
            nc.vector.tensor_tensor(pf, pf, fs[:, 1], ALU.add).then_inc(set_f, 1)
            dve.wait_ge(set_f, 3)
            nc.vector.memset(eg[:, 0:2], 0.0)
            nc.vector.memset(ev[:, 0:2], 0.0)
            nc.vector.tensor_tensor(pf, pf, fwide(3), ALU.add).then_inc(set_f, 1)
            dve.wait_ge(set_f, 4)
            dve.wait_ge(xl2_done, KB)
            dve.wait_ge(r2_done, 1)

            def conv(F, off_b, u, per, i, g, bias_sem, e_t, c_t, step_sem, kept):
                dve.wait_ge(unit_done[slot_of(u)], nth(u, per, i) + 1)
                dve.wait_ge(bias_sem, F)
                dve.wait_ge(step_sem, 3 * F)
                dve.wait_ge(kept, F)
                nc.vector.tensor_tensor(view3(e_t[:, 2:2 + C]), accv[g], view3(rms), ALU.mult).then_inc(acc_free[g], 1)
                dve.wait_ge(bias_sem, F + 1)
                for t in range(2):
                    dve.wait_ge(step_sem, 3 * F + t)
                    nc.vector.scalar_tensor_tensor(c_t[:, 0:NT], e_t[:, t:t + NT], fpr[:, bass.ds(t * UB + off_b + F, 1)],
                                                   c_t[:, 0:NT], ALU.mult, ALU.add).then_inc(step_sem, 1)
                nc.vector.scalar_tensor_tensor(c_t[:, NT:C], e_t[:, NT + 2:C + 2], fpr[:, bass.ds(2 * UB + off_b + F, 1)],
                                               fps[:, bass.ds((off_b + F) * NS, NS)], ALU.mult, ALU.add).then_inc(step_sem, 1)
                nc.vector.tensor_copy(ubuf[:, bass.ds((off_b + F) * UW, UW)], e_t[:, C + 2 - UW:C + 2]).then_inc(kept, 1)

            def ffn_block(F, u, per, i, half, f, adds):
                conv(F, 0, u, per, i, 0, gbias_ready, eg, cg, gconv_step, gkept)
                conv(F, FB, u + 1, per, i, 1, vbias_ready, ev, cv, vconv_step, vkept)
                adds(0)
                dve.wait_ge(ggelu_done, F + 1)
                dve.wait_ge(vconv_step, 3 * F + 3)
                dve.wait_ge(acth_done, F)
                dve.wait_ge(actl_done, F)
                nc.vector.tensor_tensor(act_t, cg, cv, ALU.mult).then_inc(act_done, 1)
                adds(1)
                dve.wait_ge(acth_done, F + 1)
                b = (half * GRP + f) * C
                nc.vector.tensor_tensor(AL[:, b:b + C], act_t, AH[:, b:b + C].bitcast(F32), ALU.subtract).then_inc(actl_done, 1)

            def add(n_down, grp, m, u_last, per, i):
                g = m % 2
                if m < KB - 1:
                    dve.wait_ge(down_mm, (KB - 1) * n_down + m + 1)
                else:
                    dve.wait_ge(unit_done[slot_of(u_last)], nth(u_last, per, i) + 1)
                dve.wait_ge(acc_free[g], G_FFN[g] + grp + m // 2)
                nc.vector.tensor_tensor(view3(blk(X2, m)), accv[g], view3(blk(X2, m)), ALU.add).then_inc(acc_free[g], 1)

            GU, GD = GRP, KB // 2
            NU, ND = 2 * GRP, GRP
            per, gper = 2 * (NU + ND), 2 * (GU + GD)

            def ffn_group(F0_, u0, grp0, half, n_down=None, i=0):
                def down(m):
                    add(n_down, grp0 + GRP, m, u0 + NU + ND - 1, per, i)
                for f in range(GRP):
                    last = f == GRP - 1 and n_down is not None
                    ffn_block(F0_ + f, u0 + 2 * f, per, i, half, f, down if last else lambda k: None)
                if n_down is not None:
                    for m in range(2, KB):
                        down(m)

            ffn_group(0, U_FFN, 0, 0)
            with dve.Fori(0, NGRP // 2 - 1) as i:
                ffn_group(2 * GRP * i + GRP, U_FFN + NU, GU + gper * i, 1, 2 * i, i)
                ffn_group(2 * GRP * i + 2 * GRP, U_FFN + 2 * NU + ND, 2 * GU + GD + gper * i, 0, 2 * i + 1, i)
            n = NGRP // 2 - 1
            ffn_group(GRP * (NGRP - 1), U_FFN + NU + n * per, GU + gper * n, 1, 2 * n)
            for m in range(KB):
                add(NGRP - 1, 2 * GU + GD + gper * n, m, N_UNITS - 1, 0, 0)
                dve.wait_ge(sq3_done, m + 1)
                if m == 0:
                    nc.vector.tensor_copy(ysum, ysq).then_inc(sum3_done, 1)
                else:
                    dve.wait_ge(sum3_done, m)
                    nc.vector.tensor_tensor(ysum, ysum, ysq, ALU.add).then_inc(sum3_done, 1)
            dve.wait_ge(r3_done, 1)
            for k in range(KB):
                nc.vector.scalar_tensor_tensor(blk(X2, k), blk(X2, k), par("gf", k), yrs, ALU.mult, ALU.mult).then_inc(y_done, 1)


def weight_units(w_in, w_a, w_b, w_out, w_up, w_down):
    import numpy as np

    def column_units(w):
        n = w.shape[1] // P
        return w.reshape(KB, P, n, P).transpose(2, 1, 0, 3).reshape(n, P, D)

    edges = np.cumsum([D, D, QK, QK, D, RANK, D, D, D])
    rg_x, rg_y, q, k, v, low, go, m_a, m_b = np.split(w_in, edges[:-1], axis=1)
    low = np.concatenate([low, np.zeros((D, P - RANK), w_in.dtype)], axis=1)

    def paired(a, b):
        return np.stack([column_units(a), column_units(b)], axis=1).reshape(-1, P, D)

    ups = paired(w_up[:, :FF], w_up[:, FF:])

    def down_units(g):
        t = w_down[g * GRP * P:(g + 1) * GRP * P].reshape(GRP, P, KB, P).transpose(2, 0, 1, 3)
        return t.reshape(GRP, KB, P, P).transpose(0, 2, 1, 3).reshape(GRP, P, D)

    parts = [column_units(low), column_units(q), column_units(k), column_units(v), paired(rg_x, rg_y),
             column_units(go), paired(m_b, w_b), paired(m_a, w_a), column_units(w_out)]
    n = 2 * GRP
    parts.append(ups[:n])
    for g in range(1, NGRP):
        parts += [ups[g * n:(g + 1) * n], down_units(g - 1)]
    parts.append(down_units(NGRP - 1))
    return np.ascontiguousarray(np.concatenate(parts))


def kernel(**inputs):
    import ml_dtypes
    import numpy as np
    from concourse import bacc
    from concourse.bass_utils import run_bass_kernel_spmd

    a = {k: np.asarray(v) for k, v in inputs.items()}
    f32 = np.float32

    def by_partition(rows):
        r = rows.reshape(rows.shape[:-1] + (-1, P))
        return np.moveaxis(r, -1, 0)

    def samples_last(s, r0, r1):
        t = by_partition(s[:, r0:r1])
        t = t.transpose(0, 2, 3, 1)
        return np.concatenate([t, np.zeros(t.shape[:3] + (NS - NB,), f32)], axis=3)

    tokens = np.concatenate([a["meta_tokens"], a["x_prompt"][0], a["x_sample"][:, 0], np.zeros((NS - NB, D), f32)])
    x = np.ascontiguousarray(tokens.T.reshape(KB, P, C))
    vecs = [a["rg_conv_w"][0][i] for i in range(4)] + [a["rg_conv_b"][0], a["rg_ba"][0], a["rg_bx"][0],
            a["rg_lambda"][0], a["norm1_g"][0], a["gla_norm_g"][0].reshape(-1), a["norm2_g"][0], a["final_norm_g"]]
    gates = np.zeros((KB, P, 2, P), f32)
    for c, w in enumerate((a["rg_wa"][0], a["rg_wx"][0])):
        w = w.reshape(KB, 2, 64, 64)
        gates[:, 0:64, c, 0:64] = w[:, 0]
        gates[:, 64:128, c, 64:128] = w[:, 1]
    t = np.arange(P)
    ins = {
        "x": x,
        "w": weight_units(a["w_in"][0], a["w_branch_a"][0], a["w_branch_b"][0], a["w_out"][0], a["w_ffn_up"][0],
                          a["w_ffn_down"][0]),
        "params": np.ascontiguousarray(by_partition(np.stack(vecs)).reshape(P, RP_N)),
        "rg_states": np.ascontiguousarray(samples_last(a["state_rg_conv"][0], 0, 3).reshape(P, -1)),
        "h0": np.ascontiguousarray(samples_last(a["state_rg_h"][0][:, None], 0, 1).reshape(P, -1)),
        "rg_old": np.ascontiguousarray(a["state_rg_conv"][0][:, 1:].reshape(16, -1)),
        "ffn_old": np.ascontiguousarray(a["state_ffn_conv"][0][:, 1:].reshape(16, -1)),
        "gla_bias": np.ascontiguousarray(by_partition(a["gla_b_gate"][0])),
        "gla_w_gate": np.ascontiguousarray(a["gla_w_gate"][0]),
        "gla_state": np.ascontiguousarray(a["state_gla"][0].transpose(0, 2, 1, 3).reshape(NB, P, H * DV)),
        "rg_gates": gates.reshape(KB, P, 2 * P),
        "ffn_states": np.ascontiguousarray(samples_last(a["state_ffn_conv"][0], 0, 2).reshape(P, -1)),
        "ffn_params": np.ascontiguousarray(by_partition(np.concatenate([a["ffn_conv_w"][0], a["ffn_conv_b"]])).reshape(P, -1)),
        "reset": np.tile((np.arange(4 * PAIR) % CH != 0), (P, 1)).astype(ml_dtypes.bfloat16),
        "reset16": np.tile((np.arange(4 * NMETA) % NMETA != 0), (P, 1)).astype(ml_dtypes.bfloat16),
        "ident": np.eye(P, dtype=f32),
        "mask": ((t[None, :] >= t[:, None]) & (t[None, :] // CH == t[:, None] // CH)).astype(np.int32),
    }
    out_shapes = {
        "y": (KB, P, C), "gla_prompt": (P, H * DV), "gla_sample": (NB, P, H * DV), "rg_last": (P, KB * RGW),
        "h_last": (P, KB * HW), "u_last": (P, UB * UW), "rg_old": ins["rg_old"].shape, "ffn_old": ins["ffn_old"].shape,
    }
    nc = bacc.Bacc("TRN2", target_bir_lowering=False, num_devices=1)
    I = {n: nc.dram_tensor(f"in_{n}", v.shape, mybir.dt.from_np(v.dtype), kind="ExternalInput").ap() for n, v in ins.items()}
    O = {n: nc.dram_tensor(f"out_{n}", s, F32, kind="ExternalOutput").ap() for n, s in out_shapes.items()}
    build(nc, I, O)
    got = run_bass_kernel_spmd(nc, [{f"in_{n}": v for n, v in ins.items()}], core_ids=[0]).results[0]
    o = {n: np.asarray(got[f"out_{n}"]) for n in out_shapes}

    y = o["y"].reshape(D, C).T
    def rows(packed, n, w):
        return packed.reshape(P, n, w).transpose(2, 1, 0).reshape(w, n * P)
    rg, h, u = rows(o["rg_last"], KB, RGW), rows(o["h_last"], KB, HW), rows(o["u_last"], UB, UW)
    rg_old = o["rg_old"].reshape(NB, 2, D)
    ffn_old = o["ffn_old"].reshape(NB, 1, 2 * FF)
    c = np.ascontiguousarray
    return (
        c(y[NMETA:NT])[None], c(y[NT:NT + NB])[:, None],
        c(rg[0:3])[None, None], c(h[0])[None, None],
        c(o["gla_prompt"].reshape(P, H, DV).transpose(1, 0, 2))[None, None], c(u[0:2])[None, None],
        np.concatenate([rg_old, rg[3:3 + NB][:, None]], axis=1)[None], c(h[1:1 + NB])[None],
        c(o["gla_sample"].reshape(NB, P, H, DV).transpose(0, 2, 1, 3))[None],
        np.concatenate([ffn_old, u[2:2 + NB][:, None]], axis=1)[None],
    )
```

```python
from contextlib import ExitStack

import concourse.bass as bass
from concourse import mybir

ALU = mybir.AluOpType
ACT = mybir.ActivationFunctionType
F32 = mybir.dt.float32
F32R = mybir.dt.float32r
BF16 = mybir.dt.bfloat16
I32 = mybir.dt.int32
LN_EXP = "natural_log_exp_and_others"

P = 128
D = 1024
KB = D // P
NMETA = 16
SEQ = 1024
NT = NMETA + SEQ
NB = 8
NS = 10
C = NT + NS
NW = C // 3
H = 4
DK = 128
DV = 256
QK = H * DK
RANK = 16
CH = 64
PAIR = 2 * CH
NPAIR = SEQ // PAIR
FF = 3 * D
FB = FF // P
UB = 2 * FB
GRP = 3
NGRP = FB // GRP
RGW = 13
HW = 11
UW = 12
EPS = 1e-6
TINY = 2.0 ** -63

U_QKV = 1
U_RG = U_QKV + 16
U_GO = U_RG + 16
U_B = U_GO + 8
U_A = U_B + 16
U_OUT = U_A + 16
U_FFN = U_OUT + 8
N_UNITS = U_FFN + UB + FB
U_LAST = N_UNITS - GRP
G_QKV = (1, 0)
G_RG = (9, 8)
G_GO = (25, 24)
G_B = (29, 28)
G_A = (37, 36)
G_OUT = (45, 44)
G_FFN = (49, 48)
G_LAST = tuple(g + (UB + KB * (NGRP - 1)) // 2 for g in G_FFN)

RP = {n: i * KB for i, n in enumerate(["w0", "w1", "w2", "w3", "b", "ba", "bx", "lam", "g1", "gn", "g2", "gf"])}
RP_N = 12 * KB



def view3(t):
    return t.rearrange("p (a n) -> p a n", a=3)


def hd(t, n, w):
    return t[:, 0:n * w].rearrange("p (h t) -> p h t", h=n)


def slot_of(u):
    return u % 2


def nth(u, per=0, i=0):
    return u // 2 + per // 2 * i


def build(nc, I, O):
    ctx = ExitStack()
    with ctx:
        base = 16512
        CB = 4 * C
        TB = (CB + 31) // 32 * 32

        def at(name, off, cols, dt=F32, parts=P):
            return nc.alloc_sbuf_tensor_at(name, [parts, cols], dt, offset=base + off)[:, :]

        A0 = 0
        V0 = 16 * CB
        W0 = V0 + KB * CB
        R0 = W0 + 6 * 4096
        B0 = R0
        M0 = B0 + KB * CB
        T0 = M0 + KB * CB
        E0 = T0 + 3 * TB
        XH, XL = at("xn_hi", A0, KB * C, F32R), at("xn_lo", A0 + KB * CB, KB * C, F32R)
        X1 = at("x_in", V0, KB * C)
        V = at("v_o", V0, KB * C)
        raw = [at(f"w_raw{s}", W0 + 4096 * s, D) for s in range(2)]
        whi = [at(f"w_hi{s}", W0 + 8192 + 8192 * s, D, F32R) for s in range(2)]
        wlo = [at(f"w_lo{s}", W0 + 12288 + 8192 * s, D, F32R) for s in range(2)]
        off = [R0]

        def nxt(name, cols, dt=F32, size=4, parts=P):
            t = at(name, off[0], cols, dt, parts)
            off[0] += (cols * size + 31) // 32 * 32
            return t

        ext = nxt("rg_ext", C + 3)
        xc = nxt("rg_xc_h", C)
        rt = nxt("rg_r", C)
        it = nxt("rg_i_b", C)
        av = nxt("rg_a", C)
        th = nxt("rg_mult", C)
        gy = nxt("rg_gelu_ha", C)
        zg = nxt("gla_z_g_osq", 8 * PAIR)
        z_t, g_t = zg[:, 0:4 * PAIR], zg[:, 4 * PAIR:8 * PAIR]
        bc = nxt("gla_bc_keT", 4 * PAIR)
        eb = nxt("gla_exp_bc", 4 * PAIR)
        kk = nxt("gla_kd_ke_vcopy", 8 * PAIR)
        kd, ke = kk[:, 0:4 * PAIR], kk[:, 4 * PAIR:8 * PAIR]
        qd = nxt("gla_qd", 4 * PAIR)
        vtm = nxt("gla_v_tokens", D)
        am = nxt("gla_scores", 4 * PAIR)
        qs = nxt("gla_qs", 4 * PAIR)
        S = nxt("gla_state", H * DV)
        qkp_at = off[0]
        qkp = nxt("gla_qk_pair", 8 * PAIR)
        rgst = at("rg_states", qkp_at, 3 * KB * NS)
        rgtmp = at("rg_states_tmp", qkp_at + 1024, KB * NS)
        glr = nxt("gla_low_rank", C)
        gw = nxt("rg_gate_weights", 2 * P)
        sS = nxt("smp_state", H * DV)
        svb = nxt("smp_v_rows", D)
        svt = svb
        wg = nxt("gla_gate_weights", QK)
        reset = nxt("scan_reset", 4 * PAIR, BF16, 2)
        rs16 = nxt("scan_reset16", 4 * NMETA, BF16, 2)
        ident = nxt("ident", P)
        mask = nxt("causal_mask", P, I32)
        rgp = nxt("rg_smp_conv", KB * NS)
        h0 = nxt("rg_h0", KB * NS)
        der = nxt("rg_derived", 5 * KB)
        gbz = nxt("gla_bias", H)
        sqk = nxt("smp_qk", 8 * NS)
        sdec = nxt("smp_decay", H * NS)
        srv = nxt("smp_rinv", H * NS)
        off[0] = max(off[0], E0)
        rgo = nxt("rg_last_columns", KB * RGW)
        hco = nxt("h_last_columns", KB * HW)
        prm = nxt("params", RP_N)
        ones = nxt("ones", P)
        cst = nxt("consts", 2)
        rms = nxt("rms", C)
        assert off[0] + base <= 229344, off[0] + base
        OBH, OBL = at("o_hi", B0, KB * C, F32R), at("o_lo", V0, KB * C, F32R)
        HAH, HAL = at("h_hi", V0, KB * C, F32R), at("h_lo", B0, KB * C, F32R)
        HA = at("h", B0, KB * C)
        MG = at("merged", M0, KB * C)
        MGH, MGL = at("merged_hi", A0, KB * C, F32R), at("merged_lo", A0 + KB * CB, KB * C, F32R)
        X2 = at("residual", V0, KB * C)
        X2H, X2L = at("xn2_hi", B0, KB * C, F32R), at("xn2_lo", M0, KB * C, F32R)
        T = [at(f"tmp{i}", T0 + TB * i, C) for i in range(3)]
        sqsum = T[2]
        act_bytes = (2 * GRP * CB + 31) // 32 * 32
        AH = at("act_hi", A0, 2 * GRP * C, F32R)
        AL = at("act_lo", A0 + act_bytes, 2 * GRP * C, F32R)
        fst = at("ffn_states", A0, 2 * UB * NS)
        F0 = A0 + 2 * act_bytes
        eg = at("gate_ext", F0, C + 2)
        ev = at("val_ext", F0 + TB, C + 2)
        cg = at("gate_conv", F0 + 2 * TB, C)
        fpr = at("ffn_params", F0 + 3 * TB, 4 * UB)
        fps = at("ffn_smp_conv", F0 + 3 * TB + 768, UB * NS)
        assert F0 + 3 * TB + 768 + 4 * UB * NS <= V0
        cv, act_t, ubuf = T[0], T[1], at("u_last_columns", T0 + 2 * TB, UB * UW)
        lhi = [at(f"last_hi{u}", B0 + 8192 * u, D, F32R) for u in range(GRP)]
        llo = [at(f"last_lo{u}", B0 + 8192 * u + 4096, D, F32R) for u in range(GRP)]
        assert 8192 * GRP <= KB * CB
        Y = at("y", M0, KB * C)
        ysq, ysum, yrs = at("y_square", F0, 2 * NW), at("y_square_sum", F0 + TB, C), at("y_rms", F0 + 2 * TB, C)

        acc = [ctx.enter_context(nc.psum_tensor(f"acc{s}", [P, 3, 512], F32)) for s in range(2)]
        sb6 = ctx.enter_context(nc.psum_tensor("small6", [P, 512], F32))
        sb7 = ctx.enter_context(nc.psum_tensor("small7", [P, 512], F32))
        accv = [a[:, :, 0:NW] for a in acc]

        def last_bank(m):
            return acc[(m - 2) // 3][:, (m - 2) % 3] if m >= 2 else (sb6, sb7)[m]

        qk_scr = nc.dram_tensor("qk_scratch", (8, P, C), F32).ap()
        sv_scr = nc.dram_tensor("smp_v_scratch", (NB, D), F32).ap()
        ha_scr = nc.dram_tensor("ha_scratch", (KB, P, C), F32).ap()

        def sem(n):
            return ctx.enter_context(nc.semaphore(n))

        def sems(n, k=2):
            return [sem(f"{n}{i}") for i in range(k)]

        def col(t, j, n=1, w=1):
            return t[:, bass.ds(j * w, n)]

        def blk(t, j):
            return t[:, bass.ds(j * C, C)]

        def par(name, j):
            return prm[:, bass.ds(j + RP[name], 1)]

        def squares(w):
            return zg[:, 0:8 * w].rearrange("p (h e t) -> p h e t", h=H, e=2)

        V3 = V.rearrange("p (k c) -> p k c", k=KB)

        w_loaded, w_hi_done, w_split, unit_done = sems("w_loaded"), sems("w_hi_done"), sems("w_split"), sems("unit_done")
        acc_free = sems("acc_free")
        gate_mm, down_mm = sem("gate_mm"), sem("down_mm")
        x_loaded, prm_loaded = sems("x_loaded", KB), sem("prm_loaded")
        par_loaded, const_loaded, gwt_loaded = sem("par_loaded"), sem("const_loaded"), sem("gwt_loaded")
        sq1_done, sum1_done, sum1_mm, lnr1_done, r1_done = (
            sem(n) for n in ("sq1_done", "sum1_done", "sum1_mm", "lnr1_done", "r1_done"))
        xh1_done, xl1_done = sem("xh1_done"), sem("xl1_done")
        set_v, set_a = sem("set_v"), sem("set_a")
        ones_done = sem("ones_done")
        qk_stored = sems("qk_stored")
        qk_loaded = sem("qk_loaded")
        zg_mm, z_ready, absz_done, expz_done, lnz_done = (sem(n) for n in ("zg_mm", "z_ready", "absz_done", "expz_done", "lnz_done"))
        g_ready, bc_ready, bl_ready, bm_ready, eb_ready, em_ready, enm_ready, eke_ready = (
            sem(n) for n in ("g_ready", "bc_ready", "bl_ready", "bm_ready", "eb_ready", "em_ready", "enm_ready", "eke_ready"))
        qs_ready, qd_ready, kd_ready, ke_ready = sem("qs_ready"), sem("qd_ready"), sem("kd_ready"), sem("ke_ready")
        vT_mm, vT_ready, keT_mm, keT_ready, A_mm, A_ready = (
            sem(n) for n in ("vT_mm", "vT_ready", "keT_mm", "keT_ready", "A_mm", "A_ready"))
        vcp_ready = sem("vcp_ready")
        dS_mm, S_ready, O_mm, o_copied, o_squared, o_summed = (
            sem(n) for n in ("dS_mm", "S_ready", "O_mm", "o_copied", "o_squared", "o_summed"))
        onorm_mm, olog_done, orinv_ready, o_ready = (sem(n) for n in ("onorm_mm", "olog_done", "orinv_ready", "o_ready"))
        sqk_loaded, sT_mm, sT_ready, sg_ready, sS_loaded, sS_stored = (
            sem(n) for n in ("sqk_loaded", "sT_mm", "sT_ready", "sg_ready", "sS_loaded", "sS_stored"))
        sv_stored, svb_loaded, sS_decayed, sS_ready, so_mm, so_ready = (
            sem(n) for n in ("sv_stored", "svb_loaded", "sS_decayed", "sS_ready", "so_mm", "so_ready"))
        s_act = sem("s_act")
        xbias_ready, xc_step, rgo_kept, gelu_ready, th_ready, a_ready, a2_ready, w_ready, ml_done, m_ready = (
            sem(n) for n in ("xbias_ready", "xc_step", "rgo_kept", "gelu_ready", "th_ready", "a_ready",
                             "a2_ready", "w_ready", "ml_done", "m_ready"))
        ix_ready, b_ready, h_step, ha_ready, ha_stored = (
            sem(n) for n in ("ix_ready", "b_ready", "h_step", "ha_ready", "ha_stored"))
        tanh_done = sem("tanh_done")
        silu_done, og_done, obh_done, obl_done = sem("silu_done"), sem("og_done"), sem("obh_done"), sem("obl_done")
        hl_loaded, o_used = sems("hl_loaded", KB), sem("o_used")
        hah_done, hal_done, ma_done = sem("hah_done"), sem("hal_done"), sem("ma_done")
        mgh_done, mgl_done = sem("mgh_done"), sem("mgl_done")
        xr_loaded = sems("xr_loaded", KB)
        sq2_done, sum2_done, sum2_mm, lnr2_done, r2_done, xh2_done, xl2_done = (
            sem(n) for n in ("sq2_done", "sum2_done", "sum2_mm", "lnr2_done", "r2_done", "xh2_done", "xl2_done"))
        fst_loaded, set_f = sem("fst_loaded"), sem("set_f")
        gbias_ready, gconv_step, vbias_ready, vconv_step, gkept, vkept = (
            sem(n) for n in ("gbias_ready", "gconv_step", "vbias_ready", "vconv_step", "gkept", "vkept"))
        ggelu_done, act_done, acth_done, actl_done = (
            sem(n) for n in ("ggelu_done", "act_done", "acth_done", "actl_done"))
        last_mm, last_added, sq3_done, sum3_done, sum3_mm, lnr3_done, r3_done, yg_done, y_pool_done, y_done = (
            sem(n) for n in ("last_mm", "last_added", "sq3_done", "sum3_done", "sum3_mm", "lnr3_done", "r3_done", "yg_done",
                             "y_pool_done", "y_done"))
        stored = sem("stored")
        y_stored = sem("y_stored")

        block = ctx.enter_context(nc.Block())

        @block.sync
        def _(sp):
            sp.dma_start(raw[0], I["w"][0]).then_inc(w_loaded[0], 16)
            sp.dma_start(prm, I["params"]).then_inc(prm_loaded, 16)
            sp.dma_start(blk(X1, 1), I["x"][1]).then_inc(x_loaded[1], 16)
            sp.dma_start(raw[1], I["w"][1]).then_inc(w_loaded[1], 16)
            for k in range(3, KB, 2):
                sp.dma_start(blk(X1, k), I["x"][k]).then_inc(x_loaded[k], 16)
            for t, name in ((rgst, "rg_states"), (h0, "h0"), (gbz, "gla_bias")):
                sp.dma_start(t, I[name]).then_inc(par_loaded, 16)
            sp.dma_start(wg[0:RANK, :], I["gla_w_gate"]).then_inc(const_loaded, 16)
            for t, name in ((reset, "reset"), (rs16, "reset16"), (ident, "ident"), (mask, "mask")):
                sp.dma_start(t, I[name]).then_inc(const_loaded, 16)
            sp.dma_start(gw, I["rg_gates"][0]).then_inc(gwt_loaded, 16)
            sp.dma_start(O["rg_old"], I["rg_old"]).then_inc(stored, 16)
            sp.dma_start(O["ffn_old"], I["ffn_old"]).then_inc(stored, 16)
            sp.dma_start(sS, I["gla_state"][0]).then_inc(sS_loaded, 16)
            with sp.Fori(1, N_UNITS // 2) as i:
                for s in range(2):
                    sp.wait_ge(w_split[s], i)
                    sp.dma_start(raw[s], I["w"][2 * i + s]).then_inc(w_loaded[s], 16)
            sp.wait_ge(w_split[0], N_UNITS // 2)
            sp.dma_start(raw[0], I["w"][N_UNITS - 1]).then_inc(w_loaded[0], 16)
            sp.wait_ge(rgo_kept, KB)
            sp.wait_ge(h_step, 4 * KB)
            sp.dma_start(O["rg_last"], rgo).then_inc(stored, 16)
            sp.dma_start(O["h_last"], hco).then_inc(stored, 16)
            sp.wait_ge(gkept, FB)
            sp.wait_ge(vkept, FB)
            sp.dma_start(O["u_last"], ubuf).then_inc(stored, 16)
            Y3, y_out = Y.rearrange("p (k c) -> p k c", k=KB), O["y"].rearrange("k p c -> p k c")
            for n in range(2):
                sp.wait_ge(y_pool_done, KB * (n + 1))
                sp.dma_start(y_out[:, :, n * NW:(n + 1) * NW], Y3[:, :, n * NW:(n + 1) * NW]).then_inc(y_stored, 16)
            for k in range(0, KB, 2):
                sp.wait_ge(y_done, k + 2)
                sp.dma_start(y_out[:, k:k + 2, 2 * NW:], Y3[:, k:k + 2, 2 * NW:]).then_inc(y_stored, 16)
            sp.wait_ge(y_stored, 16 * (2 + KB // 2))
            sp.wait_ge(stored, 16 * 6)
            sp.wait_ge(sS_stored, 16 * NB)

        @block.gpsimd
        def _(pool):
            def split(i, s):
                pool.wait_ge(w_loaded[s], 16 * i + 16)
                if not isinstance(i, int) or i > 0:
                    pool.wait_ge(unit_done[s], i)
                nc.gpsimd.tensor_tensor(whi[s], raw[s], one, ALU.mult).then_inc(w_hi_done[s], 1)
                pool.wait_ge(w_hi_done[s], i + 1)
                nc.gpsimd.tensor_tensor(wlo[s], raw[s], whi[s].bitcast(F32), ALU.subtract).then_inc(w_split[s], 1)

            pool.wait_ge(ones_done, 1)
            one = ones[:, 0:1].broadcast_to([P, D])
            split(0, 1)
            with pool.Fori(1, (N_UNITS - GRP) // 2) as i:
                split(i, 0)
                split(i, 1)
            pool.wait_ge(unit_done[slot_of(U_LAST - 1 - GRP)], nth(U_LAST - 1 - GRP) + 1)
            for v in range(GRP):
                u = U_LAST + v
                s = slot_of(u)
                pool.wait_ge(w_loaded[s], 16 * nth(u) + 16)
                nc.gpsimd.tensor_tensor(lhi[v], raw[s], one, ALU.mult).then_inc(w_hi_done[s], 1)
                pool.wait_ge(w_hi_done[s], nth(u) + 1)
                nc.gpsimd.tensor_tensor(llo[v], raw[s], lhi[v].bitcast(F32), ALU.subtract).then_inc(w_split[s], 1)
            for n in range(2):
                c = slice(n * NW, (n + 1) * NW)
                pool.wait_ge(r3_done, n + 1)
                for m in range(KB):
                    pool.wait_ge(yg_done, KB * n + m + 1)
                    nc.gpsimd.tensor_tensor(blk(Y, m)[:, c], blk(Y, m)[:, c], yrs[:, c], ALU.mult).then_inc(y_pool_done, 1)

        @block.tensor
        def _(pe):
            def tile_products(s, t, g, xh, xl, first, last):
                for w, x, a, z in ((whi, xh, first, False), (whi, xl, False, False), (wlo, xh, False, last)):
                    for n in range(3):
                        mm = nc.tensor.matmul(accv[g][:, n], w[s][:, t * P:(t + 1) * P], x[:, n * NW:(n + 1) * NW],
                                              start=a, stop=z)
                return mm

            def unit(u, n_slot, g, n_grp, xh, xl, pieces=(), gate=None, used=None):
                s = slot_of(u)
                pe.wait_ge(w_split[s], n_slot + 1)
                pe.wait_ge(acc_free[g], n_grp)
                for k in range(KB):
                    if gate:
                        gate(k)
                    mm = tile_products(s, k, g, xh[:, k * C:(k + 1) * C], xl[:, k * C:(k + 1) * C], k == 0, k == KB - 1)
                    if k == KB - 1:
                        mm.then_inc(unit_done[s], 1)
                    elif used:
                        mm.then_inc(used, 1)
                    for f in dict(pieces).get(k, ()):
                        f()

            def norm_sum(src, n, bank, mm_sem):
                nc.tensor.matmul(bank[:, 0:NW], ones, src[:, n * NW:(n + 1) * NW], start=True, stop=True).then_inc(mm_sem, 1)

            order = [(0, 0), (0, 1), (0, 2)]
            for k in range(3, KB):
                order += [(1, k - 3), (0, k)]
            order += [(1, k) for k in range(KB - 3, KB)]
            for g, k in order:
                s = slot_of(g)
                if k == 0:
                    pe.wait_ge(w_split[s], 1)
                if g == 0:
                    pe.wait_ge(xh1_done, k + 1)
                    pe.wait_ge(xl1_done, k + 1)
                mm = tile_products(s, k, g, XH[:, k * C:(k + 1) * C], XL[:, k * C:(k + 1) * C], k == 0, k == KB - 1)
                if k == KB - 1:
                    mm.then_inc(unit_done[s], 1)
                if (g, k) == (1, KB - 3):
                    pe.wait_ge(sum1_done, KB)
                    norm_sum(xc, 0, sb6, sum1_mm)
                    norm_sum(xc, 1, sb7, sum1_mm)
                if (g, k) == (1, KB - 2):
                    pe.wait_ge(lnr1_done, 1)
                    norm_sum(xc, 2, sb6, sum1_mm)
            with pe.Fori(0, 3) as i:
                unit(U_QKV + 1, nth(U_QKV + 1, 2, i), 0, G_QKV[0] + i, XH, XL)
                unit(U_QKV + 2, nth(U_QKV + 2, 2, i), 1, G_QKV[1] + 1 + i, XH, XL)
            unit(U_QKV + 7, nth(U_QKV + 7), 0, G_QKV[0] + 3, XH, XL)

            def zg_piece(n, w, c0):
                pe.wait_ge(olog_done, n)
                for h in range(H):
                    mm = nc.tensor.matmul(sb6[:, h * w:(h + 1) * w], wg[0:RANK, h * DK:(h + 1) * DK],
                                          glr[0:RANK, bass.ds(c0, w)], start=True, stop=True)
                mm.then_inc(zg_mm, 1)

            def vT_piece(n, w, half):
                if half == 0:
                    pe.wait_ge(vcp_ready, n + 1)
                    pe.wait_ge(S_ready, 2 * n)
                pe.wait_ge(vT_ready, 2 * n + half)
                for e in range(4):
                    k = 4 * half + e
                    mm = nc.tensor.transpose(sb7[0:w, e * P:(e + 1) * P], kk[:, k * w:(k + 1) * w], ident)
                mm.then_inc(vT_mm, 1)

            def keT_piece(n, w, bank7_free=None, count=0):
                pe.wait_ge(ke_ready, n + 1)
                if bank7_free:
                    pe.wait_ge(bank7_free, count)
                for h in range(H):
                    mm = nc.tensor.transpose(sb7[0:w, h * DK:(h + 1) * DK], ke[:, h * w:(h + 1) * w], ident)
                mm.then_inc(keT_mm, 1)

            def A_piece(n, w, bank6_free, count):
                pe.wait_ge(qd_ready, n + 1)
                pe.wait_ge(kd_ready, n + 1)
                pe.wait_ge(bank6_free, count)
                for h in range(H):
                    mm = nc.tensor.matmul(sb6[0:w, h * w:(h + 1) * w], kd[:, h * w:(h + 1) * w],
                                          qd[:, h * w:(h + 1) * w], start=True, stop=True)
                mm.then_inc(A_mm, 1)

            def O_piece(bank, w, hh, inter):
                for q in range(4):
                    h, e = 2 * hh + q // 2, q % 2
                    s0 = h * DV + e * P
                    mm = nc.tensor.matmul(bank[:, q * w:(q + 1) * w], vtm[0:w, s0:s0 + P], am[0:w, h * w:(h + 1) * w],
                                          start=True, stop=not inter)
                    if inter:
                        mm = nc.tensor.matmul(bank[:, q * w:(q + 1) * w], S[:, s0:s0 + P], qs[:, h * w:(h + 1) * w],
                                              start=False, stop=True)
                mm.then_inc(O_mm, 1)

            def dS_piece(bank, n, w, hh):
                pe.wait_ge(keT_ready, n + 1)
                pe.wait_ge(o_copied, 2 * n + hh + 1)
                for h in (2 * hh, 2 * hh + 1):
                    mm = nc.tensor.matmul(bank[:, (h % 2) * DV:(h % 2 + 1) * DV], bc[0:w, h * DK:(h + 1) * DK],
                                          vtm[0:w, h * DV:(h + 1) * DV], start=True, stop=True)
                mm.then_inc(dS_mm, 1)

            def onorm_piece(n, w):
                pe.wait_ge(o_summed, n + 1)
                nc.tensor.matmul(hd(sb6, H, w), ones, squares(w)[:, :, 0], start=True, stop=True).then_inc(onorm_mm, 1)

            def zg_head():
                pe.wait_ge(lnr1_done, 3)
                pe.wait_ge(const_loaded, 16 * 5)
                pe.wait_ge(acc_free[0], 1)
                zg_piece(0, NMETA, 0)

            def zg_samples():
                pe.wait_ge(z_ready, 1)
                for h in range(H):
                    mm = nc.tensor.matmul(sb6[:, h * NS:(h + 1) * NS], wg[0:RANK, h * DK:(h + 1) * DK],
                                          glr[0:RANK, NT:C], start=True, stop=True)
                mm.then_inc(zg_mm, 1)

            def vT_samples(half):
                for e in range(4):
                    k = 4 * half + e
                    mm = nc.tensor.transpose(sb6[0:NS, e * P:(e + 1) * P], V[:, k * C + NT:k * C + NT + NS], ident)
                mm.then_inc(sT_mm, 1)

            unit(U_QKV + 8, nth(U_QKV + 8), 1, G_QKV[1] + 4, XH, XL, {1: [zg_head], 3: [zg_samples]})
            unit(U_QKV + 9, nth(U_QKV + 9), 0, G_QKV[0] + 4, XH, XL, {
                1: [lambda: keT_piece(0, NMETA)], 3: [lambda: A_piece(0, NMETA, z_ready, 2)]})
            with pe.Fori(5, 8) as i:
                unit(U_QKV, nth(U_QKV, 2, i), 1, G_QKV[1] + i, XH, XL)
                unit(U_QKV + 1, nth(U_QKV + 1, 2, i), 0, G_QKV[0] + i, XH, XL)
            pe.wait_ge(keT_ready, 1)
            vT_piece(0, NMETA, 0)
            pe.wait_ge(A_ready, 1)
            vT_samples(0)
            vT_piece(0, NMETA, 1)
            pe.wait_ge(sT_ready, 1)
            vT_samples(1)
            pe.wait_ge(vT_ready, 2)
            O_piece(sb7, NMETA, 0, False)
            pe.wait_ge(sT_ready, 2)
            O_piece(sb6, NMETA, 1, False)
            for hh, bank in ((0, sb7), (1, sb6)):
                dS_piece(bank, 0, NMETA, hh)
            pe.wait_ge(S_ready, 2)
            onorm_piece(0, NMETA)

            def smp_o(j):
                pe.wait_ge(sS_ready, j + 1)
                pe.wait_ge(vT_ready, 2 * (j + 1) + 2)
                for h in range(H):
                    for e in range(2):
                        mm = nc.tensor.matmul(sb7[:, 2 * h + e:2 * h + e + 1], sS[:, h * DV + e * P:h * DV + (e + 1) * P],
                                              sqk[:, bass.ds(h * NS + j, 1)], start=True, stop=True)
                mm.then_inc(so_mm, 1)

            def gate_product(g, n_grp, half):
                pe.wait_ge(acc_free[g], n_grp)
                for n in range(3):
                    mm = nc.tensor.matmul(accv[g][:, n], gw[:, half * P:(half + 1) * P], xc[:, n * NW:(n + 1) * NW],
                                          start=True, stop=True)
                mm.then_inc(gate_mm, 1)

            with pe.Fori(0, NPAIR) as j:
                n = j + 1
                zn = j + 2

                def zg_pair():
                    pe.wait_ge(ones_done, 1)
                    pe.wait_ge(olog_done, n)
                    for h in range(H):
                        mm = nc.tensor.matmul(sb6[:, h * PAIR:(h + 1) * PAIR], wg[0:RANK, h * DK:(h + 1) * DK],
                                              glr[0:RANK, bass.ds(NMETA + PAIR * j, PAIR)], start=True, stop=True)
                    mm.then_inc(zg_mm, 1)

                def O_pair(hh, bank):
                    if hh == 0:
                        pe.wait_ge(A_ready, n + 1)
                        pe.wait_ge(qs_ready, n)
                        pe.wait_ge(S_ready, 2 * n)
                    else:
                        pe.wait_ge(keT_ready, n + 1)
                    O_piece(bank, PAIR, hh, True)

                unit(U_RG, nth(U_RG, 2, j), 1, G_RG[1] + 2 * j, XH, XL, {
                    0: [lambda: vT_piece(n, PAIR, 0)], 2: [zg_pair], 3: [lambda: vT_piece(n, PAIR, 1)],
                    6: [lambda: smp_o(j)]})
                unit(U_RG + 1, nth(U_RG + 1, 2, j), 0, G_RG[0] + 2 * j, XH, XL, {
                    1: [lambda: keT_piece(n, PAIR, so_ready, j + 1), lambda: A_piece(n, PAIR, z_ready, zn + 1)],
                    3: [lambda: O_pair(0, sb6)], 4: [lambda: O_pair(1, sb7)],
                    6: [lambda: dS_piece(sb6, n, PAIR, 0)], 7: [lambda: dS_piece(sb7, n, PAIR, 1)]})
                pe.wait_ge(xc_step, 4 * j + 4)
                pe.wait_ge(gwt_loaded, 16 * j + 16)
                gate_product(1, G_RG[1] + 2 * j + 1, 0)
                pe.wait_ge(S_ready, 2 * n + 1)
                onorm_piece(n, PAIR)
                gate_product(0, G_RG[0] + 2 * j + 1, 1)

            def onorm_samples():
                pe.wait_ge(olog_done, NPAIR + 1)
                onorm_piece(NPAIR + 1, NS)

            unit(U_GO, nth(U_GO), 1, G_GO[1], XH, XL, {5: [onorm_samples]})
            unit(U_GO + 1, nth(U_GO + 1), 0, G_GO[0], XH, XL)
            with pe.Fori(1, KB // 2) as i:
                unit(U_GO, nth(U_GO, 2, i), 1, G_GO[1] + i, XH, XL)
                unit(U_GO + 1, nth(U_GO + 1, 2, i), 0, G_GO[0] + i, XH, XL)
            with pe.Fori(0, KB - 1) as j:
                unit(U_B, nth(U_B, 2, j), 1, G_B[1] + j, XH, XL)
                pe.wait_ge(obh_done, KB)
                pe.wait_ge(obl_done, KB)
                unit(U_B + 1, nth(U_B + 1, 2, j), 0, G_B[0] + j, OBH, OBL)
            j = KB - 1
            unit(U_B, nth(U_B, 2, j), 1, G_B[1] + j, XH, XL)
            unit(U_B + 1, nth(U_B + 1, 2, j), 0, G_B[0] + j, OBH, OBL, used=o_used)

            def h_gate(k):
                pe.wait_ge(hah_done, k + 1)
                pe.wait_ge(hal_done, k + 1)
            unit(U_A, nth(U_A), 1, G_A[1], XH, XL)
            unit(U_A + 1, nth(U_A + 1), 0, G_A[0], HAH, HAL, gate=h_gate)
            with pe.Fori(1, KB) as j:
                unit(U_A, nth(U_A, 2, j), 1, G_A[1] + j, XH, XL)
                unit(U_A + 1, nth(U_A + 1, 2, j), 0, G_A[0] + j, HAH, HAL)

            def mg_gate(k):
                pe.wait_ge(mgh_done, k + 1)
                pe.wait_ge(mgl_done, k + 1)
            unit(U_OUT, nth(U_OUT), 1, G_OUT[1], MGH, MGL, gate=mg_gate)
            unit(U_OUT + 1, nth(U_OUT + 1), 0, G_OUT[0], MGH, MGL)
            with pe.Fori(1, KB // 2) as i:
                unit(U_OUT, nth(U_OUT, 2, i), 1, G_OUT[1] + i, MGH, MGL)
                unit(U_OUT + 1, nth(U_OUT + 1, 2, i), 0, G_OUT[0] + i, MGH, MGL)
            def up(u0, per, i, grp0, gper, f0=0):
                for f in range(f0, GRP):
                    for c in range(2):
                        u = u0 + 2 * f + c
                        unit(u, nth(u, per, i), 1 - c, G_FFN[1 - c] + grp0 + f + gper * i, X2H, X2L)

            def down(u0, per, i, grp0, gper, half, n_act):
                pe.wait_ge(acth_done, n_act)
                pe.wait_ge(actl_done, n_act)
                for m in range(KB):
                    g = 1 - m % 2
                    pe.wait_ge(acc_free[g], G_FFN[g] + grp0 + m // 2 + gper * i)
                    for k in range(GRP):
                        t = m * GRP + k
                        u = u0 + t // KB
                        s = slot_of(u)
                        if t % KB == 0:
                            pe.wait_ge(w_split[s], nth(u, per, i) + 1)
                        b = (half * GRP + k) * C
                        mm = tile_products(s, t % KB, g, AH[:, b:b + C], AL[:, b:b + C], k == 0, k == GRP - 1)
                        if t % KB == KB - 1:
                            mm.then_inc(unit_done[s], 1)
                    if m < KB - 1:
                        mm.then_inc(down_mm, 1)

            def xn2_gate(k):
                pe.wait_ge(xh2_done, k + 1)
                pe.wait_ge(xl2_done, k + 1)
            NU, ND = 2 * GRP, GRP
            GU, GD = GRP, KB // 2

            def sums2():
                pe.wait_ge(sum2_done, KB)
                norm_sum(sqsum, 0, sb6, sum2_mm)
                norm_sum(sqsum, 1, sb7, sum2_mm)

            def last_sum2():
                pe.wait_ge(lnr2_done, 1)
                norm_sum(sqsum, 2, sb6, sum2_mm)
            unit(U_FFN, nth(U_FFN), 1, G_FFN[1], X2H, X2L, {6: [sums2]}, gate=xn2_gate)
            unit(U_FFN + 1, nth(U_FFN + 1), 0, G_FFN[0], X2H, X2L, {0: [last_sum2]})
            up(U_FFN, 0, 0, 0, 0, f0=1)
            per, gper = 2 * (NU + ND), 2 * (GU + GD)
            with pe.Fori(0, NGRP // 2 - 1) as i:
                up(U_FFN + NU, per, i, GU, gper)
                down(U_FFN + 2 * NU, per, i, 2 * GU, gper, 0, 2 * GRP * i + GRP)
                up(U_FFN + 2 * NU + ND, per, i, 2 * GU + GD, gper)
                down(U_FFN + 3 * NU + ND, per, i, 3 * GU + GD, gper, 1, 2 * GRP * i + 2 * GRP)
            n, gn = NGRP // 2 - 1, NGRP // 2 - 1
            u, g = U_FFN + NU + n * per, GU + gn * gper
            up(u, 0, 0, g, 0)
            down(u + NU, 0, 0, g + GU, 0, 0, GRP * (NGRP - 1))

            pe.wait_ge(acth_done, GRP * NGRP)
            pe.wait_ge(actl_done, GRP * NGRP)
            for v in range(GRP):
                pe.wait_ge(w_split[slot_of(U_LAST + v)], nth(U_LAST + v) + 1)
            pe.wait_ge(lnr2_done, 3)

            def final_sum(n):
                pe.wait_ge(sum3_done, KB * (n + 1))
                pe.wait_ge(last_added, KB * (n + 1))
                norm_sum(ysum, n, last_bank(KB - 1), sum3_mm)
            for n in range(3):
                for m in range(KB):
                    if n == 0 and m in (2, 5):
                        pe.wait_ge(acc_free[(m - 2) // 3], G_LAST[(m - 2) // 3])
                    if n > 0:
                        pe.wait_ge(last_added, KB * (n - 1) + m + 1)
                        if m == KB - 1:
                            pe.wait_ge(lnr3_done, n)
                    for k in range(GRP):
                        v, t = divmod(m * GRP + k, KB)
                        b = (GRP + k) * C + n * NW
                        for w, x, a, z in ((lhi, AH, k == 0, False), (lhi, AL, False, False), (llo, AH, False, k == GRP - 1)):
                            mm = nc.tensor.matmul(last_bank(m)[:, 0:NW], w[v][:, t * P:(t + 1) * P], x[:, b:b + NW],
                                                  start=a, stop=z)
                    mm.then_inc(last_mm, 1)
                    if n > 0 and m == 2:
                        final_sum(n - 1)
            final_sum(2)

        @block.scalar
        def _(act):
            def ready(u, per=0, i=0):
                act.wait_ge(unit_done[slot_of(u)], nth(u, per, i) + 1)

            def plain():
                act.wait_ge(ones_done, 1)

            for k in range(0, KB, 2):
                act.dma_start(blk(X1, k), I["x"][k]).then_inc(x_loaded[k], 16)

            def norm_factor(mm_sem, ln_sem, r_sem):
                for n, bank in enumerate((sb6, sb7, sb6)):
                    act.wait_ge(mm_sem, n + 1)
                    nc.scalar.activation(rms[:, n * NW:(n + 1) * NW], bank[:, 0:NW], ACT.Ln, scale=1.0 / D, bias=cst[:, 0:1])\
                        .then_inc(ln_sem, 1)
                act.wait_ge(ln_sem, 3)
                nc.scalar.activation(rms, rms, ACT.Exp, scale=-0.5).then_inc(r_sem, 1)

            act.preload_act_table_set(LN_EXP)
            act.wait_ge(w_loaded[0], 16)
            nc.scalar.activation(whi[0], raw[0], ACT.Copy).then_inc(w_hi_done[0], 1)
            act.wait_ge(prm_loaded, 16)
            for k in range(KB):
                act.wait_ge(x_loaded[k], 16)
                nc.scalar.activation(blk(XH, k), blk(X1, k), ACT.Identity, scale=par("g1", k)).then_inc(xh1_done, 1)
                if k >= 2:
                    act.wait_ge(sum1_done, k - 1)
                nc.scalar.activation((rt, it)[k % 2], blk(X1, k), ACT.Square).then_inc(sq1_done, 1)
            act.wait_ge(ones_done, 1)
            norm_factor(sum1_mm, lnr1_done, r1_done)

            lam = prm[:, RP["lam"]:RP["lam"] + KB]
            nc.scalar.activation(der[:, 0:KB], lam, ACT.Abs).then_inc(set_a, 1)
            act.wait_ge(set_a, 1)
            nc.scalar.activation(der[:, 0:KB], der[:, 0:KB], ACT.Exp, scale=-1.0).then_inc(set_a, 1)
            act.wait_ge(set_a, 2)
            nc.scalar.activation(der[:, 0:KB], der[:, 0:KB], ACT.Ln, bias=1.0).then_inc(set_a, 1)

            with act.Fori(0, 4) as i:
                for s, g in ((0, 1), (1, 0)):
                    act.wait_ge(acc_free[g], G_QKV[g] + i + 1)
                    act.dma_start(qk_scr[2 * i + s], (rt, it)[s]).then_inc(qk_stored[s], 16)

            def load_qk(w, c0):
                act.dma_start(hd(qkp, 8, w), qk_scr[:, :, bass.ds(c0, w)].rearrange("k p c -> p k c")).then_inc(qk_loaded, 16)

            def v_copy(n, w, c0, n_k):
                plain()
                act.wait_ge(vT_mm, 2 * n)
                act.wait_ge(A_mm, n_k)
                act.wait_ge(keT_mm, n_k)
                nc.scalar.activation(hd(kk, 8, w), V3[:, :, bass.ds(c0, w)], ACT.Copy).then_inc(vcp_ready, 1)

            def log_gate(nz, z, g, between=None):
                act.wait_ge(z_ready, nz + 1)
                nc.scalar.activation(g, z, ACT.Abs).then_inc(absz_done, 1)
                act.wait_ge(absz_done, nz + 1)
                nc.scalar.activation(g, g, ACT.Exp, scale=-1.0).then_inc(expz_done, 1)
                if between:
                    between()
                act.wait_ge(expz_done, nz + 1)
                nc.scalar.activation(g, g, ACT.Ln, bias=1.0).then_inc(lnz_done, 1)

            def v_tokens(n, w, half):
                act.wait_ge(vT_mm, 2 * n + half + 1)
                act.wait_ge(dS_mm, 2 * n)
                nc.scalar.activation(vtm[0:w, half * 512:(half + 1) * 512], sb7[0:w, :], ACT.Copy).then_inc(vT_ready, 1)

            def decays(n, w):
                act.wait_ge(bc_ready, n + 1)
                nc.scalar.activation(eb[:, 0:4 * w], bc[:, 0:4 * w], ACT.Exp, scale=1.0 / 16).then_inc(eb_ready, 1)
                act.wait_ge(bl_ready, n + 1)
                nc.scalar.activation(z_t[:, 0:4 * w], z_t[:, 0:4 * w], ACT.Exp, scale=1.0 / 16).then_inc(eke_ready, 1)
                act.wait_ge(bm_ready, n + 1)
                nc.scalar.activation(qd[:, 0:4 * w], g_t[:, 0:4 * w], ACT.Exp, scale=1.0 / 16).then_inc(em_ready, 1)
                act.wait_ge(em_ready, n + 1)
                nc.scalar.activation(g_t[:, 0:4 * w], g_t[:, 0:4 * w], ACT.Exp, scale=-1.0 / 16).then_inc(enm_ready, 1)

            def ke_tokens(n, w):
                act.wait_ge(keT_mm, n + 1)
                nc.scalar.activation(bc[0:w, :], sb7[0:w, :], ACT.Copy).then_inc(keT_ready, 1)

            def o_square(n, w, c0, hh):
                plain()
                act.wait_ge(o_copied, 2 * n + hh + 1)
                nc.scalar.activation(zg[:, 4 * w * hh:4 * w * (hh + 1)].rearrange("p (k t) -> p k t", k=4),
                                     V3[:, 4 * hh:4 * hh + 4, bass.ds(c0, w)], ACT.Square).then_inc(o_squared, 1)

            def o_rms(nn, out, w, between=None):
                act.wait_ge(onorm_mm, nn + 1)
                nc.scalar.activation(out, sb6[:, 0:4 * w], ACT.Ln, scale=1.0 / DV, bias=cst[:, 0:1]).then_inc(olog_done, 1)
                if between:
                    between()
                act.wait_ge(olog_done, nn + 1)
                nc.scalar.activation(out, out, ACT.Exp, scale=-0.5).then_inc(orinv_ready, 1)

            for s in range(2):
                act.wait_ge(qk_stored[s], 64)
            act.wait_ge(set_v, 12)
            load_qk(NMETA, 0)
            act.dma_start(hd(sqk, 8, NS), qk_scr[:, :, NT:C].rearrange("k p c -> p k c")).then_inc(sqk_loaded, 16)
            act.preload_act_table_set(LN_EXP)
            log_gate(0, z_t[:, 0:4 * NMETA], g_t[:, 0:4 * NMETA])
            decays(0, NMETA)
            log_gate(1, sdec, srv)
            act.wait_ge(sg_ready, 1)
            nc.scalar.activation(sdec, sdec, ACT.Exp, scale=1.0 / 16).then_inc(s_act, 1)

            def sample_tokens(q, t, bank):
                act.wait_ge(sT_mm, q + 1)
                nc.scalar.activation(t, bank[0:NS, :], ACT.Copy).then_inc(sT_ready, 1)

            ke_tokens(0, NMETA)
            for used in (qd_ready, kd_ready, ke_ready):
                act.wait_ge(used, 1)
            load_qk(PAIR, NMETA)
            act.wait_ge(acc_free[0], G_RG[0])
            act.wait_ge(acc_free[1], G_RG[1])
            v_copy(0, NMETA, 0, 1)
            v_tokens(0, NMETA, 0)
            sample_tokens(0, svt[0:NS, 0:512], sb6)
            v_tokens(0, NMETA, 1)
            sample_tokens(1, svt[0:NS, 512:1024], sb6)
            act.wait_ge(sT_ready, 2)
            act.dma_start(sv_scr, svt[0:NB, :]).then_inc(sv_stored, 16)
            v_copy(1, PAIR, NMETA, 1)
            o_square(0, NMETA, 0, 0)
            o_square(0, NMETA, 0, 1)
            o_rms(0, qd[:, 0:4 * NMETA], NMETA)
            v_tokens(1, PAIR, 0)

            def load_sample_v(j):
                act.dma_start(svb, sv_scr[bass.ds(j, 1)].broadcast_to([P, D])).then_inc(svb_loaded, 16)
            act.wait_ge(sv_stored, 16)
            load_sample_v(0)

            def rg_tail_exps(m):
                plain()
                nc.scalar.activation(av, rt, ACT.Exp, scale=col(der, m + 2 * KB), bias=col(der, m + 2 * KB)).then_inc(a_ready, 1)
                nc.scalar.activation(rt, rt, ACT.Exp, scale=col(der, m + 3 * KB), bias=col(der, m + 3 * KB)).then_inc(a2_ready, 1)

            def rg_tail_mult(m):
                act.wait_ge(w_ready, m + 1)
                nc.scalar.activation(th, th, ACT.Ln, bias=cst[:, 1:2]).then_inc(ml_done, 1)
                act.wait_ge(ml_done, m + 1)
                nc.scalar.activation(th, th, ACT.Exp, scale=0.5).then_inc(m_ready, 1)

            def rg_prefetch(j):
                act.wait_ge(qs_ready, j + 1)
                for used in (qd_ready, kd_ready, ke_ready):
                    act.wait_ge(used, j + 2)
                load_qk(PAIR, NMETA + PAIR * (j + 1))
                load_sample_v(j + 1)
                act.wait_ge(sS_stored, 16 * j + 16)
                act.wait_ge(so_mm, j + 1)
                act.dma_start(sS, I["gla_state"][j + 1]).then_inc(sS_loaded, 16)

            def rg_body(j, first, last):
                n = j + 1
                if not first:
                    rg_tail_exps(j - 1)
                log_gate(j + 2, z_t, g_t, lambda: v_tokens(n, PAIR, 1))
                if not first:
                    rg_tail_mult(j - 1)
                decays(n, PAIR)
                if not first:
                    act.wait_ge(ha_ready, j)
                    act.dma_start(ha_scr[j - 1], gy).then_inc(ha_stored, 16)
                ke_tokens(n, PAIR)
                if not last:
                    v_copy(n + 1, PAIR, NMETA + PAIR * (j + 1), n + 1)
                plain()
                act.wait_ge(acc_free[1], G_RG[1] + 2 * j + 1)
                act.wait_ge(ha_ready, j)
                nc.scalar.activation(xc, ext[:, 3:3 + C], ACT.Identity, scale=par("w3", j), bias=par("b", j))\
                    .then_inc(xbias_ready, 1)
                act.wait_ge(sS_ready, j + 1)
                act.dma_start(O["gla_sample"][j], sS).then_inc(sS_stored, 16)
                if not last:
                    rg_prefetch(j)
                o_square(n, PAIR, NMETA + PAIR * j, 0)
                o_square(n, PAIR, NMETA + PAIR * j, 1)
                act.wait_ge(acc_free[0], G_RG[0] + 2 * j + 1)
                nc.scalar.activation(gy, gy, ACT.Gelu_apprx_tanh).then_inc(gelu_ready, 1)
                plain()
                act.wait_ge(gate_mm, 2 * j + 1)
                nc.scalar.activation(view3(rt), accv[1], ACT.Tanh, scale=0.5, bias=col(der, j)).then_inc(acc_free[1], 1)
                plain()
                act.wait_ge(acc_free[1], G_RG[1] + 2 * j + 2)
                act.wait_ge(b_ready, j)
                nc.scalar.activation(th, rt, ACT.Tanh, scale=col(der, j + 4 * KB), bias=col(der, j + 4 * KB)).then_inc(th_ready, 1)
                plain()
                act.wait_ge(gate_mm, 2 * j + 2)
                act.wait_ge(h_step, 4 * j)
                nc.scalar.activation(view3(it), accv[0], ACT.Tanh, scale=0.5, bias=col(der, j + KB)).then_inc(acc_free[0], 1)
                act.preload_act_table_set(LN_EXP)
                o_rms(n, qd, PAIR, None if last else lambda: v_tokens(n + 1, PAIR, 0))

            def gate_weights(j):
                act.dma_start(gw, I["rg_gates"][j + 1]).then_inc(gwt_loaded, 16)

            rg_body(0, True, False)
            gate_weights(0)
            with act.Fori(1, NPAIR - 1) as j:
                rg_body(j, False, False)
                gate_weights(j)
            rg_body(NPAIR - 1, False, True)
            act.wait_ge(so_ready, NB)
            act.wait_ge(onorm_mm, NPAIR + 1)
            nc.scalar.activation(hd(zg, 8, NS), V3[:, :, NT:C], ACT.Square).then_inc(s_act, 2)
            rg_tail_exps(NPAIR - 1)
            o_rms(NPAIR + 1, srv, NS)
            rg_tail_mult(NPAIR - 1)
            act.wait_ge(ha_ready, NPAIR)
            act.dma_start(ha_scr[NPAIR - 1], gy).then_inc(ha_stored, 16)
            act.dma_start(O["gla_prompt"], S[:, 0:H * DV]).then_inc(stored, 16)
            act.wait_ge(h_step, 4 * NPAIR)
            act.wait_ge(sS_stored, 16 * NB)
            act.wait_ge(o_ready, NPAIR + 2)

            def gate_o(i):
                for s, g in ((0, 1), (1, 0)):
                    act.wait_ge(acc_free[g], G_GO[g] + i + 1)
                    nc.scalar.activation(T[s], T[s], ACT.Silu).then_inc(silu_done, 1)
                    plain()
                    act.wait_ge(og_done, 2 * i + s + 1)
                    nc.scalar.activation(blk(OBH, 2 * i + s), T[s], ACT.Copy).then_inc(obh_done, 1)
            gate_o(0)
            act.wait_ge(ha_stored, 16 * NPAIR)
            act.wait_ge(stored, 48)
            with act.Fori(1, KB // 2) as i:
                gate_o(i)
            with act.Fori(0, KB) as j:
                act.wait_ge(acc_free[1], G_B[1] + j + 1)
                nc.scalar.activation(T[2], T[2], ACT.Tanh, scale=0.5).then_inc(tanh_done, 1)
            for k in range(KB):
                if k < KB - 1:
                    act.wait_ge(o_used, k + 1)
                else:
                    ready(U_A - 1)
                act.dma_start(blk(HA, k), ha_scr[k]).then_inc(hl_loaded[k], 16)
            for k in range(KB):
                act.wait_ge(hl_loaded[k], 16)
                nc.scalar.activation(blk(HAH, k), blk(HA, k), ACT.Copy).then_inc(hah_done, 1)
            with act.Fori(0, KB) as j:
                act.wait_ge(acc_free[1], G_A[1] + j + 1)
                nc.scalar.activation(T[2], T[2], ACT.Tanh, scale=0.5).then_inc(tanh_done, 1)
            act.wait_ge(acc_free[1], G_OUT[1])
            for k in range(KB):
                if k == KB - 1:
                    ready(U_OUT - 1)
                    for m in range(KB):
                        act.dma_start(blk(X2, m), I["x"][m]).then_inc(xr_loaded[m], 16)
                act.wait_ge(ma_done, KB if k == KB - 1 else k + 1)
                nc.scalar.activation(blk(MGH, k), blk(MG, k), ACT.Copy, scale=0.5).then_inc(mgh_done, 1)
            for k in range(KB):
                act.wait_ge(acc_free[1 - k % 2], G_OUT[1 - k % 2] + k // 2 + 1)
                nc.scalar.activation(blk(X2H, k), blk(X2, k), ACT.Identity, scale=par("g2", k)).then_inc(xh2_done, 1)
                if k >= 2:
                    act.wait_ge(sum2_done, k - 1)
                nc.scalar.activation(T[k % 2], blk(X2, k), ACT.Square).then_inc(sq2_done, 1)
            act.dma_start(fst, I["ffn_states"]).then_inc(fst_loaded, 16)
            act.dma_start(fpr, I["ffn_params"]).then_inc(fst_loaded, 16)
            act.preload_act_table_set(LN_EXP)
            norm_factor(sum2_mm, lnr2_done, r2_done)

            def ffn_block(F, grp):
                plain()
                act.wait_ge(acc_free[1], G_FFN[1] + grp + 1)
                act.wait_ge(act_done, F)
                nc.scalar.activation(cg, eg[:, 2:2 + C], ACT.Identity, scale=fpr[:, bass.ds(2 * UB + F, 1)],
                                     bias=fpr[:, bass.ds(3 * UB + F, 1)]).then_inc(gbias_ready, 1)
                act.wait_ge(gconv_step, 3 * F + 3)
                nc.scalar.activation(cg, cg, ACT.Gelu_apprx_tanh).then_inc(ggelu_done, 1)
                plain()
                act.wait_ge(acc_free[0], G_FFN[0] + grp + 1)
                nc.scalar.activation(cv, ev[:, 2:2 + C], ACT.Identity, scale=fpr[:, bass.ds(2 * UB + FB + F, 1)],
                                     bias=fpr[:, bass.ds(3 * UB + FB + F, 1)]).then_inc(vbias_ready, 1)
                act.wait_ge(act_done, F + 1)

            def ffn_hi(half, f):
                b = (half * GRP + f) * C
                nc.scalar.activation(AH[:, b:b + C], act_t, ACT.Copy).then_inc(acth_done, 1)

            GU, GD = GRP, KB // 2

            def ffn_group(F0_, grp, half):
                for f in range(GRP):
                    ffn_block(F0_ + f, grp + f)
                    ffn_hi(half, f)

            act.wait_ge(set_f, 4)
            ffn_group(0, 0, 0)
            gper = 2 * (GU + GD)
            with act.Fori(0, NGRP // 2 - 1) as i:
                ffn_group(2 * GRP * i + GRP, GU + gper * i, 1)
                act.wait_ge(acc_free[0], G_FFN[0] + 2 * GU + GD + gper * i)
                ffn_group(2 * GRP * i + 2 * GRP, 2 * GU + GD + gper * i, 0)
                act.wait_ge(acc_free[0], G_FFN[0] + 3 * GU + 2 * GD + gper * i)
            n = NGRP // 2 - 1
            ffn_group(GRP * (NGRP - 1), GU + gper * n, 1)
            act.preload_act_table_set(LN_EXP)

            def final_factor(n):
                c = slice(n * NW, (n + 1) * NW)
                act.wait_ge(sum3_mm, n + 1)
                nc.scalar.activation(yrs[:, c], last_bank(KB - 1)[:, 0:NW], ACT.Ln, scale=1.0 / D, bias=cst[:, 0:1])\
                    .then_inc(lnr3_done, 1)
                act.wait_ge(lnr3_done, n + 1)
                nc.scalar.activation(yrs[:, c], yrs[:, c], ACT.Exp, scale=-0.5).then_inc(r3_done, 1)
            for n in range(3):
                c = slice(n * NW, (n + 1) * NW)
                for m in range(KB):
                    t = KB * n + m
                    act.wait_ge(last_added, t + 1)
                    if t >= 2:
                        act.wait_ge(sum3_done, t - 1)
                    nc.scalar.activation(ysq[:, t % 2 * NW:(t % 2 + 1) * NW], blk(X2, m)[:, c], ACT.Square).then_inc(sq3_done, 1)
                    nc.scalar.activation(blk(Y, m)[:, c], blk(X2, m)[:, c], ACT.Identity, scale=par("gf", m)).then_inc(yg_done, 1)
                    if n > 0 and m == 2:
                        final_factor(n - 1)
            final_factor(2)

        @block.vector
        def _(dve):
            nc.vector.memset(ones, 1.0)
            nc.vector.memset(cst[:, 0:1], EPS)
            nc.vector.memset(ext[:, 0:3], 0.0)
            nc.vector.memset(am, 0.0)
            nc.vector.memset(cst[:, 1:2], TINY).then_inc(ones_done, 1)
            def plain():
                dve.wait_ge(ones_done, 1)

            dve.wait_ge(w_hi_done[0], 1)
            nc.vector.tensor_tensor(wlo[0], raw[0], whi[0].bitcast(F32), ALU.subtract).then_inc(w_split[0], 1)
            dve.wait_ge(prm_loaded, 16)
            for k in range(KB):
                dve.wait_ge(xh1_done, k + 1)
                nc.vector.scalar_tensor_tensor(blk(XL, k), blk(X1, k), par("g1", k), blk(XH, k).bitcast(F32),
                                               ALU.mult, ALU.subtract).then_inc(xl1_done, 1)
                dve.wait_ge(sq1_done, k + 1)
                if k == 0:
                    nc.vector.tensor_copy(xc, rt).then_inc(sum1_done, 1)
                else:
                    dve.wait_ge(sum1_done, k)
                    nc.vector.tensor_tensor(xc, xc, (rt, it)[k % 2], ALU.add).then_inc(sum1_done, 1)

            def evacuate(u, per, i, g, out, n_part=P):
                dve.wait_ge(unit_done[slot_of(u)], nth(u, per, i) + 1)
                nc.vector.tensor_tensor(view3(out), acc[g][0:n_part, :, 0:NW], view3(rms[0:n_part, :]), ALU.mult)\
                    .then_inc(acc_free[g], 1)

            dve.wait_ge(r1_done, 1)
            evacuate(0, 0, 0, 0, glr[0:RANK, :], RANK)
            dve.wait_ge(sum1_done, KB)

            def stage_qk(i):
                for s, g in ((0, 1), (1, 0)):
                    if not isinstance(i, int):
                        dve.wait_ge(qk_stored[s], 16 * i)
                    evacuate(U_QKV + s, 2, i, g, (rt, it)[s])
            stage_qk(0)

            dve.wait_ge(par_loaded, 48)
            steps = [0]

            def step(ins):
                steps[0] += 1
                ins.then_inc(set_v, 1)
                dve.wait_ge(set_v, steps[0])

            st = rgst.rearrange("p (r k b) -> p r k b", r=3, k=KB)

            def wide(name):
                return prm[:, RP[name]:RP[name] + KB].unsqueeze(2).broadcast_to([P, KB, NS])
            pk, tk = hd(rgp, KB, NS), hd(rgtmp, KB, NS)
            step(nc.vector.tensor_tensor(pk, st[:, 0], wide("w0"), ALU.mult))
            for r in (1, 2):
                step(nc.vector.tensor_tensor(tk, st[:, r], wide(f"w{r}"), ALU.mult))
                step(nc.vector.tensor_tensor(pk, pk, tk, ALU.add))
            step(nc.vector.tensor_tensor(pk, pk, wide("b"), ALU.add))
            dve.wait_ge(set_a, 3)
            d = [der[:, i * KB:(i + 1) * KB] for i in range(5)]
            lam = prm[:, RP["lam"]:RP["lam"] + KB]
            step(nc.vector.tensor_scalar(d[1], lam, -1.0, 0.0, ALU.mult, ALU.max))
            step(nc.vector.tensor_tensor(d[4], d[0], d[1], ALU.add))
            step(nc.vector.tensor_scalar(d[2], d[4], -4.0, None, ALU.mult))
            step(nc.vector.tensor_scalar(d[3], d[4], -8.0, None, ALU.mult))
            step(nc.vector.tensor_scalar(d[4], d[4], 4.0, None, ALU.mult))
            step(nc.vector.tensor_scalar(d[0], prm[:, RP["ba"]:RP["ba"] + KB], 0.5, None, ALU.mult))
            step(nc.vector.tensor_scalar(d[1], prm[:, RP["bx"]:RP["bx"] + KB], 0.5, None, ALU.mult))

            with dve.Fori(1, 4) as i:
                stage_qk(i)

            def logits(nz, w, z):
                dve.wait_ge(zg_mm, nz + 1)
                nc.vector.tensor_tensor(hd(z, H, w), hd(sb6, H, w), gbz.unsqueeze(2).broadcast_to([P, H, w]), ALU.add)\
                    .then_inc(z_ready, 1)

            def log_sigmoid(nz, z, g, out):
                dve.wait_ge(lnz_done, nz + 1)
                return nc.vector.scalar_tensor_tensor(out, z, 0.0, g, ALU.min, ALU.subtract)

            def running_sum(n, w, reset_t):
                log_sigmoid(n if isinstance(n, int) and n == 0 else n + 1, z_t[:, 0:4 * w], g_t[:, 0:4 * w],
                            g_t[:, 0:4 * w]).then_inc(g_ready, 1)
                dve.wait_ge(g_ready, n + 1)
                dve.wait_ge(dS_mm, 2 * n)
                nc.vector.tensor_tensor_scan(bc[:, 0:4 * w], reset_t, g_t[:, 0:4 * w], 0.0, ALU.mult, ALU.add)\
                    .then_inc(bc_ready, 1)
                dve.wait_ge(bc_ready, n + 1)
                b, z, g = hd(bc, H, w), hd(z_t, H, w), hd(g_t, H, w)
                nc.vector.tensor_tensor(z, b[:, :, w - 1:w].broadcast_to([P, H, w]), b, ALU.subtract).then_inc(bl_ready, 1)
                nc.vector.tensor_tensor(g, b, b[:, :, w // 2 - 1:w // 2].broadcast_to([P, H, w]), ALU.subtract)\
                    .then_inc(bm_ready, 1)

            def scaled_qk(n, w, inter=True):
                dve.wait_ge(qk_loaded, 16 * n + 16)
                if inter:
                    dve.wait_ge(eb_ready, n + 1)
                    nc.vector.scalar_tensor_tensor(qs[:, 0:4 * w], qkp[:, 0:4 * w], DK ** -0.5, eb[:, 0:4 * w],
                                                   ALU.mult, ALU.mult).then_inc(qs_ready, 1)
                    dve.wait_ge(vT_mm, 2 * n + 2)
                dve.wait_ge(eke_ready, n + 1)
                nc.vector.tensor_tensor(ke[:, 0:4 * w], qkp[:, 4 * w:8 * w], z_t[:, 0:4 * w], ALU.mult).then_inc(ke_ready, 1)
                dve.wait_ge(em_ready, n + 1)
                nc.vector.scalar_tensor_tensor(qd[:, 0:4 * w], qkp[:, 0:4 * w], DK ** -0.5, qd[:, 0:4 * w],
                                               ALU.mult, ALU.mult).then_inc(qd_ready, 1)
                dve.wait_ge(enm_ready, n + 1)
                nc.vector.tensor_tensor(kd[:, 0:4 * w], qkp[:, 4 * w:8 * w], g_t[:, 0:4 * w], ALU.mult).then_inc(kd_ready, 1)

            def scores(n, w):
                dve.wait_ge(const_loaded, 16 * 5)
                dve.wait_ge(A_mm, n + 1)
                nc.vector.copy_predicated(hd(am[0:w], H, w), mask[0:w, 0:w].unsqueeze(1).broadcast_to([w, H, w]),
                                          hd(sb6[0:w], H, w)).then_inc(A_ready, 1)

            def o_copy(n, w, c0, hh, bank):
                plain()
                dve.wait_ge(O_mm, 2 * n + hh + 1)
                nc.vector.tensor_copy(V3[:, 4 * hh:4 * hh + 4, bass.ds(c0, w)], hd(bank, 4, w)).then_inc(o_copied, 1)

            def state(n, w, hh, bank):
                dve.wait_ge(dS_mm, 2 * n + hh + 1)
                for h in (2 * hh, 2 * hh + 1):
                    t = S[:, h * DV:(h + 1) * DV]
                    ins = nc.vector.scalar_tensor_tensor(t, t, eb[:, (h + 1) * w - 1:(h + 1) * w],
                                                         bank[:, (h % 2) * DV:(h % 2 + 1) * DV], ALU.mult, ALU.add)
                ins.then_inc(S_ready, 1)

            def sum_halves(n, w):
                q = squares(w)
                nc.vector.tensor_tensor(q[:, :, 0], q[:, :, 0], q[:, :, 1], ALU.add).then_inc(o_summed, 1)

            def o_scale(n, w, c0, rinv):
                dve.wait_ge(orinv_ready, n + 1)
                dve.wait_ge(o_copied, 2 * n + 2)
                o = V3[:, :, bass.ds(c0, w)].rearrange("p (h e) t -> p h e t", h=H)
                r = hd(rinv, H, w).unsqueeze(2).broadcast_to([P, H, 2, w])
                nc.vector.tensor_tensor(o, o, r, ALU.mult).then_inc(o_ready, 1)

            dve.wait_ge(const_loaded, 16 * 5)
            logits(0, NMETA, z_t)
            running_sum(0, NMETA, rs16)
            logits(1, NS, sdec)
            scaled_qk(0, NMETA, False)
            log_sigmoid(1, sdec, srv, sdec).then_inc(sg_ready, 1)
            dve.wait_ge(sqk_loaded, 16)
            nc.vector.tensor_scalar(sqk[:, 0:H * NS], sqk[:, 0:H * NS], DK ** -0.5, None, ALU.mult).then_inc(sg_ready, 1)
            dve.wait_ge(xl1_done, KB)
            evacuate(U_QKV + 8, 0, 0, 1, blk(V, 0))
            scores(0, NMETA)
            evacuate(U_QKV + 9, 0, 0, 0, blk(V, 1))
            with dve.Fori(1, 4) as i:
                evacuate(U_QKV + 8, 2, i, 1, blk(V, 2 * i))
                evacuate(U_QKV + 9, 2, i, 0, blk(V, 2 * i + 1))
            o_copy(0, NMETA, 0, 0, sb7)
            o_copy(0, NMETA, 0, 1, sb6)
            for hh, bank in ((0, sb7), (1, sb6)):
                dve.wait_ge(dS_mm, hh + 1)
                nc.vector.tensor_copy(S[:, hh * 2 * DV:(hh + 1) * 2 * DV], bank[:, :]).then_inc(S_ready, 1)
            dve.wait_ge(o_squared, 2)
            sum_halves(0, NMETA)
            o_scale(0, NMETA, 0, qd)
            def sample_state(j):
                dve.wait_ge(sS_loaded, 16 * j + 16)
                heads = [sS[:, h * DV:(h + 1) * DV] for h in range(H)]
                for h, t in enumerate(heads):
                    ins = nc.vector.tensor_scalar(t, t, sdec[:, bass.ds(h * NS + j, 1)], None, ALU.mult)
                ins.then_inc(sS_decayed, 1)
                dve.wait_ge(svb_loaded, 16 * j + 16)
                dve.wait_ge(sS_decayed, j + 1)
                for h, t in enumerate(heads):
                    ins = nc.vector.scalar_tensor_tensor(t, svb[:, h * DV:(h + 1) * DV], sqk[:, bass.ds((H + h) * NS + j, 1)], t,
                                                         ALU.mult, ALU.add)
                ins.then_inc(sS_ready, 1)

            def rg_tail_w(m):
                dve.wait_ge(acc_free[0], G_RG[0] + 2 * m + 2)
                nc.vector.scalar_tensor_tensor(it, it, 1.0, xc, ALU.add, ALU.mult).then_inc(ix_ready, 1)
                dve.wait_ge(a2_ready, m + 1)
                dve.wait_ge(th_ready, m + 1)
                nc.vector.scalar_tensor_tensor(th, rt, 1.0, th, ALU.add, ALU.mult).then_inc(w_ready, 1)

            def rg_tail_b(m):
                dve.wait_ge(m_ready, m + 1)
                dve.wait_ge(ix_ready, m + 1)
                nc.vector.scalar_tensor_tensor(it, it, 0.5, th, ALU.mult, ALU.mult).then_inc(b_ready, 1)

            def rg_tail_h(m):
                dve.wait_ge(a_ready, m + 1)
                dve.wait_ge(b_ready, m + 1)
                nc.vector.tensor_tensor(xc[:, NT:C], av[:, NT:C], col(h0, m, NS, NS), ALU.mult).then_inc(h_step, 1)
                nc.vector.tensor_tensor_scan(xc[:, 0:NT], av[:, 0:NT], it[:, 0:NT], 0.0, ALU.mult, ALU.add).then_inc(h_step, 1)
                dve.wait_ge(h_step, 4 * m + 1)
                nc.vector.tensor_tensor(xc[:, NT:C], xc[:, NT:C], it[:, NT:C], ALU.add).then_inc(h_step, 1)
                plain()
                dve.wait_ge(h_step, 4 * m + 3)
                nc.vector.tensor_copy(col(hco, m, HW, HW), xc[:, NT - 1:C]).then_inc(h_step, 1)
                dve.wait_ge(gelu_ready, m + 1)
                nc.vector.tensor_tensor(gy, xc, gy, ALU.mult).then_inc(ha_ready, 1)

            def rg_body(j, first):
                n = j + 1
                sample_state(j)
                if not first:
                    o_scale(n - 1, PAIR, NMETA + PAIR * (j - 1), qd)
                logits(j + 2, PAIR, z_t)
                if not first:
                    rg_tail_w(j - 1)
                running_sum(n, PAIR, reset)
                if not first:
                    rg_tail_b(j - 1)
                scaled_qk(n, PAIR)
                plain()
                dve.wait_ge(so_mm, j + 1)
                nc.vector.tensor_copy(V3[:, :, bass.ds(NT + j, 1)], hd(sb7, 8, 1)).then_inc(so_ready, 1)
                if not first:
                    rg_tail_h(j - 1)
                    dve.wait_ge(xc_step, 4 * j)
                    dve.wait_ge(rgo_kept, j)
                    dve.wait_ge(xbias_ready, j)
                evacuate(U_RG, 2, j, 1, ext[:, 3:3 + C])
                scores(n, PAIR)
                c0 = NMETA + PAIR * j
                dve.wait_ge(xbias_ready, j + 1)
                dve.wait_ge(acc_free[1], G_RG[1] + 2 * j + 1)
                for t in range(3):
                    dve.wait_ge(xc_step, 4 * j + t)
                    nc.vector.scalar_tensor_tensor(xc[:, 0:NT], ext[:, t:t + NT], par(f"w{t}", j), xc[:, 0:NT],
                                                   ALU.mult, ALU.add).then_inc(xc_step, 1)
                nc.vector.scalar_tensor_tensor(xc[:, NT:C], ext[:, NT + 3:C + 3], par("w3", j), col(rgp, j, NS, NS),
                                               ALU.mult, ALU.add).then_inc(xc_step, 1)
                nc.vector.tensor_copy(col(rgo, j, RGW, RGW), ext[:, C + 3 - RGW:C + 3]).then_inc(rgo_kept, 1)
                o_copy(n, PAIR, c0, 0, sb6)
                o_copy(n, PAIR, c0, 1, sb7)
                state(n, PAIR, 0, sb6)
                dve.wait_ge(o_squared, 2 * n + 2)
                sum_halves(n, PAIR)
                if not first:
                    dve.wait_ge(ha_stored, 16 * j)
                evacuate(U_RG + 1, 2, j, 0, gy)
                state(n, PAIR, 1, sb7)

            dve.wait_ge(s_act, 1)
            dve.wait_ge(sg_ready, 2)
            dve.wait_ge(set_v, steps[0])
            rg_body(0, True)
            with dve.Fori(1, NPAIR) as j:
                rg_body(j, False)
            o_scale(NPAIR, PAIR, NMETA + PAIR * (NPAIR - 1), qd)
            dve.wait_ge(s_act, 3)
            sum_halves(NPAIR + 1, NS)
            rg_tail_w(NPAIR - 1)
            rg_tail_b(NPAIR - 1)
            rg_tail_h(NPAIR - 1)
            dve.wait_ge(orinv_ready, NPAIR + 2)
            dve.wait_ge(so_ready, NB)
            o = V3[:, :, NT:C].rearrange("p (h e) t -> p h e t", h=H)
            nc.vector.tensor_tensor(o, o, hd(srv, H, NS).unsqueeze(2).broadcast_to([P, H, 2, NS]), ALU.mult).then_inc(o_ready, 1)
            dve.wait_ge(o_ready, NPAIR + 2)

            dve.wait_ge(sS_stored, 16 * NB)
            dve.wait_ge(gate_mm, 2 * NPAIR)

            def gate_o(i):
                for s, g in ((0, 1), (1, 0)):
                    k = 2 * i + s
                    if not isinstance(i, int):
                        dve.wait_ge(obl_done, k - 1)
                    evacuate(U_GO + s, 2, i, g, T[s])
                    dve.wait_ge(silu_done, k + 1)
                    nc.vector.scalar_tensor_tensor(T[s], blk(V, k), par("gn", k), T[s], ALU.mult, ALU.mult).then_inc(og_done, 1)
                    dve.wait_ge(obh_done, k + 1)
                    nc.vector.tensor_tensor(blk(OBL, k), T[s], blk(OBH, k).bitcast(F32), ALU.subtract).then_inc(obl_done, 1)
            gate_o(0)
            with dve.Fori(1, KB // 2) as i:
                gate_o(i)
            with dve.Fori(0, KB) as j:
                dve.wait_ge(acc_free[0], G_B[0] + j)
                evacuate(U_B, 2, j, 1, T[2])
                dve.wait_ge(tanh_done, j + 1)
                dve.wait_ge(unit_done[0], nth(U_B + 1, 2, j) + 1)
                nc.vector.scalar_tensor_tensor(view3(blk(MG, j)), view3(T[2]), 1.0, accv[0], ALU.add, ALU.mult)\
                    .then_inc(acc_free[0], 1)
            for k in range(KB):
                dve.wait_ge(hah_done, k + 1)
                nc.vector.tensor_tensor(blk(HAL, k), blk(HA, k), blk(HAH, k).bitcast(F32), ALU.subtract).then_inc(hal_done, 1)

            def merged_low(k):
                dve.wait_ge(mgh_done, k + 1)
                nc.vector.scalar_tensor_tensor(blk(MGL, k), blk(MG, k), 0.5, blk(MGH, k).bitcast(F32), ALU.mult, ALU.subtract)\
                    .then_inc(mgl_done, 1)

            def merge_gate(j):
                dve.wait_ge(acc_free[0], G_A[0] + j)
                evacuate(U_A, 2, j, 1, T[2])

            def merge(j):
                dve.wait_ge(tanh_done, j + KB + 1)
                dve.wait_ge(unit_done[0], nth(U_A + 1, 2, j) + 1)
                nc.vector.scalar_tensor_tensor(view3(T[0]), view3(T[2]), 1.0, accv[0], ALU.add, ALU.mult)\
                    .then_inc(acc_free[0], 1)
                dve.wait_ge(acc_free[0], G_A[0] + j + 1)
                nc.vector.tensor_tensor(blk(MG, j), blk(MG, j), T[0], ALU.add).then_inc(ma_done, 1)
                dve.wait_ge(ma_done, j + 1)
            with dve.Fori(0, KB - 1) as j:
                merge_gate(j)
                merge(j)
            merge_gate(KB - 1)
            for k in range(KB - 1):
                merged_low(k)
            merge(KB - 1)
            merged_low(KB - 1)
            for k in range(KB):
                g = 1 - k % 2
                dve.wait_ge(unit_done[slot_of(U_OUT + k)], nth(U_OUT + k) + 1)
                dve.wait_ge(xr_loaded[k], 16)
                nc.vector.tensor_tensor(view3(blk(X2, k)), accv[g], view3(blk(X2, k)), ALU.add).then_inc(acc_free[g], 1)
                dve.wait_ge(xh2_done, k + 1)
                nc.vector.scalar_tensor_tensor(blk(X2L, k), blk(X2, k), par("g2", k), blk(X2H, k).bitcast(F32),
                                               ALU.mult, ALU.subtract).then_inc(xl2_done, 1)
                dve.wait_ge(sq2_done, k + 1)
                if k == 0:
                    nc.vector.tensor_copy(sqsum, T[0]).then_inc(sum2_done, 1)
                else:
                    dve.wait_ge(sum2_done, k)
                    nc.vector.tensor_tensor(sqsum, sqsum, T[k % 2], ALU.add).then_inc(sum2_done, 1)
            dve.wait_ge(fst_loaded, 32)
            fs = fst.rearrange("p (r k b) -> p r k b", r=2, k=UB)

            def fwide(r):
                return fpr[:, r * UB:(r + 1) * UB].unsqueeze(2).broadcast_to([P, UB, NS])
            pf = hd(fps, UB, NS)
            nc.vector.tensor_tensor(pf, fs[:, 0], fwide(0), ALU.mult).then_inc(set_f, 1)
            nc.vector.tensor_tensor(fs[:, 1], fs[:, 1], fwide(1), ALU.mult).then_inc(set_f, 1)
            dve.wait_ge(set_f, 2)
            nc.vector.tensor_tensor(pf, pf, fs[:, 1], ALU.add).then_inc(set_f, 1)
            dve.wait_ge(set_f, 3)
            nc.vector.memset(eg[:, 0:2], 0.0)
            nc.vector.memset(ev[:, 0:2], 0.0)
            nc.vector.tensor_tensor(pf, pf, fwide(3), ALU.add).then_inc(set_f, 1)
            dve.wait_ge(set_f, 4)
            dve.wait_ge(xl2_done, KB)
            dve.wait_ge(r2_done, 1)

            def conv(F, off_b, u, per, i, g, bias_sem, e_t, c_t, step_sem, kept):
                dve.wait_ge(unit_done[slot_of(u)], nth(u, per, i) + 1)
                dve.wait_ge(bias_sem, F)
                dve.wait_ge(step_sem, 3 * F)
                dve.wait_ge(kept, F)
                nc.vector.tensor_tensor(view3(e_t[:, 2:2 + C]), accv[g], view3(rms), ALU.mult).then_inc(acc_free[g], 1)
                dve.wait_ge(bias_sem, F + 1)
                for t in range(2):
                    dve.wait_ge(step_sem, 3 * F + t)
                    nc.vector.scalar_tensor_tensor(c_t[:, 0:NT], e_t[:, t:t + NT], fpr[:, bass.ds(t * UB + off_b + F, 1)],
                                                   c_t[:, 0:NT], ALU.mult, ALU.add).then_inc(step_sem, 1)
                nc.vector.scalar_tensor_tensor(c_t[:, NT:C], e_t[:, NT + 2:C + 2], fpr[:, bass.ds(2 * UB + off_b + F, 1)],
                                               fps[:, bass.ds((off_b + F) * NS, NS)], ALU.mult, ALU.add).then_inc(step_sem, 1)
                nc.vector.tensor_copy(ubuf[:, bass.ds((off_b + F) * UW, UW)], e_t[:, C + 2 - UW:C + 2]).then_inc(kept, 1)

            def ffn_block(F, u, per, i, half, f, adds):
                conv(F, 0, u, per, i, 1, gbias_ready, eg, cg, gconv_step, gkept)
                conv(F, FB, u + 1, per, i, 0, vbias_ready, ev, cv, vconv_step, vkept)
                adds(0)
                dve.wait_ge(ggelu_done, F + 1)
                dve.wait_ge(vconv_step, 3 * F + 3)
                dve.wait_ge(acth_done, F)
                dve.wait_ge(actl_done, F)
                nc.vector.tensor_tensor(act_t, cg, cv, ALU.mult).then_inc(act_done, 1)
                adds(1)
                dve.wait_ge(acth_done, F + 1)
                b = (half * GRP + f) * C
                nc.vector.tensor_tensor(AL[:, b:b + C], act_t, AH[:, b:b + C].bitcast(F32), ALU.subtract).then_inc(actl_done, 1)

            def add(n_down, grp, m, u_last, per, i):
                g = 1 - m % 2
                if m < KB - 1:
                    dve.wait_ge(down_mm, (KB - 1) * n_down + m + 1)
                else:
                    dve.wait_ge(unit_done[slot_of(u_last)], nth(u_last, per, i) + 1)
                dve.wait_ge(acc_free[g], G_FFN[g] + grp + m // 2)
                nc.vector.tensor_tensor(view3(blk(X2, m)), accv[g], view3(blk(X2, m)), ALU.add).then_inc(acc_free[g], 1)

            GU, GD = GRP, KB // 2
            NU, ND = 2 * GRP, GRP
            per, gper = 2 * (NU + ND), 2 * (GU + GD)

            def ffn_group(F0_, u0, grp0, half, n_down=None, i=0):
                def down(m):
                    add(n_down, grp0 + GRP, m, u0 + NU + ND - 1, per, i)
                for f in range(GRP):
                    last = f == GRP - 1 and n_down is not None
                    ffn_block(F0_ + f, u0 + 2 * f, per, i, half, f, down if last else lambda k: None)
                if n_down is not None:
                    for m in range(2, KB):
                        down(m)

            ffn_group(0, U_FFN, 0, 0)
            with dve.Fori(0, NGRP // 2 - 1) as i:
                ffn_group(2 * GRP * i + GRP, U_FFN + NU, GU + gper * i, 1, 2 * i, i)
                ffn_group(2 * GRP * i + 2 * GRP, U_FFN + 2 * NU + ND, 2 * GU + GD + gper * i, 0, 2 * i + 1, i)
            n = NGRP // 2 - 1
            ffn_group(GRP * (NGRP - 1), U_FFN + NU + n * per, GU + gper * n, 1, 2 * n)
            def square_sum(t):
                n, m = divmod(t, KB)
                c, q = slice(n * NW, (n + 1) * NW), ysq[:, t % 2 * NW:(t % 2 + 1) * NW]
                dve.wait_ge(sq3_done, t + 1)
                if m == 0:
                    nc.vector.tensor_copy(ysum[:, c], q).then_inc(sum3_done, 1)
                else:
                    dve.wait_ge(sum3_done, t)
                    nc.vector.tensor_tensor(ysum[:, c], ysum[:, c], q, ALU.add).then_inc(sum3_done, 1)
            for n in range(3):
                c = slice(n * NW, (n + 1) * NW)
                for m in range(KB):
                    dve.wait_ge(last_mm, KB * n + m + 1)
                    nc.vector.tensor_tensor(blk(X2, m)[:, c], last_bank(m)[:, 0:NW], blk(X2, m)[:, c], ALU.add)\
                        .then_inc(last_added, 1)
                    if KB * n + m > 0:
                        square_sum(KB * n + m - 1)
                if n < 2:
                    continue
                square_sum(3 * KB - 1)
                dve.wait_ge(r3_done, 3)
                for m in range(KB):
                    dve.wait_ge(yg_done, KB * n + m + 1)
                    nc.vector.tensor_tensor(blk(Y, m)[:, c], blk(Y, m)[:, c], yrs[:, c], ALU.mult).then_inc(y_done, 1)


def weight_units(w_in, w_a, w_b, w_out, w_up, w_down):
    import numpy as np

    def column_units(w):
        n = w.shape[1] // P
        return w.reshape(KB, P, n, P).transpose(2, 1, 0, 3).reshape(n, P, D)

    edges = np.cumsum([D, D, QK, QK, D, RANK, D, D, D])
    rg_x, rg_y, q, k, v, low, go, m_a, m_b = np.split(w_in, edges[:-1], axis=1)
    low = np.concatenate([low, np.zeros((D, P - RANK), w_in.dtype)], axis=1)

    def paired(a, b):
        return np.stack([column_units(a), column_units(b)], axis=1).reshape(-1, P, D)

    ups = paired(w_up[:, :FF], w_up[:, FF:])

    def down_units(g):
        t = w_down[g * GRP * P:(g + 1) * GRP * P].reshape(GRP, P, KB, P).transpose(2, 0, 1, 3)
        return t.reshape(GRP, KB, P, P).transpose(0, 2, 1, 3).reshape(GRP, P, D)

    parts = [column_units(low), column_units(q), column_units(k), column_units(v), paired(rg_x, rg_y),
             column_units(go), paired(m_b, w_b), paired(m_a, w_a), column_units(w_out)]
    n = 2 * GRP
    parts.append(ups[:n])
    for g in range(1, NGRP):
        parts += [ups[g * n:(g + 1) * n], down_units(g - 1)]
    parts.append(down_units(NGRP - 1))
    return np.ascontiguousarray(np.concatenate(parts))


def kernel(**inputs):
    import ml_dtypes
    import numpy as np
    from concourse import bacc
    from concourse.bass_utils import run_bass_kernel_spmd

    a = {k: np.asarray(v) for k, v in inputs.items()}
    f32 = np.float32

    def by_partition(rows):
        r = rows.reshape(rows.shape[:-1] + (-1, P))
        return np.moveaxis(r, -1, 0)

    def samples_last(s, r0, r1):
        t = by_partition(s[:, r0:r1])
        t = t.transpose(0, 2, 3, 1)
        return np.concatenate([t, np.zeros(t.shape[:3] + (NS - NB,), f32)], axis=3)

    tokens = np.concatenate([a["meta_tokens"], a["x_prompt"][0], a["x_sample"][:, 0], np.zeros((NS - NB, D), f32)])
    x = np.ascontiguousarray(tokens.T.reshape(KB, P, C))
    vecs = [a["rg_conv_w"][0][i] for i in range(4)] + [a["rg_conv_b"][0], a["rg_ba"][0], a["rg_bx"][0],
            a["rg_lambda"][0], a["norm1_g"][0], a["gla_norm_g"][0].reshape(-1), a["norm2_g"][0], a["final_norm_g"]]
    gates = np.zeros((KB, P, 2, P), f32)
    for c, w in enumerate((a["rg_wa"][0], a["rg_wx"][0])):
        w = w.reshape(KB, 2, 64, 64)
        gates[:, 0:64, c, 0:64] = w[:, 0]
        gates[:, 64:128, c, 64:128] = w[:, 1]
    t = np.arange(P)
    ins = {
        "x": x,
        "w": weight_units(a["w_in"][0], a["w_branch_a"][0], a["w_branch_b"][0], a["w_out"][0], a["w_ffn_up"][0],
                          a["w_ffn_down"][0]),
        "params": np.ascontiguousarray(by_partition(np.stack(vecs)).reshape(P, RP_N)),
        "rg_states": np.ascontiguousarray(samples_last(a["state_rg_conv"][0], 0, 3).reshape(P, -1)),
        "h0": np.ascontiguousarray(samples_last(a["state_rg_h"][0][:, None], 0, 1).reshape(P, -1)),
        "rg_old": np.ascontiguousarray(a["state_rg_conv"][0][:, 1:].reshape(16, -1)),
        "ffn_old": np.ascontiguousarray(a["state_ffn_conv"][0][:, 1:].reshape(16, -1)),
        "gla_bias": np.ascontiguousarray(by_partition(a["gla_b_gate"][0])),
        "gla_w_gate": np.ascontiguousarray(a["gla_w_gate"][0]),
        "gla_state": np.ascontiguousarray(a["state_gla"][0].transpose(0, 2, 1, 3).reshape(NB, P, H * DV)),
        "rg_gates": gates.reshape(KB, P, 2 * P),
        "ffn_states": np.ascontiguousarray(samples_last(a["state_ffn_conv"][0], 0, 2).reshape(P, -1)),
        "ffn_params": np.ascontiguousarray(by_partition(np.concatenate([a["ffn_conv_w"][0], a["ffn_conv_b"]])).reshape(P, -1)),
        "reset": np.tile((np.arange(4 * PAIR) % PAIR != 0), (P, 1)).astype(ml_dtypes.bfloat16),
        "reset16": np.tile((np.arange(4 * NMETA) % NMETA != 0), (P, 1)).astype(ml_dtypes.bfloat16),
        "ident": np.eye(P, dtype=f32),
        "mask": (t[None, :] >= t[:, None]).astype(np.int32),
    }
    out_shapes = {
        "y": (KB, P, C), "gla_prompt": (P, H * DV), "gla_sample": (NB, P, H * DV), "rg_last": (P, KB * RGW),
        "h_last": (P, KB * HW), "u_last": (P, UB * UW), "rg_old": ins["rg_old"].shape, "ffn_old": ins["ffn_old"].shape,
    }
    nc = bacc.Bacc("TRN2", target_bir_lowering=False, num_devices=1)
    I = {n: nc.dram_tensor(f"in_{n}", v.shape, mybir.dt.from_np(v.dtype), kind="ExternalInput").ap() for n, v in ins.items()}
    O = {n: nc.dram_tensor(f"out_{n}", s, F32, kind="ExternalOutput").ap() for n, s in out_shapes.items()}
    build(nc, I, O)
    got = run_bass_kernel_spmd(nc, [{f"in_{n}": v for n, v in ins.items()}], core_ids=[0]).results[0]
    o = {n: np.asarray(got[f"out_{n}"]) for n in out_shapes}

    y = o["y"].reshape(D, C).T
    def rows(packed, n, w):
        return packed.reshape(P, n, w).transpose(2, 1, 0).reshape(w, n * P)
    rg, h, u = rows(o["rg_last"], KB, RGW), rows(o["h_last"], KB, HW), rows(o["u_last"], UB, UW)
    rg_old = o["rg_old"].reshape(NB, 2, D)
    ffn_old = o["ffn_old"].reshape(NB, 1, 2 * FF)
    c = np.ascontiguousarray
    return (
        c(y[NMETA:NT])[None], c(y[NT:NT + NB])[:, None],
        c(rg[0:3])[None, None], c(h[0])[None, None],
        c(o["gla_prompt"].reshape(P, H, DV).transpose(1, 0, 2))[None, None], c(u[0:2])[None, None],
        np.concatenate([rg_old, rg[3:3 + NB][:, None]], axis=1)[None], c(h[1:1 + NB])[None],
        c(o["gla_sample"].reshape(NB, P, H, DV).transpose(0, 2, 1, 3))[None],
        np.concatenate([ffn_old, u[2:2 + NB][:, None]], axis=1)[None],
    )
```
